# Optimizing a Trainium2 kernel written in Bass

```python
import math
import jax, jax.numpy as jnp
from jax import lax
import numpy as np

D_MODEL = 1024
BATCH = 1
SEQ = 1024
DEPTH = 1
DEC_BATCH = 8
DEC_SEQ = 1
PAST_LEN = 4096
PAGE_SIZE = 128

SWA_CONFIGS = ((128, 1), (512, 4), (2048, 16))
N_SWA_GROUPS = 3
SWA_HEADS = 8
SWA_HEAD_DIM = 64
SWA_WIDTH = N_SWA_GROUPS * SWA_HEADS * SWA_HEAD_DIM
SWA_OUT = SWA_HEADS * SWA_HEAD_DIM
SWA_BLOCK = 128
DN_HEADS = 8
DN_DK = 128
DN_DV = 128
DN_CONV = 4
DN_CONV_DIM = DN_HEADS * (2 * DN_DK + DN_DV)
DN_CHUNK = 64
N_EXPERT_GROUPS = 4
EXPERTS_PER_GROUP = 8
N_EXPERTS = N_EXPERT_GROUPS * EXPERTS_PER_GROUP
TOP_K_IN_GROUP = 2
D_EXPERT = 512
MOE_BLOCK = 128
EPS = 1e-6

IN_SIZES = (SWA_WIDTH, SWA_WIDTH, SWA_WIDTH, DN_CONV_DIM, DN_HEADS, DN_HEADS, DN_HEADS * DN_DV, D_MODEL, D_MODEL)
IN_WIDTH = 3 * SWA_WIDTH + DN_CONV_DIM + 2 * DN_HEADS + DN_HEADS * DN_DV + 2 * D_MODEL

kernel_name = "dilated_swa_gdn_hmoe_step"

def _split_points():
    pts, acc = [], 0
    for s in IN_SIZES[:-1]:
        acc += s
        pts.append(acc)
    return pts

def _rmsnorm(x, g):
    xf = x.astype(jnp.float32)
    y = xf * lax.rsqrt(jnp.mean(xf * xf, axis=-1, keepdims=True) + EPS)
    return (y * g.astype(jnp.float32)).astype(x.dtype)

def _l2norm(x):
    return x * lax.rsqrt(jnp.sum(x * x, axis=-1, keepdims=True) + EPS)

def _dilated_window_prompt(q, k, v, win, dil):
    Bn, L, H, E = q.shape
    M = L // dil
    n_blk = -(-M // SWA_BLOCK)
    Mp = n_blk * SWA_BLOCK
    span = win // dil

    def to_blocks(a):
        a = a.astype(jnp.float32).reshape(Bn, M, dil, H, E)
        a = jnp.pad(a, ((0, 0), (0, Mp - M), (0, 0), (0, 0), (0, 0)))
        return a.reshape(Bn, n_blk, SWA_BLOCK, dil, H, E)

    def with_prev(a):
        prev = jnp.pad(a, ((0, 0), (1, 0), (0, 0), (0, 0), (0, 0), (0, 0)))[:, :-1]
        return jnp.concatenate([prev, a], axis=2)

    qb, kb, vb = to_blocks(q), to_blocks(k), to_blocks(v)
    kk, vv = with_prev(kb), with_prev(vb)
    s = jnp.einsum('bnqrhe,bnkrhe->bnrhqk', qb, kk) * (E ** -0.5)
    qi = jnp.arange(SWA_BLOCK)[:, None]
    ki = jnp.arange(2 * SWA_BLOCK)[None, :]
    dist = SWA_BLOCK + qi - ki
    band = (dist >= 0) & (dist <= span)
    after_start = (jnp.arange(n_blk)[:, None, None] > 0) | (ki >= SWA_BLOCK)[None]
    mask = band[None] & after_start
    s = jnp.where(mask[None, :, None, None], s, -jnp.inf)
    mx = jnp.max(s, axis=-1, keepdims=True)
    p = jnp.exp(s - mx)
    den = jnp.sum(p, axis=-1)
    o = jnp.einsum('bnrhqk,bnkrhe->bnqrhe', p, vv) / jnp.moveaxis(den, 4, 2)[..., None]
    lse = jnp.moveaxis(mx[..., 0] + jnp.log(den), 4, 2)
    o = o.reshape(Bn, Mp, dil, H, E)[:, :M].reshape(Bn, L, H, E)
    lse = lse.reshape(Bn, Mp, dil, H)[:, :M].reshape(Bn, L, H)
    return o, lse

def _dilated_window_step(q, k, v, buf, win, dil):
    Bn, T, H, E = q.shape
    Wb = buf.shape[1]
    keys = jnp.concatenate([buf[:, :, 0].astype(jnp.float32), k.astype(jnp.float32)], axis=1)
    vals = jnp.concatenate([buf[:, :, 1].astype(jnp.float32), v.astype(jnp.float32)], axis=1)
    j = jnp.arange(win // dil + 1)
    idx = Wb + jnp.arange(T)[:, None] - j[None, :] * dil
    valid = idx >= 0
    idx = jnp.maximum(idx, 0)
    kg = keys[:, idx]
    vg = vals[:, idx]
    s = jnp.einsum('bthe,btjhe->bthj', q.astype(jnp.float32), kg) * (E ** -0.5)
    s = jnp.where(valid[None, :, None, :], s, -jnp.inf)
    mx = jnp.max(s, axis=-1, keepdims=True)
    p = jnp.exp(s - mx)
    den = jnp.sum(p, axis=-1)
    o = jnp.einsum('bthj,btjhe->bthe', p, vg) / den[..., None]
    return o, mx[..., 0] + jnp.log(den)

def _dn_inputs(qkv_raw, conv_prev, conv_w, b_raw, a_raw, a_log, dt_bias):
    Bn, L, _ = qkv_raw.shape
    xp = jnp.concatenate([conv_prev.astype(qkv_raw.dtype), qkv_raw], axis=1)
    conv = conv_w[0] * xp[:, 0:L]
    for i in range(1, DN_CONV):
        conv = conv + conv_w[i] * xp[:, i:i + L]
    new_conv = xp[:, -(DN_CONV - 1):]
    act = jax.nn.silu(conv.astype(jnp.float32))
    qd, kd, vd = jnp.split(act, [DN_HEADS * DN_DK, 2 * DN_HEADS * DN_DK], axis=-1)
    qd = _l2norm(qd.reshape(Bn, L, DN_HEADS, DN_DK)) * (DN_DK ** -0.5)
    kd = _l2norm(kd.reshape(Bn, L, DN_HEADS, DN_DK))
    vd = vd.reshape(Bn, L, DN_HEADS, DN_DV)
    beta = jax.nn.sigmoid(b_raw.astype(jnp.float32))
    g = -jnp.exp(a_log.astype(jnp.float32)) * jax.nn.softplus(a_raw.astype(jnp.float32) + dt_bias.astype(jnp.float32))
    return qd, kd, vd, beta, g, new_conv

def _gated_delta_chunked(q, k, v, beta, g, s0):
    Bn, L, H, _ = q.shape
    C = min(DN_CHUNK, L)
    Lp = -(-L // C) * C
    n = Lp // C

    def chunks(a):
        a = jnp.pad(a, [(0, 0), (0, Lp - L)] + [(0, 0)] * (a.ndim - 2))
        return a.reshape((Bn, n, C) + a.shape[2:])

    q, k, v, beta, g = chunks(q), chunks(k), chunks(v), chunks(beta), chunks(g)
    gc = jnp.cumsum(g, axis=2)
    gch = jnp.moveaxis(gc, 3, 2)
    causal = jnp.tril(jnp.ones((C, C), dtype=bool))
    strict = jnp.tril(jnp.ones((C, C), dtype=bool), -1)
    decay = jnp.exp(jnp.where(causal, gch[..., :, None] - gch[..., None, :], -jnp.inf))
    kb = k * beta[..., None]
    lower = jnp.where(strict, jnp.einsum('bnihd,bnjhd->bnhij', kb, k) * decay, 0.0)
    eye = jnp.eye(C, dtype=jnp.float32)
    tmat = jax.lax.linalg.triangular_solve(lower + eye, jnp.broadcast_to(eye, lower.shape), left_side=True, lower=True)
    u = jnp.einsum('bnhij,bnjhd->bnihd', tmat, v * beta[..., None])
    w = jnp.einsum('bnhij,bnjhd->bnihd', tmat, kb * jnp.exp(gc)[..., None])
    a_intra = jnp.einsum('bnihd,bnjhd->bnhij', q, k) * decay
    q_dec = q * jnp.exp(gc)[..., None]
    k_dec = k * jnp.exp(gc[:, :, -1:] - gc)[..., None]
    g_tot = jnp.exp(gc[:, :, -1])
    xs = (jnp.moveaxis(u, 1, 0), jnp.moveaxis(w, 1, 0), jnp.moveaxis(a_intra, 1, 0),
          jnp.moveaxis(q_dec, 1, 0), jnp.moveaxis(k_dec, 1, 0), jnp.moveaxis(g_tot, 1, 0))

    def step(S, xc):
        u_i, w_i, a_i, qd_i, kd_i, gt_i = xc
        v_new = u_i - jnp.einsum('bihk,bhkv->bihv', w_i, S)
        o_i = jnp.einsum('bihk,bhkv->bihv', qd_i, S) + jnp.einsum('bhij,bjhv->bihv', a_i, v_new)
        S = S * gt_i[..., None, None] + jnp.einsum('bihk,bihv->bhkv', kd_i, v_new)
        return S, o_i

    S, o = lax.scan(step, s0, xs)
    o = jnp.moveaxis(o, 0, 1).reshape(Bn, Lp, H, DN_DV)[:, :L]
    return o, S

def _experts_dropless(h, experts, weights, w_gate, w_up, w_down):
    N, D = h.shape
    A = N * TOP_K_IN_GROUP
    e_flat = experts.reshape(-1)
    tok_flat = jnp.repeat(jnp.arange(N, dtype=jnp.int32), TOP_K_IN_GROUP)
    w_flat = weights.reshape(-1)
    order = jnp.argsort(e_flat)
    e_s, tok_s, w_s = e_flat[order], tok_flat[order], w_flat[order]
    counts = jax.ops.segment_sum(jnp.ones_like(e_flat), e_flat, num_segments=N_EXPERTS)
    start = jnp.cumsum(counts) - counts
    pcounts = (counts + MOE_BLOCK - 1) // MOE_BLOCK * MOE_BLOCK
    pend = jnp.cumsum(pcounts)
    pstart = pend - pcounts
    dest = pstart[e_s] + (jnp.arange(A, dtype=jnp.int32) - start[e_s])
    n_blocks = -(-A // MOE_BLOCK) + N_EXPERTS
    P = n_blocks * MOE_BLOCK
    row_tok = jnp.full((P,), N, dtype=jnp.int32).at[dest].set(tok_s)
    row_w = jnp.zeros((P,), jnp.float32).at[dest].set(w_s)
    blk_e = jnp.minimum(jnp.searchsorted(pend, jnp.arange(n_blocks) * MOE_BLOCK, side='right'), N_EXPERTS - 1)
    h_pad = jnp.concatenate([h, jnp.zeros((1, D), h.dtype)], axis=0)
    xb = h_pad[row_tok].reshape(n_blocks, MOE_BLOCK, D)

    def block_ffn(args):
        xblk, e = args
        return (jax.nn.silu(xblk @ w_gate[e]) * (xblk @ w_up[e])) @ w_down[e]

    yb = lax.map(block_ffn, (xb, blk_e)).reshape(P, D)
    y = jax.ops.segment_sum(yb.astype(jnp.float32) * row_w[:, None], row_tok, num_segments=N + 1)[:N]
    return y.astype(h.dtype)

def _hier_moe(x, ln2_g, w_rg, b_rg, w_re, b_re, w_e_gate, w_e_up, w_e_down):
    Bn, L, D = x.shape
    h = _rmsnorm(x, ln2_g).reshape(-1, D)
    N = h.shape[0]
    hf = h.astype(jnp.float32)
    lg = hf @ w_rg.astype(jnp.float32) + b_rg.astype(jnp.float32)
    pg = jax.nn.softmax(lg, axis=-1)
    gsel = jnp.argmax(lg, axis=-1)
    le = (hf @ w_re.astype(jnp.float32) + b_re.astype(jnp.float32)).reshape(N, N_EXPERT_GROUPS, EXPERTS_PER_GROUP)
    le_sel = jnp.take_along_axis(le, gsel[:, None, None], axis=1)[:, 0]
    top_v, top_i = lax.top_k(le_sel, TOP_K_IN_GROUP)
    w_sel = jax.nn.softmax(top_v, axis=-1) * jnp.take_along_axis(pg, gsel[:, None], axis=1)
    experts = (gsel[:, None] * EXPERTS_PER_GROUP + top_i).astype(jnp.int32)
    y = _experts_dropless(h, experts, w_sel, w_e_gate, w_e_up, w_e_down)
    return x + y.reshape(Bn, L, D)

def _layer(x, swa_bufs, conv_prev, s0, ln1_g, w_in, q_norm_g, k_norm_g, dn_conv_w, dn_a_log, dn_dt_bias,
           dn_norm_g, w_out_a, w_out_b, w_o, ln2_g, w_rg, b_rg, w_re, b_re, w_e_gate, w_e_up, w_e_down):
    Bn, L, _ = x.shape
    h = _rmsnorm(x, ln1_g)
    z = h @ w_in
    q_a, k_a, v_a, qkv_dn, b_raw, a_raw, z_out, gate_a, gate_b = jnp.split(z, _split_points(), axis=-1)
    shp = (Bn, L, N_SWA_GROUPS, SWA_HEADS, SWA_HEAD_DIM)
    q_a = _rmsnorm(q_a.reshape(shp), q_norm_g[:, None, :])
    k_a = _rmsnorm(k_a.reshape(shp), k_norm_g[:, None, :])
    v_a = v_a.reshape(shp)
    outs, lses, new_swa = [], [], []
    for gi in range(N_SWA_GROUPS):
        win, dil = SWA_CONFIGS[gi]
        qg, kg, vg = q_a[:, :, gi], k_a[:, :, gi], v_a[:, :, gi]
        if swa_bufs is None:
            o, lse = _dilated_window_prompt(qg, kg, vg, win, dil)
            keep = min(win, L)
            new_swa.append(jnp.stack([kg[:, L - keep:], vg[:, L - keep:]], axis=2))
        else:
            o, lse = _dilated_window_step(qg, kg, vg, swa_bufs[gi], win, dil)
            new_swa.append(jnp.stack([kg, vg], axis=2))
        outs.append(o)
        lses.append(lse)
    alpha = jax.nn.softmax(jnp.stack(lses, axis=0), axis=0)
    o_a = jnp.einsum('gblh,gblhe->blhe', alpha, jnp.stack(outs, axis=0)).reshape(Bn, L, SWA_OUT).astype(x.dtype)
    y_a = o_a @ w_out_a

    if conv_prev is None:
        conv_prev = jnp.zeros((Bn, DN_CONV - 1, DN_CONV_DIM), x.dtype)
    if s0 is None:
        s0 = jnp.zeros((Bn, DN_HEADS, DN_DK, DN_DV), jnp.float32)
    qd, kd, vd, beta, g, new_conv = _dn_inputs(qkv_dn, conv_prev, dn_conv_w, b_raw, a_raw, dn_a_log, dn_dt_bias)
    o_d, s_new = _gated_delta_chunked(qd, kd, vd, beta, g, s0.astype(jnp.float32))
    o_d = _rmsnorm(o_d, dn_norm_g) * jax.nn.silu(z_out.astype(jnp.float32).reshape(Bn, L, DN_HEADS, DN_DV))
    y_b = o_d.reshape(Bn, L, DN_HEADS * DN_DV).astype(x.dtype) @ w_out_b

    mix = jax.nn.sigmoid(gate_a) * y_a + jax.nn.sigmoid(gate_b) * y_b
    x = x + mix @ w_o
    x = _hier_moe(x, ln2_g, w_rg, b_rg, w_re, b_re, w_e_gate, w_e_up, w_e_down)
    return x, new_swa, new_conv, s_new

def setup_inputs(seed: int = 0) -> dict:
    key = jax.random.key(seed)
    ks = jax.random.split(key, 32)
    f32 = jnp.float32

    def nrm(k, shape, scale):
        return jax.random.normal(k, shape, f32) * scale

    dt = jnp.exp(jax.random.uniform(ks[13], (DEPTH, DN_HEADS), f32, math.log(1e-3), math.log(1e-1)))
    return {
        "x_prompt": nrm(ks[0], (BATCH, SEQ, D_MODEL), 1.0),
        "x_sample": nrm(ks[1], (DEC_BATCH, DEC_SEQ, D_MODEL), 1.0),
        "cache_swa0_kv": nrm(ks[2], (DEPTH, DEC_BATCH, min(SWA_CONFIGS[0][0], PAST_LEN), 2, SWA_HEADS, SWA_HEAD_DIM), 1.0),
        "cache_swa1_kv": nrm(ks[3], (DEPTH, DEC_BATCH, min(SWA_CONFIGS[1][0], PAST_LEN), 2, SWA_HEADS, SWA_HEAD_DIM), 1.0),
        "cache_swa2_kv": nrm(ks[4], (DEPTH, DEC_BATCH, min(SWA_CONFIGS[2][0], PAST_LEN), 2, SWA_HEADS, SWA_HEAD_DIM), 1.0),
        "state_dn_conv": nrm(ks[5], (DEPTH, DEC_BATCH, DN_CONV - 1, DN_CONV_DIM), 1.0),
        "state_dn_S": nrm(ks[6], (DEPTH, DEC_BATCH, DN_HEADS, DN_DK, DN_DV), 0.1),
        "ln1_g": 1.0 + nrm(ks[7], (DEPTH, D_MODEL), 0.02),
        "w_in": nrm(ks[8], (DEPTH, D_MODEL, IN_WIDTH), D_MODEL ** -0.5),
        "q_norm_g": 1.0 + nrm(ks[9], (DEPTH, N_SWA_GROUPS, SWA_HEAD_DIM), 0.02),
        "k_norm_g": 1.0 + nrm(ks[10], (DEPTH, N_SWA_GROUPS, SWA_HEAD_DIM), 0.02),
        "dn_conv_w": nrm(ks[11], (DEPTH, DN_CONV, DN_CONV_DIM), DN_CONV ** -0.5),
        "dn_a_log": jnp.log(jax.random.uniform(ks[12], (DEPTH, DN_HEADS), f32, 1.0, 16.0)),
        "dn_dt_bias": dt + jnp.log(-jnp.expm1(-dt)),
        "dn_norm_g": 1.0 + nrm(ks[14], (DEPTH, DN_DV), 0.02),
        "w_out_a": nrm(ks[15], (DEPTH, SWA_OUT, D_MODEL), SWA_OUT ** -0.5),
        "w_out_b": nrm(ks[16], (DEPTH, DN_HEADS * DN_DV, D_MODEL), (DN_HEADS * DN_DV) ** -0.5),
        "w_o": nrm(ks[17], (DEPTH, D_MODEL, D_MODEL), D_MODEL ** -0.5),
        "ln2_g": 1.0 + nrm(ks[18], (DEPTH, D_MODEL), 0.02),
        "w_rg": nrm(ks[19], (DEPTH, D_MODEL, N_EXPERT_GROUPS), D_MODEL ** -0.5),
        "b_rg": nrm(ks[20], (DEPTH, N_EXPERT_GROUPS), 0.01),
        "w_re": nrm(ks[21], (DEPTH, D_MODEL, N_EXPERTS), D_MODEL ** -0.5),
        "b_re": nrm(ks[22], (DEPTH, N_EXPERTS), 0.01),
        "w_e_gate": nrm(ks[23], (DEPTH, N_EXPERTS, D_MODEL, D_EXPERT), D_MODEL ** -0.5),
        "w_e_up": nrm(ks[24], (DEPTH, N_EXPERTS, D_MODEL, D_EXPERT), D_MODEL ** -0.5),
        "w_e_down": nrm(ks[25], (DEPTH, N_EXPERTS, D_EXPERT, D_MODEL), D_EXPERT ** -0.5),
    }

def reference(x_prompt, x_sample, cache_swa0_kv, cache_swa1_kv, cache_swa2_kv, state_dn_conv, state_dn_S,
              ln1_g, w_in, q_norm_g, k_norm_g, dn_conv_w, dn_a_log, dn_dt_bias, dn_norm_g, w_out_a, w_out_b,
              w_o, ln2_g, w_rg, b_rg, w_re, b_re, w_e_gate, w_e_up, w_e_down):
    yp, ys = x_prompt, x_sample
    p_sw0, p_sw1, p_sw2, p_cv, p_S = [], [], [], [], []
    s_sw0, s_sw1, s_sw2, s_cv, s_S = [], [], [], [], []
    for l in range(DEPTH):
        lw = (ln1_g[l], w_in[l], q_norm_g[l], k_norm_g[l], dn_conv_w[l], dn_a_log[l], dn_dt_bias[l],
              dn_norm_g[l], w_out_a[l], w_out_b[l], w_o[l], ln2_g[l], w_rg[l], b_rg[l], w_re[l], b_re[l],
              w_e_gate[l], w_e_up[l], w_e_down[l])
        yp, pw, pc, pS = _layer(yp, None, None, None, *lw)
        ys, sw, sc, sS = _layer(ys, (cache_swa0_kv[l], cache_swa1_kv[l], cache_swa2_kv[l]),
                                state_dn_conv[l], state_dn_S[l], *lw)
        p_sw0.append(pw[0]); p_sw1.append(pw[1]); p_sw2.append(pw[2]); p_cv.append(pc); p_S.append(pS)
        s_sw0.append(sw[0]); s_sw1.append(sw[1]); s_sw2.append(sw[2]); s_cv.append(sc); s_S.append(sS)
    return (yp, ys,
            jnp.stack(p_sw0), jnp.stack(p_sw1), jnp.stack(p_sw2), jnp.stack(p_cv), jnp.stack(p_S),
            jnp.stack(s_sw0), jnp.stack(s_sw1), jnp.stack(s_sw2), jnp.stack(s_cv), jnp.stack(s_S))


_drawn_inputs = setup_inputs


def setup_inputs(seed=0):
    import zlib

    import numpy as np

    out = dict(_drawn_inputs(seed))
    spreads = {}
    factors = {'q_norm_g': 7.129,
     'k_norm_g': 3.713,
     'dn_norm_g': 3.351,
     'b_rg': 16.103,
     'b_re': 4.527,
     'ln2_g': 2.922}
    for name, (base, spread) in spreads.items():
        noise = np.random.default_rng([zlib.crc32(name.encode()), seed]).standard_normal(out[name].shape)
        drawn = base * np.exp(spread * noise) if base else spread * noise
        out[name] = __import__('jax').numpy.asarray(drawn.astype(out[name].dtype))
    for name, factor in factors.items():
        out[name] = (out[name] * factor).astype(out[name].dtype)
    return out
```

```python
from contextlib import ExitStack

import concourse.bass as bass
from concourse import mybir

F32 = mybir.dt.float32
BF16 = mybir.dt.bfloat16
I32 = mybir.dt.int32
U32 = mybir.dt.uint32
ALU = mybir.AluOpType
ACT = mybir.ActivationFunctionType
AX = mybir.AxisListType

P = 128
D = 1024
KD = D // P
SEQ = 1024
NB = 8
TOK = SEQ + NB
NT = SEQ // P
EPS = 1e-6
NG, NH, E = 3, 8, 64
HW = NH * E
SWA = ((128, 1), (512, 4), (2048, 16))
DNH, DK = 8, 128
COL_Q, COL_K, COL_V = 0, 1536, 3072
COL_DN = 4608
COL_BETA = COL_DN + 3072
COL_Z = COL_BETA + 16
COL_GA = COL_Z + 1024
COL_GB = COL_GA + 1024
OROW = HW + 2 * NH
NEG = -1.0e30
NE, NGE, EPG = 32, 4, 8
MAXB = 50
RING = 6
SLOT = KD * 512


class Shared:
    pass


class Chain:

    def __init__(self, eng, sem):
        self.eng, self.sem, self.n = eng, sem, 0

    def __call__(self, ins):
        self.n += 1
        ins.then_inc(self.sem, 1)
        self.eng.wait_ge(self.sem, self.n)


def bcast(ap, shape):
    return ap.to_broadcast(shape)


def perm_tokens(hT, g, t, k):
    if g == 0:
        return hT[:, k, t * P:(t + 1) * P]
    if g == 1:
        s = 512 * (t % 2) + t // 2
        return hT[:, k, s:s + 4 * (P - 1) + 1:4]
    return hT[:, k, t:t + 8 * (P - 1) + 1:8]


def perm_rows(dram, g, t):
    if g == 0:
        return dram[t * P:(t + 1) * P, :]
    if g == 1:
        s = 512 * (t % 2) + t // 2
        return dram[s:s + 4 * (P - 1) + 1:4, :]
    return dram[t:t + 8 * (P - 1) + 1:8, :]


def weight_plan():
    plan = []
    for g in range(NG):
        plan += [("q", g), ("k", g), ("v", g)]
    plan += [("dn", h) for h in range(DNH)]
    for kind in ("ga", "gb", "wb", "wo"):
        plan += [(kind, 0), (kind, 1)]
    return plan


SLOTS = [0, 1, 2, 3, 4, 5, 0, 1, 2] + [3, 4] * 4 + [3, 4, 0, 1, 2, 5, 3, 0]


def dmas_of(plan, n):
    return 4 if plan[n][0] == "dn" else 1


def load_chunk(sp, m, n):
    kind, i = m.plan[n]
    slot = m.ring[:, SLOTS[n], :]
    before = [j for j in range(n) if SLOTS[j] == SLOTS[n]]
    if before and before[-1] in m.last_use:
        sp.wait_ge(*m.last_use[before[-1]])
    if kind in "qkv":
        c = {"q": COL_Q, "k": COL_K, "v": COL_V}[kind] + i * HW
        parts = [(slot.rearrange("p (k n) -> p k n", k=KD), m.w_in_v[:, :, c:c + HW])]
    elif kind == "dn":
        v = slot.rearrange("p (k w n) -> p k w n", k=KD, w=4)
        parts = [(v[:, :, w, :], m.w_in_v[:, :, c:c + DK]) for w, c in
                 enumerate((COL_DN + i * DK, COL_DN + 1024 + i * DK, COL_DN + 2048 + i * DK, COL_Z + i * DK))]
    elif kind in ("ga", "gb"):
        c = (COL_GA if kind == "ga" else COL_GB) + i * 512
        parts = [(slot.rearrange("p (k n) -> p k n", k=KD), m.w_in_v[:, :, c:c + 512])]
    elif kind == "wb":
        parts = [(slot.rearrange("p (k n) -> p k n", k=KD),
                  m.w_out_b.rearrange("(k p) n -> p k n", p=P)[:, :, i * 512:(i + 1) * 512])]
    else:
        parts = [(slot.rearrange("p (k n) -> p k n", k=KD),
                  m.w_o.rearrange("(k p) n -> p k n", p=P)[:, :, i * 512:(i + 1) * 512])]
    for dst, src in parts:
        sp.dma_start(dst, src).then_inc(m.w_landed[SLOTS[n]], 16)


def chunk(pe, m, kind, i):
    n = m.plan.index((kind, i))
    pe.wait_ge(m.w_landed[SLOTS[n]], 16 * sum(dmas_of(m.plan, j) for j in range(n + 1) if SLOTS[j] == SLOTS[n]))
    return m.ring[:, SLOTS[n], :]


def stage_constants(nc, m):
    with nc.Block() as block:
        @block.sync
        def _(sp):
            for dst, src in m.small_loads:
                sp.dma_start(dst, src).then_inc(m.small_landed, 16)
            sp.wait_ge(m.small_landed, 16 * len(m.small_loads))

        @block.gpsimd
        def _(pool):
            step = Chain(pool, m.pool_step)
            nc.gpsimd.iota(m.odd, pattern=[[1, P]], base=0, channel_multiplier=1).then_inc(m.iota_ready, 1)
            for ap, value in ((m.ident, 0.0), (m.scratch_mask, 0.0), (m.ones, 1.0), (m.minus_half, -0.5)):
                step(nc.gpsimd.memset(ap, value))
            step(nc.gpsimd.affine_select(out=m.ident, in_=m.ident, compare_op=ALU.not_equal, fill=1.0, base=0,
                                         pattern=[[-1, P]], channel_multiplier=1))
            step(nc.gpsimd.tensor_copy(m.ident_b, m.ident))
            pool.wait_ge(m.small_landed, 16 * len(m.small_loads))
            step(nc.gpsimd.tensor_scalar(m.qk_gain[:, 0], m.qk_gain[:, 0], float(E) ** -0.5, None, ALU.mult))
            step(nc.gpsimd.affine_select(out=m.triu, in_=m.ones, compare_op=ALU.is_ge, fill=0.0, base=0,
                                         pattern=[[1, P]], channel_multiplier=-1))
            step(nc.gpsimd.memset(m.pick_row, 0.0))
            step(nc.gpsimd.affine_select(out=m.pick_row, in_=m.pick_row, compare_op=ALU.not_equal, fill=1.0, base=0,
                                         pattern=[[-1, NB], [0, P]], channel_multiplier=1))
            step(nc.gpsimd.memset(m.pick_col, 0.0))
            step(nc.gpsimd.affine_select(out=m.pick_col, in_=m.pick_col, compare_op=ALU.not_equal, fill=1.0, base=0,
                                         pattern=[[-1, NB], [1, NB]], channel_multiplier=0))
            step(nc.gpsimd.affine_select(out=m.scratch_mask[:, 0:P], in_=m.scratch_mask[:, 0:P],
                                         compare_op=ALU.is_ge, fill=NEG, base=0,
                                         pattern=[[1, P]], channel_multiplier=-1))
            step(nc.gpsimd.affine_select(out=m.scratch_mask[:, P:2 * P], in_=m.scratch_mask[:, P:2 * P],
                                         compare_op=ALU.is_ge, fill=NEG, base=0,
                                         pattern=[[-1, P]], channel_multiplier=1))
            step(nc.gpsimd.tensor_copy(m.mask_band, m.scratch_mask))
            pool.wait_ge(m.parity_ready, 3)
            step(nc.gpsimd.tensor_tensor(m.mask_pair, m.scratch_mask[:, P:2 * P], m.odd_f, ALU.add))
            step(nc.gpsimd.memset(m.scratch_mask, 0.0))
            step(nc.gpsimd.affine_select(out=m.scratch_mask[:, 0:P], in_=m.scratch_mask[:, 0:P],
                                         compare_op=ALU.is_ge, fill=-NEG, base=0,
                                         pattern=[[-1, P]], channel_multiplier=1))
            step(nc.gpsimd.tensor_copy(m.mask_decay, m.scratch_mask[:, 0:P]))

        @block.vector
        def _(dve):
            dve.wait_ge(m.iota_ready, 1)
            step = Chain(dve, m.parity_ready)
            step(nc.vector.tensor_single_scalar(m.odd, m.odd, 1, ALU.bitwise_and))
            step(nc.vector.tensor_copy(m.odd_f, m.odd))
            step(nc.vector.tensor_scalar(m.odd_f, m.odd_f, NEG, None, ALU.mult))


def semaphore(nc, m, name):
    m.taken.append(nc.alloc_semaphore(name))
    return m.taken[-1]


def semaphores(nc, m, stage, names):
    return {x: semaphore(nc, m, f"{stage}_{x}") for x in names.split()}


def stage_norm1(nc, m):
    tiles = [(t, P) for t in range(NT)] + [(NT, NB)]
    XB = 4
    with ExitStack() as ctx:
        xs = ctx.enter_context(nc.sbuf_tensor("n1_x", [P, XB, D], F32))
        hs = ctx.enter_context(nc.sbuf_tensor("n1_h", [P, 2, D], F32))
        junk = ctx.enter_context(nc.sbuf_tensor("n1_junk", [P, D], F32))
        ssq = ctx.enter_context(nc.sbuf_tensor("n1_ssq", [P, 2, 3], F32))
        hps = ctx.enter_context(nc.psum_tensor("n1_hps", [P, 2, KD, P], F32))
        x_landed = [semaphore(nc, m, f"n1_x_landed{i}") for i in range(XB)]
        squares_summed, rstd_ready, normed, turned, written, rstd_step = (
            semaphore(nc, m, f"n1_{x}") for x in
            ("squares_summed", "rstd_ready", "normed", "turned", "written", "rstd_step"))
        with nc.Block() as block:
            @block.sync
            def _(sp):
                for t, n in tiles:
                    if t >= XB:
                        sp.wait_ge(normed, t - XB + 1)
                    src = m.x_prompt[t * P:(t + 1) * P, :] if t < NT else m.x_sample
                    sp.dma_start(xs[0:n, t % XB, :], src).then_inc(x_landed[t % XB], 16)
                    if t in (3, 5, 7):
                        load_chunk(sp, m, (t - 3) // 2)
                for n in range(3, RING):
                    load_chunk(sp, m, n)

            @block.scalar
            def _(act):
                for t, n in tiles:
                    act.wait_ge(x_landed[t % XB], 16 * (t // XB + 1))
                    if t >= 2:
                        act.wait_ge(rstd_ready, t - 1)
                    if t >= 1:
                        act.wait_ge(squares_summed, t)
                    nc.scalar.activation(junk[0:n, :], xs[0:n, t % XB, :], ACT.Square,
                                         accum_out=ssq[0:n, t % 2, 0:1]).then_inc(squares_summed, 1)

            @block.gpsimd
            def _(pool):
                for t, n in tiles:
                    s = ssq[0:n, t % 2, :]
                    pool.wait_ge(squares_summed, t + 1)
                    if t >= 2:
                        pool.wait_ge(normed, t - 1)
                    nc.gpsimd.tensor_scalar(s[:, 1:2], s[:, 0:1], 1.0 / D, EPS, ALU.mult, ALU.add).then_inc(rstd_step, 1)
                    pool.wait_ge(rstd_step, t + 1)
                    nc.gpsimd.tensor_tensor(s[:, 2:3], s[:, 1:2], m.minus_half[0:n, 0:1], ALU.pow).then_inc(rstd_ready, 1)

            @block.vector
            def _(dve):
                for t, n in tiles + [(NT + 1, 0)]:
                    if t <= NT:
                        dve.wait_ge(rstd_ready, t + 1)
                        if t >= 2:
                            dve.wait_ge(turned, t - 1)
                        nc.vector.tensor_scalar(hs[0:n, t % 2, :], xs[0:n, t % XB, :], ssq[0:n, t % 2, 2:3], None,
                                                ALU.mult).then_inc(normed, 1)
                    if t >= 1:
                        u, w = tiles[t - 1]
                        dve.wait_ge(turned, u + 1)
                        nc.vector.tensor_tensor(m.hT[:, :, u * P:u * P + w], hps[:, u % 2, :, 0:w],
                                                bcast(m.ln1.unsqueeze(2), [P, KD, w]), ALU.mult).then_inc(written, 1)

            @block.tensor
            def _(pe):
                for t, n in tiles:
                    pe.wait_ge(normed, t + 1)
                    if t >= 2:
                        pe.wait_ge(written, t - 1)
                    for k in range(KD):
                        last = nc.tensor.transpose(hps[:, t % 2, k, 0:n], hs[0:n, t % 2, k::KD], m.ident[0:n, 0:n])
                    last.then_inc(turned, 1)




def stage_attention(nc, m):
    jobs = [(g, t) for g in range(NG) for t in range(NT + 1)]
    prompt = [j for j in jobs if j[1] < NT]
    number = {j: n for n, j in enumerate(prompt)}

    def rows(t):
        return P if t < NT else NB

    def has_prev(g, t):
        return (g == 0 and t > 0) or (g == 1 and t % 2 == 1)

    with ExitStack() as ctx:
        def sb(name, shape, dt=F32):
            return ctx.enter_context(nc.sbuf_tensor("at_" + name, shape, dt))[:]

        qn = sb("qn", [P, HW])
        sq = sb("sq", [P, 2, HW])
        stat = sb("stat", [P, 2, 3, NH])
        kv = sb("kv", [P, 3, 2, HW])
        kT = sb("kT", [P, 2, 4, P])
        late = m.oBT.rearrange("p h t -> p (h t)")[:, 3 * NG * HW + NB * P:]
        prob, pT = (late[:, 1024 * i:1024 * (i + 1)].rearrange("p (a h k) -> p a h k", a=2, h=2) for i in range(2))
        qT = late[:, 2048:2560].rearrange("p (h k) -> p h k", h=4)
        orow = sb("orow", [P, 2, OROW])
        pq, pk, po, tps = (ctx.enter_context(nc.psum_tensor(f"at_p{i}", [P, 512], F32))[:] for i in range(4))
        pv = pq
        sbanks = ctx.enter_context(nc.psum_tensor("at_scores", [P, 2, 2, 512], F32))[:]
        sps = sbanks[:, :, :, 0:2 * P]
        tk = sbanks[:, 1, 0, :]
        S = semaphores(nc, m, "at", "q_projected k_projected v_projected q_squared k_squared q_summed k_summed "
                       "q_rstd k_rstd q_scaled k_scaled q_normed k_normed v_copied q_turned k_turned qT_ready "
                       "kT_ready scores_ready max_ready probs_ready probs_turned pT_ready heads_done o_ready "
                       "q_mean k_mean")
        kv_out = [semaphore(nc, m, f"at_kv_out{i}") for i in range(3)]
        o_out = [semaphore(nc, m, f"at_o_out{i}") for i in range(2)]
        for g in range(NG):
            for i, x in enumerate(("q_projected", "k_projected", "v_projected")):
                m.last_use[3 * g + i] = (S[x], (g + 1) * (NT + 1))
        steps = [(jobs[n] if n >= 0 and jobs[n][1] < NT else None, jobs[n + 1] if n + 1 < len(jobs) else None)
                 for n in range(-1, len(jobs))]
        kv_stores = [0, 0, 0]
        stored_before = []
        for n, (g, t) in enumerate(jobs):
            stored_before.append(kv_stores[n % 3])
            if t < NT and (g == 2 or (g == 1 and t % 2 == 1) or (g == 0 and t == NT - 1)):
                kv_stores[n % 3] += 1

        def kv_free(eng, n):
            if stored_before[n]:
                eng.wait_ge(kv_out[n % 3], 16 * stored_before[n])

        def kv_rows(n, which):
            g, t = jobs[n]
            return kv[:, n % 3, which, :] if t < NT else m.kv_s[:, g, which, :]

        with nc.Block() as block:
            @block.sync
            def _(sp):
                o_stores = [0, 0]
                for n, (g, t) in enumerate(jobs):
                    if t == NT:
                        sp.wait_ge(S["k_normed"], n + 1)
                        sp.wait_ge(S["v_copied"], n + 1)
                        sp.dma_start(m.s_swa[g], m.kv_s[:, g, :, :]).then_inc(m.outputs_stored, 16)
                        m.n_outputs += 1
                        for j in {0: (6, 7, 8), 1: (9, 10), 2: ()}[g]:
                            load_chunk(sp, m, j)
                    elif g == 2 or (g == 1 and t % 2 == 1) or (g == 0 and t == NT - 1):
                        sp.wait_ge(S["k_normed"], n + 1)
                        sp.wait_ge(S["v_copied"], n + 1)
                        if g == 0:
                            dst = m.p_swa[0]
                        elif g == 1:
                            dst = m.p_swa[1][t // 2:t // 2 + 4 * (P - 1) + 1:4, :]
                        else:
                            dst = perm_rows(m.p_swa[2], 2, t)
                        sp.dma_start(dst, kv[:, n % 3, :, :].rearrange("p a b -> p (a b)")).then_inc(kv_out[n % 3], 16)
                    if n >= 1 and jobs[n - 1] in number:
                        a = number[jobs[n - 1]]
                        sp.wait_ge(S["o_ready"], a + 1)
                        sp.dma_start(perm_rows(m.o_scr[:, jobs[n - 1][0], :], *jobs[n - 1]), orow[:, a % 2, :]
                                     ).then_inc(o_out[a % 2], 16)
                for i in range(3):
                    sp.wait_ge(kv_out[i], 16 * kv_stores[i])
                for i in range(2):
                    sp.wait_ge(o_out[i], 16 * (len(prompt) // 2))

            @block.tensor
            def _(pe):
                def projections(n):
                    g, t = jobs[n]
                    if n >= 1:
                        pe.wait_ge(S["v_copied"], n)
                    for w, (name, bank) in enumerate((("q", pq), ("k", pk), ("v", pv))):
                        if n >= 1 and name == "k":
                            pe.wait_ge(S["k_scaled"], n)
                        if name == "v":
                            pe.wait_ge(S["q_scaled"], n + 1)
                        weights = chunk(pe, m, name, g).rearrange("p (k n) -> p k n", k=KD)
                        for k in range(KD):
                            tok = perm_tokens(m.hT, g, t, k) if t < NT else m.hT[:, k, SEQ:TOK]
                            mm = nc.tensor.matmul(bank[0:rows(t), :], tok, weights[:, k, :],
                                                  start=(k == 0), stop=(k == KD - 1))
                            if k == KD - 1:
                                mm.then_inc(S[name + "_projected"], 1)
                            yield

                def fill(source, n):
                    for _ in range(n):
                        if next(source, 0) == 0:
                            return

                def scores(a, hp):
                    g, t = prompt[a]
                    first = P * (not has_prev(g, t))
                    if 4 * a + hp >= 2:
                        pe.wait_ge(S["probs_ready"], 2 * (4 * a + hp - 1))
                    mask = m.mask_pair if g == 2 else m.mask_band[:, first:2 * P]
                    for h in range(2):
                        nc.tensor.matmul(sps[:, hp % 2, h, first:2 * P], m.ident_b, mask,
                                         start=True, stop=False, skip_group_check=True)
                    for blk in range(first // P, 2):
                        for h in range(2):
                            own = slice(64 * h, 64 * h + 64)
                            mm = nc.tensor.matmul(sps[:, hp % 2, h, blk * P:(blk + 1) * P], qT[own, hp, :],
                                                  kT[own, (a + 1 + blk) % 2, hp, :],
                                                  start=False, stop=True, skip_group_check=True)
                    mm.then_inc(S["scores_ready"], 1)

                def turn_probs(a, hp):
                    g, t = prompt[a]
                    pe.wait_ge(S["probs_ready"], 2 * (4 * a + hp + 1))
                    if hp >= 1:
                        pe.wait_ge(S["pT_ready"], 4 * a + hp)
                    for h in range(2):
                        for blk in range(not has_prev(g, t), 2):
                            c = h * 2 * P + blk * P
                            mm = nc.tensor.transpose(tps[:, c:c + P], prob[:, hp % 2, h, blk * P:(blk + 1) * P],
                                                     m.ident)
                    mm.then_inc(S["probs_turned"], 1)

                def weigh_values(a, hp):
                    g, t = prompt[a]
                    n = jobs.index(prompt[a])
                    pe.wait_ge(S["pT_ready"], 4 * a + hp + 1)
                    if a >= 1 and hp == 0:
                        pe.wait_ge(S["o_ready"], a)
                    for h in range(2):
                        c = (2 * hp + h) * E
                        blks = range(not has_prev(g, t), 2)
                        for blk in blks:
                            mm = nc.tensor.matmul(po[:, c:c + E], pT[:, hp % 2, h, blk * P:(blk + 1) * P],
                                                  kv[:, (n - 1 + blk) % 3, 1, c:c + E],
                                                  start=(blk == blks[0]), stop=(blk == 1))
                    mm.then_inc(S["heads_done"], 1)

                def turn_qk(n):
                    a = number[jobs[n]]
                    for which, src, bank in (("q", qn, tps), ("k", kv[:, n % 3, 0, :], tk)):
                        pe.wait_ge(S[which + "_normed"], n + 1)
                        if a >= 1 and which == "q":
                            pe.wait_ge(S["pT_ready"], 4 * a)
                        elif a >= 1:
                            pe.wait_ge(S["probs_ready"], 8 * a)
                        for hp in range(4):
                            mm = nc.tensor.transpose(bank[:, hp * P:(hp + 1) * P], src[:, hp * P:(hp + 1) * P], m.ident)
                        mm.then_inc(S[which + "_turned"], 1)

                for att, nxt in steps:
                    source = projections(jobs.index(nxt)) if nxt else iter(())
                    if att:
                        a = number[att]
                        pe.wait_ge(S["qT_ready"], a + 1)
                        pe.wait_ge(S["kT_ready"], a + 1)
                        pe.wait_ge(S["v_copied"], jobs.index(att) + 1)
                        scores(a, 0)
                        scores(a, 1)
                        fill(source, 6)
                        turn_probs(a, 0)
                        scores(a, 2)
                        fill(source, 6)
                        weigh_values(a, 0)
                        turn_probs(a, 1)
                        scores(a, 3)
                        fill(source, 6)
                        weigh_values(a, 1)
                        turn_probs(a, 2)
                        fill(source, 5)
                        weigh_values(a, 2)
                        turn_probs(a, 3)
                        fill(source, 1)
                        weigh_values(a, 3)
                    fill(source, 24)
                    if nxt in number:
                        turn_qk(jobs.index(nxt))

            @block.vector
            def _(dve):
                def row_max(a, hp):
                    g, t = prompt[a]
                    dve.wait_ge(S["scores_ready"], 4 * a + hp + 1)
                    if a >= 2 and hp == 0:
                        dve.wait_ge(o_out[a % 2], 16 * (a // 2))
                    first = P * (not has_prev(g, t))
                    nc.vector.tensor_reduce(orow[:, a % 2, HW + 2 * hp:HW + 2 * hp + 2], sps[:, hp % 2, :, first:2 * P],
                                            AX.X, ALU.max, negate=True).then_inc(S["max_ready"], 1)

                def copy_pT(a, hp):
                    g, t = prompt[a]
                    first = P * (not has_prev(g, t))
                    dve.wait_ge(S["probs_turned"], 4 * a + hp + 1)
                    if 4 * a + hp >= 2:
                        dve.wait_ge(S["heads_done"], 4 * a + hp - 1)
                    nc.vector.tensor_copy(pT[:, hp % 2, :, first:2 * P],
                                          tps.rearrange("p (h k) -> p h k", h=2)[:, :, first:2 * P]
                                          ).then_inc(S["pT_ready"], 1)

                def square_sum(n, which):
                    t, w = jobs[n][1], "qk".index(which)
                    dve.wait_ge(S[which + "_squared"], n + 1)
                    if n >= 1:
                        dve.wait_ge(S[which + "_rstd"], n)
                    nc.vector.tensor_reduce(stat[0:rows(t), w, 0, :],
                                            sq[0:rows(t), w, :].rearrange("p (h e) -> p h e", h=NH),
                                            AX.X, ALU.add).then_inc(S[which + "_summed"], 1)

                def scale(n, which, bank):
                    t, w = jobs[n][1], "qk".index(which)
                    r = rows(t)
                    dve.wait_ge(S[which + "_rstd"], n + 1)
                    nc.vector.tensor_tensor(sq[0:r, w, :].rearrange("p (h e) -> p h e", h=NH),
                                            bank[0:r, :].rearrange("p (h e) -> p h e", h=NH),
                                            bcast(stat[0:r, w, 2, :].unsqueeze(2), [r, NH, E]),
                                            ALU.mult).then_inc(S[which + "_scaled"], 1)

                for att, nxt in steps:
                    a = number.get(att)
                    n = jobs.index(nxt) if nxt else None
                    if att:
                        row_max(a, 0)
                        row_max(a, 1)
                        copy_pT(a, 0)
                        row_max(a, 2)
                    if nxt:
                        square_sum(n, "q")
                    if att:
                        copy_pT(a, 1)
                        row_max(a, 3)
                    if nxt:
                        scale(n, "q", pq)
                        square_sum(n, "k")
                    if att:
                        copy_pT(a, 2)
                    if nxt:
                        scale(n, "k", pk)
                    if att:
                        copy_pT(a, 3)
                    if nxt in number:
                        b = number[nxt]
                        dve.wait_ge(S["q_turned"], b + 1)
                        nc.vector.tensor_copy(qT, tps.rearrange("p (h k) -> p h k", h=4)).then_inc(S["qT_ready"], 1)
                        dve.wait_ge(S["k_turned"], b + 1)
                        nc.vector.tensor_copy(kT[:, b % 2, :, :], tk.rearrange("p (h k) -> p h k", h=4)
                                              ).then_inc(S["kT_ready"], 1)

            @block.scalar
            def _(act):
                def square(n, which, bank):
                    t, w = jobs[n][1], "qk".index(which)
                    act.wait_ge(S[which + "_projected"], n + 1)
                    if n >= 1:
                        act.wait_ge(S[which + "_normed"], n)
                    nc.scalar.activation(sq[0:rows(t), w, :], bank[0:rows(t), :], ACT.Square
                                         ).then_inc(S[which + "_squared"], 1)

                def exps(a, hp):
                    g, t = prompt[a]
                    first = P * (not has_prev(g, t))
                    act.wait_ge(S["max_ready"], 4 * a + hp + 1)
                    if 4 * a + hp >= 2:
                        act.wait_ge(S["probs_turned"], 4 * a + hp - 1)
                    for h in range(2):
                        c = 2 * hp + h
                        nc.scalar.activation(prob[:, hp % 2, h, first:2 * P],
                                             sps[:, hp % 2, h, first:2 * P], ACT.Exp,
                                             bias=orow[:, a % 2, HW + c:HW + c + 1],
                                             accum_out=orow[:, a % 2, HW + NH + c:HW + NH + c + 1]
                                             ).then_inc(S["probs_ready"], 1)

                for att, nxt in steps:
                    a = number.get(att)
                    n = jobs.index(nxt) if nxt else None
                    if att:
                        exps(a, 0)
                        exps(a, 1)
                    if nxt:
                        square(n, "q", pq)
                    if att:
                        exps(a, 2)
                    if nxt:
                        square(n, "k", pk)
                    if att:
                        exps(a, 3)
                    if nxt:
                        t = nxt[1]
                        act.wait_ge(S["v_projected"], n + 1)
                        kv_free(act, n)
                        nc.scalar.activation(kv_rows(n, 1)[0:rows(t), :], pv[0:rows(t), :], ACT.Copy
                                             ).then_inc(S["v_copied"], 1)
                    if att:
                        act.wait_ge(S["heads_done"], 4 * a + 4)
                        nc.scalar.activation(orow[:, a % 2, 0:HW], po[:, :], ACT.Copy).then_inc(S["o_ready"], 1)

            @block.gpsimd
            def _(pool):
                for n, (g, t) in enumerate(jobs):
                    r = rows(t)
                    for w, which in enumerate("qk"):
                        pool.wait_ge(S[which + "_summed"], n + 1)
                        nc.gpsimd.tensor_scalar(stat[0:r, w, 1, :], stat[0:r, w, 0, :], 1.0 / E, EPS,
                                                ALU.mult, ALU.add).then_inc(S[which + "_mean"], 1)
                        pool.wait_ge(S[which + "_mean"], n + 1)
                        if n >= 1:
                            pool.wait_ge(S[which + "_scaled"], n)
                        nc.gpsimd.tensor_tensor(stat[0:r, w, 2, :], stat[0:r, w, 1, :], m.minus_half[0:r, 0:NH],
                                                ALU.pow).then_inc(S[which + "_rstd"], 1)
                        pool.wait_ge(S[which + "_scaled"], n + 1)
                        if which == "k":
                            kv_free(pool, n)
                            dst = kv_rows(n, 0)
                        else:
                            if t < NT and number[(g, t)] >= 1:
                                pool.wait_ge(S["q_turned"], number[(g, t)])
                            dst = qn if t < NT else m.q_s[:, g, :]
                        nc.gpsimd.tensor_tensor(dst[0:r, :].rearrange("p (h e) -> p h e", h=NH),
                                                sq[0:r, w, :].rearrange("p (h e) -> p h e", h=NH),
                                                bcast(m.qk_gain[0:r, w, g, :].unsqueeze(1), [r, NH, E]),
                                                ALU.mult).then_inc(S[which + "_normed"], 1)
                pool.wait_ge(S["o_ready"], len(prompt))


def stage_decode_attention(nc, m):
    with ExitStack() as ctx:
        def sb(name, shape, dt=F32):
            return ctx.enter_context(nc.sbuf_tensor("da_" + name, shape, dt))[:]

        keys, vals = ([m.ring[:, j, :].rearrange("p (b c) -> p b c", b=NB) for j in js] for js in ((0, 1), (2, 5)))
        o_s = sb("o_s", [NB, NG, OROW])
        prod = sb("prod", [P, 2, HW])
        weighed = sb("weighed", [P, 2, HW])
        score = sb("score", [P, NH, NB])
        pT = sb("pT", [P, NH, NB])
        prob = sb("prob", [NB, NH, P])
        new = sb("new", [NB, HW])
        s_new = sb("s_new", [NB, 4, NH])
        qb = ctx.enter_context(nc.psum_tensor("da_qb", [P, 2, 512], F32))[:]
        sT = ctx.enter_context(nc.psum_tensor("da_sT", [P, NH, P], F32))[0:NB]
        pb = ctx.enter_context(nc.psum_tensor("da_pb", [P, 512], F32))[:, 0:NH * NB].rearrange("p (h b) -> p h b", h=NH)
        acc = ctx.enter_context(nc.psum_tensor("da_acc", [P, 512], F32))[0:NB]
        S = semaphores(nc, m, "da", "q_spread scored dve_step scores_turned shifted exp_done new_exp_done probs_turned "
                       "pT_ready values_weighed summed_over_keys o_ready o_stored")
        keys_landed = [semaphore(nc, m, f"da_keys_landed{g}") for g in range(NG)]
        vals_landed = [semaphore(nc, m, f"da_vals_landed{g}") for g in range(NG)]

        with nc.Block() as block:
            @block.sync
            def _(sp):
                for g in range(NG):
                    d = SWA[g][1]
                    if g >= 2:
                        sp.wait_ge(S["scored"], NB * (g - 1))
                    sp.dma_start(keys[g % 2], m.caches[g][0:P * d:d, :, 0:HW]).then_inc(keys_landed[g], 16)
                    if g >= 2:
                        sp.wait_ge(S["values_weighed"], NB * (g - 1))
                    sp.dma_start(vals[g % 2], m.caches[g][0:P * d:d, :, HW:2 * HW]).then_inc(vals_landed[g], 16)
                sp.wait_ge(S["o_ready"], NG)
                sp.dma_start(m.o_s_scr, o_s).then_inc(S["o_stored"], 16)
                sp.wait_ge(S["o_stored"], 16)

            @block.tensor
            def _(pe):
                def spread_q(n):
                    if n >= 2:
                        pe.wait_ge(S["scored"], n - 1)
                    nc.tensor.matmul(qb[:, n % 2, :], m.pick_row[:, n % NB, :], m.q_s[:, n // NB, :],
                                     start=True, stop=True).then_inc(S["q_spread"], 1)

                for b in range(NB):
                    spread_q(b)
                for g in range(NG):
                    pe.wait_ge(S["scored"], NB * (g + 1))
                    for h in range(NH):
                        mm = nc.tensor.transpose(sT[:, h, :], score[:, h, :], m.ident)
                    mm.then_inc(S["scores_turned"], 1)
                    pe.wait_ge(S["exp_done"], g + 1)
                    for h in range(NH):
                        mm = nc.tensor.transpose(pb[:, h, :], prob[:, h, :], m.ident[0:NB, 0:NB])
                    mm.then_inc(S["probs_turned"], 1)
                    for b in range(NB):
                        if g + 1 < NG:
                            spread_q((g + 1) * NB + b)
                        pe.wait_ge(S["values_weighed"], g * NB + b + 1)
                        mm = nc.tensor.matmul(acc, m.pick_col[:, b, :], weighed[:, b % 2, :],
                                              start=(b == 0), stop=(b == NB - 1))
                        mm.then_inc(S["summed_over_keys"], 1)

            @block.vector
            def _(dve):
                step = Chain(dve, S["dve_step"])
                heads = "p (h e) -> p h e"

                def scores(g):
                    dve.wait_ge(keys_landed[g], 16)
                    for b in range(NB):
                        n = g * NB + b
                        dve.wait_ge(S["q_spread"], n + 1)
                        step(nc.vector.tensor_tensor(prod[:, b % 2], keys[g % 2][:, b, :], qb[:, n % 2, :], ALU.mult))
                        nc.vector.tensor_reduce(score[:, :, b], prod[:, b % 2].rearrange(heads, h=NH), AX.X, ALU.add
                                                ).then_inc(S["scored"], 1)
                    step(nc.vector.tensor_tensor(new, m.q_s[:, g], m.kv_s[:, g, 0], ALU.mult))
                    step(nc.vector.tensor_reduce(s_new[:, 0], new.rearrange(heads, h=NH), AX.X, ALU.add))

                def softmax(g):
                    row = o_s[:, g, :]
                    dve.wait_ge(S["scores_turned"], g + 1)
                    step(nc.vector.tensor_reduce(s_new[:, 3], sT, AX.X, ALU.max))
                    step(nc.vector.tensor_tensor(s_new[:, 3], s_new[:, 3], s_new[:, 0], ALU.max))
                    step(nc.vector.tensor_tensor(prob, sT, bcast(s_new[:, 3].unsqueeze(2), [NB, NH, P]), ALU.subtract))
                    nc.vector.tensor_tensor(s_new[:, 1], s_new[:, 0], s_new[:, 3], ALU.subtract).then_inc(S["shifted"], 1)
                    step(nc.vector.tensor_scalar(row[:, HW:HW + NH], s_new[:, 3], -1.0, None, ALU.mult))
                    dve.wait_ge(S["exp_done"], g + 1)
                    dve.wait_ge(S["new_exp_done"], g + 1)
                    dve.wait_ge(S["probs_turned"], g + 1)
                    nc.vector.tensor_copy(pT, pb).then_inc(S["pT_ready"], 1)
                    step(nc.vector.tensor_reduce(row[:, HW + NH:OROW], prob, AX.X, ALU.add))
                    step(nc.vector.tensor_tensor(row[:, HW + NH:OROW], row[:, HW + NH:OROW], s_new[:, 2], ALU.add))

                def finish(g):
                    row = o_s[:, g, :]
                    step(nc.vector.tensor_tensor(new.rearrange(heads, h=NH), m.kv_s[:, g, 1].rearrange(heads, h=NH),
                                                 bcast(s_new[:, 2].unsqueeze(2), [NB, NH, E]), ALU.mult))
                    dve.wait_ge(S["summed_over_keys"], NB * (g + 1))
                    nc.vector.tensor_tensor(row[:, 0:HW], acc, new, ALU.add).then_inc(S["o_ready"], 1)
                    dve.wait_ge(S["o_ready"], g + 1)

                scores(0)
                for g in range(NG):
                    softmax(g)
                    if g + 1 < NG:
                        scores(g + 1)
                    finish(g)

            @block.scalar
            def _(act):
                for g in range(NG):
                    act.wait_ge(S["shifted"], g + 1)
                    nc.scalar.activation(prob, prob, ACT.Exp).then_inc(S["exp_done"], 1)
                    nc.scalar.activation(s_new[:, 2], s_new[:, 1], ACT.Exp).then_inc(S["new_exp_done"], 1)

            @block.gpsimd
            def _(pool):
                for g in range(NG):
                    pool.wait_ge(vals_landed[g], 16)
                    pool.wait_ge(S["pT_ready"], g + 1)
                    for b in range(NB):
                        n = g * NB + b
                        if n >= 2:
                            pool.wait_ge(S["summed_over_keys"], n - 1)
                        nc.gpsimd.tensor_tensor(weighed[:, b % 2].rearrange("p (h e) -> p h e", h=NH),
                                                vals[g % 2][:, b].rearrange("p (h e) -> p h e", h=NH),
                                                bcast(pT[:, :, b].unsqueeze(2), [P, NH, E]), ALU.mult
                                                ).then_inc(S["values_weighed"], 1)


def stage_conv_state(nc, m):
    with ExitStack() as ctx:
        rows = m.ring[0:28, 0, 0:24 * P]
        ps = ctx.enter_context(nc.psum_tensor("cs_ps", [P, 4, 512], F32))[:, :, 0:6 * 32].rearrange(
            "p a (c r) -> p a c r", r=32)
        landed, turned, copied = (semaphore(nc, m, "cs_" + x) for x in ("landed", "turned", "copied"))
        with nc.Block() as block:
            @block.sync
            def _(sp):
                sp.dma_start(rows[0:24], m.conv_state_rows).then_inc(landed, 16)
                sp.dma_start(rows[24:28], m.conv_w_rows).then_inc(landed, 16)
                sp.dma_start(m.s_conv[:, 0:2, :], m.conv_state_rows.rearrange("(b i) c -> b i c", i=3)[:, 1:3, :]
                             ).then_inc(m.outputs_stored, 16)
                m.n_outputs += 1

            @block.tensor
            def _(pe):
                pe.wait_ge(landed, 32)
                for cw in range(24):
                    mm = nc.tensor.transpose(ps[:, cw // 6, cw % 6, 0:28], rows[:, cw * P:(cw + 1) * P],
                                             m.ident[0:28, 0:28])
                mm.then_inc(turned, 1)

            @block.vector
            def _(dve):
                dve.wait_ge(turned, 1)
                for a in range(4):
                    nc.vector.tensor_copy(m.conv_state[:, 6 * a:6 * a + 6].rearrange("p c b i -> p c (b i)"),
                                          ps[:, a, :, 0:24])
                    nc.vector.tensor_copy(m.conv_w[:, 6 * a:6 * a + 6], ps[:, a, :, 24:28])


def stage_deltanet(nc, m):
    G3, C3 = 3, TOK // 3
    NC = NT
    with ExitStack() as ctx:
        def sb(name, shape, dt=F32):
            return ctx.enter_context(nc.sbuf_tensor("dn_" + name, shape, dt))[:]

        work, at = m.ring[:, 0:3, :].rearrange("p a b -> p (a b)"), [0]

        def carve(n):
            at[0] += n
            return work[:, at[0] - n:at[0]]

        cm = carve(2 * 4 * TOK).rearrange("p (a w t) -> p a w t", a=2, w=4)
        raw = carve(TOK + 3)
        conv = carve(TOK)
        decay = carve(1024).rearrange("p (c k) -> p c k", c=NC)
        spare = m.ring[:, 5, :].rearrange("p (a c k) -> p a c k", a=4, c=NC)
        aT, U_, Us, T = (spare[:, i] for i in range(4))
        big = [sb(f"big{i}", [P, NC, P]) for i in range(5)]
        Tt, M, Vb, Kdec, o_all = big
        A, L = M, Us
        sqs = m.ring[:, 5, 2 * P * NC:2 * P * NC + TOK]
        rs = sb("rs", [P, 2, 2, NT + 1])
        level = sb("level", [P, 8, P])
        S_ = sb("S", [P, 2, P])
        X = sb("X", [P, P])
        vn = sb("vn", [P, P])
        qs = sb("qs", [P, P])
        st_o = sb("st_o", [P, 3, NC])
        gate = sb("gate", [P, 6, NT + 1, DNH])
        beta, egc, nbg, kd, gcp, egt = (sb(x, [P, NC, DNH]) for x in ("beta", "egc", "nbg", "kd", "gcp", "egt"))
        bankp = [ctx.enter_context(nc.psum_tensor(f"dn_p{i}", [P, 512], F32))[:] for i in range(3)]
        x = [ctx.enter_context(nc.psum_tensor(f"dn_x{i}", [P, 4, P], F32))[:] for i in range(5)]
        qk_bank = [b.rearrange("p (c k) -> p c k", c=4) for b in bankp[0:2]]
        kv_bank = [x[4], x[0], x[1], x[4]]
        S = semaphores(nc, m, "dn", "ba_done gates_stepped dve_step g_ready gc_done act_gates gates_ready projected "
                       "evac_act ssq_done evac_dve spread tap0 conv_done silu_done squared rs_ready "
                       "R_done decay_ready KK_done KA_ready QK_done kv_turned kv_ready turned_A "
                       "A_ready turned_L U_ready T2_ready Us_ready M_done M_copied TMt_done TM_done "
                       "Tt_updated T_updated ks_done qs_done X_ready qs_scaled v_done vn_copied o2_done "
                       "ds_done S_ready o_added o_squared o_summed o_rstd o_scaled o_turned oT_ready "
                       "tails_kept pool_step raw_zero tapped L_half S_zero")
        S_stored = [semaphore(nc, m, f"dn_S_stored{i}") for i in range(2)]
        for h in range(DNH):
            m.last_use[m.plan.index(("dn", h))] = (S["projected"], 12 * (h + 1))
        W_ORDER = ("k", "q", "v", "z")
        WPOS = {"q": 0, "k": 1, "v": 2, "z": 3}

        def half(t, u):
            return t[:, 4 * u:4 * u + 4]

        def evac_ready(i):
            return 8 * (i + 1) + (1 if i >= 6 else 0) + (4 if i >= 9 else 0)

        def head_items():
            return [("proj", "k"), ("proj", "q"), ("ssq", "k"), ("proj", "v"), ("spread", "k"), ("ssq", "q"),
                    ("proj", "z"), ("spread", "q")]

        def chunks_of(j):
            return [(4 * j + c, P, c * P) for c in range(4)] if j < 2 else [(NT, NB, 0)]

        with nc.Block() as block:
            @block.sync
            def _(sp):
                for h in range(DNH):
                    load_chunk(sp, m, m.plan.index(("dn", h)) + 2)
                    if h >= 1:
                        sp.wait_ge(S["S_ready"], NC * h)
                        sp.dma_start(m.p_S[h - 1], S_[:, (h - 1) % 2, :]).then_inc(S_stored[(h - 1) % 2], 16)
                sp.wait_ge(S["S_ready"], NC * DNH)
                sp.dma_start(m.p_S[DNH - 1], S_[:, (DNH - 1) % 2, :]).then_inc(S_stored[1], 16)
                for i in range(2):
                    sp.wait_ge(S_stored[i], 16 * (DNH // 2))

            @block.tensor
            def _(pe):
                pe.wait_ge(m.small_landed, 16 * len(m.small_loads))
                ba = x[0].rearrange("p c k -> p (c k)")[:, 0:16 * (NT + 1)].rearrange("p (t c) -> p t c", c=16)
                for t in range(NT + 1):
                    r = P if t < NT else NB
                    for k in range(KD):
                        mm = nc.tensor.matmul(ba[0:r, t, :], m.hT[:, k, t * P:t * P + r], m.w_ba[:, k, :],
                                              start=(k == 0), stop=(k == KD - 1))
                mm.then_inc(S["ba_done"], 1)
                pe.wait_ge(S["g_ready"], 1)
                g = m.g_all[:, 0:NT, :].rearrange("p t h -> p (t h)")
                nc.tensor.matmul(x[1][:, 0, 0:64], m.triu, g, start=True, stop=True)
                nc.tensor.matmul(x[2][:, 0, 0:64], m.ones, g, start=True, stop=True).then_inc(S["gc_done"], 1)

                def projections(h):
                    weights = chunk(pe, m, "dn", h).rearrange("p (k w n) -> p k w n", k=KD, w=4)
                    acts, dves = 12 * h, 8 * h
                    read = [(S["evac_act"], acts - 2 + j) for j in range(G3)] if h else [None] * G3
                    for kind, part in head_items():
                        which = "kq".find(part)
                        if kind == "ssq":
                            pe.wait_ge(*read[0])
                            pe.wait_ge(S["squared"], 2 * h + which + 1)
                            for t in range(NT + 1):
                                n = P if t < NT else NB
                                mm = nc.tensor.matmul(bankp[0][0:n, t:t + 1], sqs[:, t * P:t * P + n], m.ones[:, 0:1],
                                                      start=True, stop=True)
                            mm.then_inc(S["ssq_done"], 1)
                            dves += 1
                            read[0] = (S["evac_dve"], dves)
                            yield
                            continue
                        for j in range(G3):
                            if read[j]:
                                pe.wait_ge(*read[j])
                            if kind == "proj":
                                for k in range(KD):
                                    mm = nc.tensor.matmul(bankp[j][:, 0:C3], weights[:, k, WPOS[part], :],
                                                          m.hT[:, k, j * C3:(j + 1) * C3],
                                                          start=(k == 0), stop=(k == KD - 1))
                                    if k == KD - 1:
                                        mm.then_inc(S["projected"], 1)
                                    yield
                                acts += 1
                                read[j] = (S["evac_act"], acts)
                            else:
                                pe.wait_ge(S["rs_ready"], 2 * h + which + 1)
                                for t, n, col in chunks_of(j):
                                    mm = nc.tensor.matmul(bankp[j][:, col:col + n],
                                                          bcast(rs[0:n, which, 1, t:t + 1], [n, P]), m.ident[0:n, 0:n],
                                                          start=True, stop=True)
                                mm.then_inc(S["spread"], 1)
                                dves += 1
                                read[j] = (S["evac_dve"], dves)
                                yield

                def fill(source, n):
                    for _ in range(n):
                        if next(source, 0) == 0:
                            return

                def prepare(h):
                    q, k, v = (cm[:, h % 2, w] for w in range(3))

                    def own(t, c):
                        return t[:, c * P:(c + 1) * P]

                    if h >= 1:
                        pe.wait_ge(S["o_added"], NC * h)
                        pe.wait_ge(S["qs_scaled"], NC * h)
                    pe.wait_ge(S["evac_dve"], 8 * h + 4)
                    for u in range(2):
                        for c in range(4):
                            kc = own(k, 4 * u + c)
                            mm = nc.tensor.matmul(x[2 + u][:, c, :], kc, kc, start=True, stop=True)
                        mm.then_inc(S["KK_done"], 1)
                    for i, (src, u) in enumerate(((k, 0), (k, 1), (v, 0), (v, 1))):
                        if i == 2:
                            pe.wait_ge(S["silu_done"], 3 * h + 3)
                        if i == 3:
                            pe.wait_ge(S["kv_ready"], 4 * h + 1)
                        for c in range(4):
                            mm = nc.tensor.transpose(kv_bank[i][:, c, :], own(src, 4 * u + c), m.ident)
                        mm.then_inc(S["kv_turned"], 1)
                    if h >= 1:
                        turn_o(h - 1)
                    pe.wait_ge(S["gates_ready"], 1)
                    for u in range(2):
                        pe.wait_ge(S["kv_ready"], 4 * h + 2 + u)
                        if h >= 1:
                            pe.wait_ge(S["oT_ready"], 2 * (h - 1) + u + 1)
                        nc.tensor.matmul(x[u], m.ident_b, bcast(m.mask_decay.unsqueeze(1), [P, 4, P]),
                                         start=True, stop=False, skip_group_check=True)
                        for c in range(4):
                            mm = nc.tensor.matmul(x[u][:, c, :], bcast(m.g_all[:, 4 * u + c, h:h + 1], [P, P]), m.triu,
                                                  start=False, stop=True, skip_group_check=True)
                        mm.then_inc(S["R_done"], 1)
                    pe.wait_ge(S["evac_dve"], 8 * h + 8)
                    for u in range(2):
                        for c in range(4):
                            mm = nc.tensor.matmul(qk_bank[u][:, c, :], own(q, 4 * u + c), own(k, 4 * u + c),
                                                  start=True, stop=True)
                        mm.then_inc(S["QK_done"], 1)
                    for u in range(2):
                        pe.wait_ge(S["KA_ready"], 2 * h + u + 1)
                        for c in range(4):
                            mm = nc.tensor.transpose(x[2 + u][:, c, :], L[:, 4 * u + c, :], m.ident)
                        mm.then_inc(S["turned_L"], 1)
                    for u in range(2):
                        pe.wait_ge(S["A_ready"], 2 * h + u + 1)
                        for c in range(4):
                            mm = nc.tensor.transpose(qk_bank[u][:, c, :], A[:, 4 * u + c, :], m.ident)
                        mm.then_inc(S["turned_A"], 1)
                    for lev in range(6):
                        for u in range(2):
                            n = 12 * h + 2 * lev + u
                            pe.wait_ge(S["Us_ready"], n + 1)
                            if lev == 0:
                                pe.wait_ge(S["T2_ready"], 2 * h + u + 1)
                                pe.wait_ge(S["decay_ready"], 8 * h + 4 * (u + 1))
                            else:
                                pe.wait_ge(S["T_updated"], 10 * h + 2 * (lev - 1) + u + 1)
                            for c in range(4):
                                mm = nc.tensor.matmul(x[u][:, c, :], Us[:, 4 * u + c, :], T[:, 4 * u + c, :],
                                                      start=True, stop=True)
                            mm.then_inc(S["M_done"], 1)
                        for u in range(2):
                            n = 12 * h + 2 * lev + u
                            pe.wait_ge(S["M_copied"], 14 * h + 2 + 2 * lev + u + 1)
                            if lev == 0:
                                pe.wait_ge(S["U_ready"], 2 * h + u + 1)
                            else:
                                pe.wait_ge(S["Tt_updated"], 12 * h + 2 * (lev - 1) + u + 1)
                            if lev < 5:
                                for c in range(4):
                                    mm = nc.tensor.matmul(x[u][:, c, :], Tt[:, 4 * u + c, :], M[:, 4 * u + c, :],
                                                          start=True, stop=True)
                                mm.then_inc(S["TM_done"], 1)
                            for c in range(4):
                                mm = nc.tensor.matmul(x[2 + u][:, c, :], M[:, 4 * u + c, :], Tt[:, 4 * u + c, :],
                                                      start=True, stop=True)
                            mm.then_inc(S["TMt_done"], 1)

                def turn_o(h):
                    for u in range(2):
                        pe.wait_ge(S["o_scaled"], h + 1)
                        if h + 1 < DNH:
                            pe.wait_ge(S["kv_ready"], 4 * (h + 1) + 2 + u)
                        for c in range(4):
                            mm = nc.tensor.transpose(x[u][:, c, :], o_all[:, 4 * u + c, :], m.ident)
                        mm.then_inc(S["o_turned"], 1)

                def recur(h, c, point):
                    q, k = (cm[:, h % 2, w, c * P:(c + 1) * P] for w in range(2))
                    n = NC * h + c
                    state = S_[:, h % 2, :]
                    if point == 0:
                        if c:
                            pe.wait_ge(S["S_ready"], n)
                        else:
                            pe.wait_ge(S["S_zero"], h + 1)
                            pe.wait_ge(S["Tt_updated"], 12 * (h + 1))
                            pe.wait_ge(S["M_copied"], 14 * (h + 1))
                        nc.tensor.matmul(x[0][:, 0, :], k, state, start=True, stop=True).then_inc(S["ks_done"], 1)
                        if n:
                            pe.wait_ge(S["qs_scaled"], n)
                        nc.tensor.matmul(x[4][:, 0, :], q, state, start=True, stop=True).then_inc(S["qs_done"], 1)
                    elif point == 1:
                        pe.wait_ge(S["X_ready"], n + 1)
                        nc.tensor.matmul(x[1][:, 0, :], Tt[:, c, :], X, start=True, stop=True).then_inc(S["v_done"], 1)
                    else:
                        pe.wait_ge(S["vn_copied"], n + 1)
                        nc.tensor.matmul(x[3][:, 0, :], Kdec[:, c, :], vn, start=True, stop=True).then_inc(S["ds_done"], 1)
                        if n:
                            pe.wait_ge(S["o_added"], n)
                        nc.tensor.matmul(x[2][:, 0, :], aT[:, c, :], vn, start=True, stop=True).then_inc(S["o2_done"], 1)

                for h in range(-1, DNH):
                    source = projections(h + 1) if h + 1 < DNH else iter(())
                    for c in range(NC):
                        for point in range(3):
                            if h >= 0:
                                recur(h, c, point)
                            fill(source, 4)
                    fill(source, 200)
                    if h + 1 < DNH:
                        prepare(h + 1)
                    else:
                        turn_o(h)

            @block.scalar
            def _(act):
                gates = Chain(act, S["act_gates"])
                act.wait_ge(S["gates_stepped"], 1)
                nb, tokens = gate[:, 1], gate[:, 0]
                gates(nc.scalar.activation(gate[:, 1], gate[:, 1], ACT.Exp, scale=-1.0))
                gates(nc.scalar.activation(gate[:, 2], gate[:, 0], ACT.Abs))
                gates(nc.scalar.activation(gate[:, 3], gate[:, 2], ACT.Exp, scale=-1.0))
                gates(nc.scalar.activation(gate[:, 4], gate[:, 3], ACT.Ln, bias=1.0))
                gates(nc.scalar.activation(m.neg_a, m.neg_a, ACT.Exp))
                act.wait_ge(S["gc_done"], 1)
                act.wait_ge(S["gates_stepped"], 2)
                gates(nc.scalar.activation(egc, gcp, ACT.Exp))
                gates(nc.scalar.activation(kd, kd, ACT.Exp))
                gates(nc.scalar.activation(egt, x[2][:, 0, 0:64].rearrange("p (t h) -> p t h", h=DNH), ACT.Exp))

                def evacuate(h, i):
                    part, j = W_ORDER[i // 3], i % 3
                    n = 12 * h + i
                    act.wait_ge(S["projected"], n + 1)
                    bank = bankp[j][:, 0:C3]
                    if part == "z":
                        ins = nc.scalar.activation(cm[:, h % 2, 3, j * C3:(j + 1) * C3], bank, ACT.Silu)
                    else:
                        if j == 0:
                            act.wait_ge(S["raw_zero"], 1)
                            if h or i >= 3:
                                act.wait_ge(S["conv_done"], 3 * h + i // 3)
                                act.wait_ge(S["tails_kept"], 3 * h + i // 3)
                        ins = nc.scalar.activation(raw[:, 3 + j * C3:3 + (j + 1) * C3], bank, ACT.Copy)
                    ins.then_inc(S["evac_act"], 1)

                def silu(h, part):
                    i = W_ORDER.index(part)
                    act.wait_ge(S["conv_done"], 3 * h + i + 1)
                    nc.scalar.activation(cm[:, h % 2, WPOS[part], :], conv, ACT.Silu).then_inc(S["silu_done"], 1)
                    if part == "v":
                        return
                    act.wait_ge(S["silu_done"], 3 * h + i + 1)
                    if h or part == "q":
                        act.wait_ge(S["ssq_done"], 2 * h + (part == "q"))
                    nc.scalar.activation(sqs, cm[:, h % 2, WPOS[part], :], ACT.Square
                                         ).then_inc(S["squared"], 1)

                def prepare(h):
                    act.wait_ge(S["gates_ready"], 1)
                    if h:
                        act.wait_ge(S["o_scaled"], h)
                    for c in range(NC):
                        act.wait_ge(S["R_done"], 2 * h + c // 4 + 1)
                        nc.scalar.activation(decay[:, c, :], x[c // 4][:, c % 4, :], ACT.Exp,
                                             bias=gcp[:, c, h:h + 1], scale=-1.0).then_inc(S["decay_ready"], 1)
                    for u in range(2):
                        act.wait_ge(S["turned_L"], 2 * h + u + 1)
                        nc.scalar.activation(half(U_, u), x[2 + u], ACT.Copy).then_inc(S["L_half"], 1)
                    for u in range(2):
                        act.wait_ge(S["turned_A"], 2 * h + u + 1)
                        nc.scalar.activation(half(aT, u), qk_bank[u], ACT.Copy).then_inc(S["M_copied"], 1)
                    for lev in range(6):
                        for u in range(2):
                            act.wait_ge(S["M_done"], 12 * h + 2 * lev + u + 1)
                            if lev:
                                act.wait_ge(S["TMt_done"], 12 * h + 2 * (lev - 1) + u + 1)
                            else:
                                act.wait_ge(S["turned_A"], 2 * h + 2)
                            nc.scalar.activation(half(M, u), x[u], ACT.Copy).then_inc(S["M_copied"], 1)

                def recur(h, c, point):
                    n = NC * h + c
                    if point == 0:
                        act.wait_ge(S["qs_done"], n + 1)
                        if n:
                            act.wait_ge(S["o_added"], n)
                        nc.scalar.activation(qs, x[4][:, 0, :], ACT.Copy, scale=egc[:, c, h:h + 1]
                                             ).then_inc(S["qs_scaled"], 1)
                    elif point == 1:
                        act.wait_ge(S["v_done"], n + 1)
                        if n:
                            act.wait_ge(S["o2_done"], n)
                        nc.scalar.activation(vn, x[1][:, 0, :], ACT.Copy).then_inc(S["vn_copied"], 1)

                for h in range(-1, DNH):
                    done = 0
                    for c in range(NC):
                        for point in range(3):
                            if h >= 0:
                                recur(h, c, point)
                            if h + 1 < DNH:
                                filled = 4 * (3 * c + point + 1)
                                while done < 12 and evac_ready(done) <= filled:
                                    evacuate(h + 1, done)
                                    done += 1
                                if (c, point) == (3, 0):
                                    silu(h + 1, "k")
                                if (c, point) == (5, 0):
                                    silu(h + 1, "q")
                    if h + 1 < DNH:
                        while done < 12:
                            evacuate(h + 1, done)
                            done += 1
                        silu(h + 1, "v")
                    if h >= 0:
                        act.wait_ge(S["o_added"], NC * (h + 1))
                        nc.scalar.activation(decay, o_all, ACT.Square).then_inc(S["o_squared"], 1)
                    if h + 1 < DNH:
                        prepare(h + 1)

            @block.vector
            def _(dve):
                step = Chain(dve, S["dve_step"])
                ba = x[0].rearrange("p c k -> p (c k)")[:, 0:16 * (NT + 1)].rearrange("p (t c) -> p t c", c=16)
                nc.vector.memset(raw[:, 0:3], 0.0).then_inc(S["raw_zero"], 1)
                step(nc.vector.memset(rs, 1.0))
                step(nc.vector.memset(gate[:, 0:2], 0.0))
                dve.wait_ge(S["ba_done"], 1)
                for t0, t1, rows in ((0, NT, P), (NT, NT + 1, NB)):
                    step(nc.vector.tensor_copy(gate[0:rows, 1, t0:t1], ba[0:rows, t0:t1, 0:DNH]))
                    step(nc.vector.tensor_tensor(gate[0:rows, 0, t0:t1], ba[0:rows, t0:t1, DNH:16],
                                                 bcast(m.dt_bias[0:rows].unsqueeze(1), [rows, t1 - t0, DNH]), ALU.add))
                nc.vector.tensor_copy(gate[:, 5], gate[:, 0]).then_inc(S["gates_stepped"], 1)
                dve.wait_ge(S["act_gates"], 5)
                dve.wait_ge(S["gates_stepped"], 1)
                step(nc.vector.tensor_scalar(gate[:, 1], gate[:, 1], 1.0, None, ALU.add))
                step(nc.vector.reciprocal(m.beta_all, gate[:, 1]))
                step(nc.vector.scalar_tensor_tensor(out=gate[:, 5], in0=gate[:, 0], scalar=0.0, in1=gate[:, 4],
                                                    op0=ALU.max, op1=ALU.add))
                step(nc.vector.tensor_scalar(m.neg_a, m.neg_a, -1.0, None, ALU.mult))
                nc.vector.tensor_tensor(m.g_all, gate[:, 5], bcast(m.neg_a.unsqueeze(1), [P, NT + 1, DNH]), ALU.mult
                                        ).then_inc(S["g_ready"], 1)
                dve.wait_ge(S["gc_done"], 1)
                gc = x[1][:, 0, 0:64].rearrange("p (t h) -> p t h", h=DNH)
                gt = x[2][:, 0, 0:64].rearrange("p (t h) -> p t h", h=DNH)
                step(nc.vector.tensor_copy(gcp, gc))
                step(nc.vector.tensor_tensor(kd, gt, gcp, ALU.subtract))
                nc.vector.tensor_copy(beta, m.beta_all[:, 0:NT]).then_inc(S["gates_stepped"], 1)
                dve.wait_ge(S["act_gates"], 8)
                dve.wait_ge(S["gates_stepped"], 2)
                nc.vector.scalar_tensor_tensor(out=nbg, in0=beta, scalar=-1.0, in1=egc, op0=ALU.mult, op1=ALU.mult
                                               ).then_inc(S["gates_ready"], 1)
                dve.wait_ge(S["gates_ready"], 1)

                def conv_taps(h, part, tap):
                    i = W_ORDER.index(part)
                    cw = 8 * WPOS[part] + h
                    n = 3 * h + i
                    if tap == 1:
                        dve.wait_ge(S["tap0"], n + 1)
                    else:
                        dve.wait_ge(S["tapped"], 2 * n + tap - 1)
                    ins = nc.vector.scalar_tensor_tensor(out=conv[:, 0:SEQ], in0=raw[:, tap:tap + SEQ],
                                                         scalar=m.conv_w[:, cw, tap:tap + 1], in1=conv[:, 0:SEQ],
                                                         op0=ALU.mult, op1=ALU.add)
                    if tap < 3:
                        ins.then_inc(S["tapped"], 1)
                        return
                    new = conv[:, SEQ:TOK]
                    step(nc.vector.tensor_scalar(new, raw[:, 3 + SEQ:3 + TOK], m.conv_w[:, cw, 3:4], None, ALU.mult))
                    for j in range(3):
                        ins = nc.vector.scalar_tensor_tensor(out=new, in0=m.conv_state[:, cw, :, j],
                                                             scalar=m.conv_w[:, cw, j:j + 1], in1=new,
                                                             op0=ALU.mult, op1=ALU.add)
                        if j < 2:
                            step(ins)
                    ins.then_inc(S["conv_done"], 1)

                def ssq_copy(h, part):
                    w = "kq".index(part)
                    dve.wait_ge(S["ssq_done"], 2 * h + w + 1)
                    if h:
                        dve.wait_ge(S["rs_ready"], 2 * (h - 1) + w + 1)
                    nc.vector.tensor_scalar(rs[:, w, 0, 0:NT], bankp[0][:, 0:NT], EPS, None, ALU.add)
                    nc.vector.tensor_scalar(rs[0:NB, w, 0, NT:NT + 1], bankp[0][0:NB, NT:NT + 1], EPS, None, ALU.add
                                            ).then_inc(S["evac_dve"], 1)

                def normalise(h, part):
                    w = "kq".index(part)
                    v = cm[:, h % 2, WPOS[part], :]
                    for j in range(G3):
                        dve.wait_ge(S["spread"], 6 * h + 3 * w + j + 1)
                        t = slice(512 * j, min(512 * j + 512, TOK))
                        n = t.stop - t.start
                        nc.vector.scalar_tensor_tensor(out=v[:, t], in0=v[:, t], scalar=(float(DK) ** -0.5 if w else 1.0),
                                                       in1=bankp[j][:, 0:n], op0=ALU.mult, op1=ALU.mult
                                                       ).then_inc(S["evac_dve"], 1)

                side = {(2, 0): lambda h: conv_taps(h, "k", 1), (2, 1): lambda h: conv_taps(h, "k", 2),
                        (2, 2): lambda h: conv_taps(h, "k", 3),
                        (4, 0): lambda h: (ssq_copy(h, "k"), conv_taps(h, "q", 1)), (4, 1): lambda h: conv_taps(h, "q", 2),
                        (4, 2): lambda h: conv_taps(h, "q", 3),
                        (6, 0): lambda h: normalise(h, "k"), (6, 1): lambda h: ssq_copy(h, "q"),
                        (7, 0): lambda h: conv_taps(h, "v", 1), (7, 1): lambda h: conv_taps(h, "v", 2),
                        (7, 2): lambda h: conv_taps(h, "v", 3)}

                def prepare(h):
                    for u in range(2):
                        dve.wait_ge(S["KK_done"], 2 * h + u + 1)
                        dve.wait_ge(S["decay_ready"], 8 * h + 4 * (u + 1))
                        if h:
                            dve.wait_ge(S["M_done"], 12 * h)
                        for c in range(4 * u, 4 * u + 4):
                            ins = nc.vector.scalar_tensor_tensor(out=L[:, c, :], in0=x[2 + u][:, c - 4 * u, :],
                                                                 scalar=beta[:, c, h:h + 1], in1=decay[:, c, :],
                                                                 op0=ALU.mult, op1=ALU.mult)
                        ins.then_inc(S["KA_ready"], 1)
                    dve.wait_ge(S["KA_ready"], 2 * h + 1)
                    step(nc.vector.tensor_tensor(half(T, 0), half(L, 0), bcast(level[:, 6, :].unsqueeze(1), [P, 4, P]),
                                                 ALU.mult))
                    nc.vector.tensor_tensor(half(T, 0), bcast(m.ident.unsqueeze(1), [P, 4, P]), half(T, 0),
                                            ALU.subtract).then_inc(S["T2_ready"], 1)
                    for u in range(2):
                        dve.wait_ge(S["QK_done"], 2 * h + u + 1)
                        nc.vector.tensor_tensor(half(A, u), qk_bank[u], half(decay, u), ALU.mult).then_inc(S["A_ready"], 1)
                    dve.wait_ge(S["Us_ready"], 12 * h)  if h else None
                    for u in range(2):
                        dve.wait_ge(S["L_half"], 2 * h + u + 1)
                        step(nc.vector.tensor_tensor(half(Tt, u), half(U_, u),
                                                     bcast(level[:, 0, :].unsqueeze(1), [P, 4, P]), ALU.mult))
                        nc.vector.tensor_tensor(half(Tt, u), bcast(m.ident.unsqueeze(1), [P, 4, P]), half(Tt, u),
                                                ALU.subtract).then_inc(S["U_ready"], 1)
                    for lev in range(6):
                        for u in range(2):
                            if lev < 5:
                                dve.wait_ge(S["TM_done"], 10 * h + 2 * lev + u + 1)
                                nc.vector.tensor_tensor(half(T, u), half(T, u), x[u], ALU.subtract
                                                        ).then_inc(S["T_updated"], 1)
                            dve.wait_ge(S["TMt_done"], 12 * h + 2 * lev + u + 1)
                            nc.vector.tensor_tensor(half(Tt, u), half(Tt, u), x[2 + u], ALU.subtract
                                                    ).then_inc(S["Tt_updated"], 1)

                def keys_values(h):
                    for i, (dst, col) in enumerate(((Kdec, kd), (Kdec, kd), (Vb, beta), (Vb, beta))):
                        u = i % 2
                        dve.wait_ge(S["kv_turned"], 4 * h + i + 1)
                        nc.vector.tensor_tensor(half(dst, u), kv_bank[i], half(bcast(col[:, :, h:h + 1], [P, NC, P]), u),
                                                ALU.mult).then_inc(S["kv_ready"], 1)

                def recur(h, c, point):
                    n = NC * h + c
                    state = S_[:, h % 2, :]
                    if point == 0:
                        dve.wait_ge(S["ks_done"], n + 1)
                        nc.vector.scalar_tensor_tensor(out=X, in0=x[0][:, 0, :], scalar=nbg[:, c, h:h + 1],
                                                       in1=Vb[:, c, :], op0=ALU.mult, op1=ALU.add
                                                       ).then_inc(S["X_ready"], 1)
                    elif point == 2:
                        dve.wait_ge(S["ds_done"], n + 1)
                        nc.vector.scalar_tensor_tensor(out=state, in0=state, scalar=egt[:, c, h:h + 1],
                                                       in1=x[3][:, 0, :], op0=ALU.mult, op1=ALU.add
                                                       ).then_inc(S["S_ready"], 1)
                        dve.wait_ge(S["o2_done"], n + 1)
                        dve.wait_ge(S["qs_scaled"], n + 1)
                        nc.vector.tensor_tensor(o_all[:, c, :], x[2][:, 0, :], qs, ALU.add).then_inc(S["o_added"], 1)

                for h in range(-1, DNH):
                    if h >= 0:
                        if h >= 2:
                            dve.wait_ge(S_stored[h % 2], 16 * (h // 2))
                        nc.vector.memset(S_[:, h % 2, :], 0.0).then_inc(S["S_zero"], 1)
                        dve.wait_ge(S["S_zero"], h + 1)
                    for c in range(NC):
                        for point in range(3):
                            if h >= 0:
                                recur(h, c, point)
                            if h + 1 < DNH and (c, point) in side:
                                side[(c, point)](h + 1)
                    if h + 1 < DNH:
                        normalise(h + 1, "q")
                    if h >= 0:
                        dve.wait_ge(S["o_squared"], h + 1)
                        nc.vector.tensor_reduce(st_o[:, 0, :], decay, AX.X, ALU.add).then_inc(S["o_summed"], 1)
                    if h + 1 < DNH:
                        keys_values(h + 1)
                    if h >= 0:
                        dve.wait_ge(S["o_rstd"], h + 1)
                        nc.vector.tensor_tensor(o_all, o_all, bcast(st_o[:, 2, :].unsqueeze(2), [P, NC, P]), ALU.mult
                                                ).then_inc(S["o_scaled"], 1)
                        dve.wait_ge(S["evac_act"], 12 * (h + 1))
                        for u in range(2):
                            dve.wait_ge(S["o_turned"], 2 * h + u + 1)
                            nc.vector.scalar_tensor_tensor(
                                out=m.oBT[:, h, 512 * u:512 * u + 512], in0=x[u].rearrange("p c k -> p (c k)"),
                                scalar=m.dn_gain[:, 0:1], in1=cm[:, h % 2, 3, 512 * u:512 * u + 512],
                                op0=ALU.mult, op1=ALU.mult).then_inc(S["oT_ready"], 1)
                    if h + 1 < DNH:
                        prepare(h + 1)

            @block.gpsimd
            def _(pool):
                step = Chain(pool, S["pool_step"])

                def tap0(h, part):
                    i = W_ORDER.index(part)
                    cw = 8 * WPOS[part] + h
                    n = 3 * h + i
                    pool.wait_ge(S["evac_act"], 12 * h + 3 * i + 3)
                    if n:
                        pool.wait_ge(S["silu_done"], n)
                    nc.gpsimd.tensor_scalar(conv[:, 0:SEQ], raw[:, 0:SEQ], m.conv_w[:, cw, 0:1], None, ALU.mult
                                            ).then_inc(S["tap0"], 1)
                    nc.gpsimd.tensor_copy(m.tails[:, cw, :], raw[:, SEQ:SEQ + 11]).then_inc(S["tails_kept"], 1)

                def rsqrt(h, part):
                    w = "kq".index(part)
                    pool.wait_ge(S["evac_dve"], 8 * h + (5 if w else 1))
                    if h:
                        pool.wait_ge(S["spread"], 6 * (h - 1) + 3 * w + 3)
                    nc.gpsimd.tensor_tensor(rs[:, w, 1], rs[:, w, 0], m.minus_half[:, 0:NT + 1], ALU.pow
                                            ).then_inc(S["rs_ready"], 1)

                step(nc.gpsimd.memset(level, 0.0))
                for lev, s in list(enumerate((1, 2, 4, 8, 16, 32))) + [(7, 64), (6, 1)]:
                    first, second = (0, 1) if lev == 6 else (1, 0)
                    view = level[:, lev, :].rearrange("p (b x r) -> p b x r", x=2, r=s)[:, :, first, :]
                    step(nc.gpsimd.memset(view, 1.0))
                    lo = -second * s
                    step(nc.gpsimd.affine_select(out=view, in_=view, compare_op=ALU.is_ge, fill=0.0, base=lo,
                                                 pattern=[[-2 * s, P // (2 * s)], [0, s]], channel_multiplier=1))
                    step(nc.gpsimd.affine_select(out=view, in_=view, compare_op=ALU.is_ge, fill=0.0, base=s - 1 - lo,
                                                 pattern=[[2 * s, P // (2 * s)], [0, s]], channel_multiplier=-1))

                for h in range(-1, DNH):
                    if h + 1 < DNH:
                        g = h + 1
                        tap0(g, "k")
                        tap0(g, "q")
                        rsqrt(g, "k")
                        tap0(g, "v")
                        rsqrt(g, "q")
                    if h >= 0:
                        pool.wait_ge(S["o_summed"], h + 1)
                        step(nc.gpsimd.tensor_scalar(st_o[:, 1, :], st_o[:, 0, :], 1.0 / DK, EPS, ALU.mult, ALU.add))
                        nc.gpsimd.tensor_tensor(st_o[:, 2, :], st_o[:, 1, :], m.minus_half[:, 0:NC], ALU.pow
                                                ).then_inc(S["o_rstd"], 1)
                    if h + 1 < DNH:
                        g = h + 1
                        pool.wait_ge(S["evac_dve"], 8 * g + 8)
                        pool.wait_ge(S["silu_done"], 3 * g + 3)
                        pool.wait_ge(S["evac_act"], 12 * g + 12)
                        step(nc.gpsimd.tensor_copy(m.dn_s[:, :, g, :], cm[:, g % 2, :, SEQ:TOK]))
                        pool.wait_ge(S["KA_ready"], 2 * g + 2)
                        step(nc.gpsimd.tensor_tensor(half(T, 1), half(L, 1), bcast(level[:, 6, :].unsqueeze(1), [P, 4, P]),
                                                     ALU.mult))
                        pool.wait_ge(S["T2_ready"], 2 * g + 1)
                        nc.gpsimd.tensor_tensor(half(T, 1), bcast(m.ident.unsqueeze(1), [P, 4, P]), half(T, 1),
                                                ALU.subtract).then_inc(S["T2_ready"], 1)
                        pool.wait_ge(S["turned_L"], 2 * g + 2)
                        for lev in range(6):
                            for u in range(2):
                                n = 12 * g + 2 * lev + u
                                if lev == 0:
                                    pool.wait_ge(S["L_half"], 2 * g + u + 1)
                                if n >= 2:
                                    pool.wait_ge(S["M_done"], n - 1)
                                nc.gpsimd.tensor_tensor(half(Us, u), half(U_, u),
                                                        bcast(level[:, 1 + lev if lev < 5 else 7, :].unsqueeze(1), [P, 4, P]),
                                                        ALU.mult).then_inc(S["Us_ready"], 1)


def stage_decode_deltanet(nc, m):
    HB = DNH * NB
    with ExitStack() as ctx:
        def sb(name, shape, dt=F32):
            return ctx.enter_context(nc.sbuf_tensor("dd_" + name, shape, dt))[:]

        def ps(name, shape):
            return ctx.enter_context(nc.psum_tensor("dd_" + name, shape, F32))[:]

        state = [m.ring[:, j, :].rearrange("p (b h v) -> p b h v", b=4, h=DNH) for j in (2, 5)]
        diag = sb("diag", [NB, 2, DNH, NB])
        beta, eg, qk, vnew, o, o2, rstd, junk = (sb(x, [P, DNH, NB]) for x in
                                                 ("beta", "eg", "qk", "vnew", "o", "o2", "rstd", "junk"))
        qkprod = sb("qkprod", [P, DNH, NB])
        outer = sb("outer", [P, 2, 4, DK])
        tail_rows = sb("tail_rows", [11, 24 * P])
        small = ps("small", [P, 512])
        products = ps("products", [P, 512])[:, 0:2 * HB].rearrange("p (h b w) -> p h b w", h=DNH, b=NB)
        spread = ps("spread", [P, 2, 4, DK])
        tails = ps("tails", [P, 4, 512])[0:11]
        S = semaphores(nc, m, "dd", "diag_ready gates_spread eg_ready step qk_spread multiplied vnew_ready v_spread "
                       "outer_ready S_ready squares_summed mean_ready rstd_ready tails_turned tails_copied")
        S_landed = [semaphore(nc, m, f"dd_S_landed{i}") for i in range(2)]
        q, k, v, z = (m.dn_s[:, w] for w in range(4))
        pairs = [(b, h) for b in range(NB) for h in range(DNH)]

        with nc.Block() as block:
            @block.sync
            def _(sp):
                for i in range(2):
                    sp.dma_start(state[i].rearrange("p b h v -> p (b h) v"),
                                 m.state_S[4 * i:4 * i + 4].rearrange("b h k v -> k (b h) v")).then_inc(S_landed[i], 16)
                sp.wait_ge(S["tails_copied"], 6)
                sp.dma_start(m.p_conv, tail_rows[0:3]).then_inc(m.outputs_stored, 16)
                sp.dma_start(m.s_conv[:, 2, :], tail_rows[3:11]).then_inc(m.outputs_stored, 16)
                for i in range(2):
                    sp.wait_ge(S["S_ready"], 32 * (i + 1))
                    sp.dma_start(m.s_S[4 * i:4 * i + 4].rearrange("b h k v -> k (b h) v"),
                                 state[i].rearrange("p b h v -> p (b h) v")).then_inc(m.outputs_stored, 16)
                m.n_outputs += 4
                sp.wait_ge(m.outputs_stored, 16 * m.n_outputs)

            @block.tensor
            def _(pe):
                pe.wait_ge(S["diag_ready"], 3)
                nc.tensor.matmul(small[:, 0:2 * HB], m.ones[0:NB, :], diag.rearrange("p w h b -> p (w h b)"),
                                 start=True, stop=True)
                nc.tensor.matmul(small[:, 2 * HB:3 * HB], m.ones, qkprod.rearrange("p h b -> p (h b)"),
                                 start=True, stop=True).then_inc(S["gates_spread"], 1)
                for n, (b, h) in enumerate(pairs):
                    if n % 32 == 0:
                        pe.wait_ge(S_landed[n // 32], 16)
                    mm = nc.tensor.matmul(products[:, h, b, :], state[b // 4][:, b % 4, h, :], m.dn_s[:, 0:2, h, b],
                                          start=True, stop=True)
                mm.then_inc(S["multiplied"], 1)
                for j in range(6):
                    if j >= 4:
                        pe.wait_ge(S["tails_copied"], j - 3)
                    for c in range(4):
                        mm = nc.tensor.transpose(tails[:, j % 4, c * P:(c + 1) * P], m.tails[:, 4 * j + c, :], m.ident)
                    mm.then_inc(S["tails_turned"], 1)
                pe.wait_ge(S["vnew_ready"], 1)
                for j in range(16):
                    if j >= 2:
                        pe.wait_ge(S["outer_ready"], 4 * (j - 1))
                    for c in range(4):
                        b, h = pairs[4 * j + c]
                        mm = nc.tensor.matmul(spread[:, j % 2, c, :], bcast(vnew[:, h, b:b + 1], [P, P]), m.ident,
                                              start=True, stop=True)
                    mm.then_inc(S["v_spread"], 1)
                    if j == 0:
                        pe.wait_ge(S["vnew_ready"], 2)
                        nc.tensor.matmul(small[:, 3 * HB:4 * HB], m.ones, o2.rearrange("p h b -> p (h b)"),
                                         start=True, stop=True).then_inc(S["squares_summed"], 1)

            @block.vector
            def _(dve):
                step = Chain(dve, S["step"])
                for w, src in enumerate((m.beta_all, m.g_all)):
                    nc.vector.tensor_tensor(diag[:, w], bcast(src[0:NB, NT, :].unsqueeze(2), [NB, DNH, NB]),
                                            bcast(m.ident[0:NB, 0:NB].unsqueeze(1), [NB, DNH, NB]), ALU.mult
                                            ).then_inc(S["diag_ready"], 1)
                nc.vector.tensor_tensor(qkprod, q, k, ALU.mult).then_inc(S["diag_ready"], 1)
                dve.wait_ge(S["eg_ready"], 1)

                def at(i):
                    return small[:, i * HB:(i + 1) * HB].rearrange("p (h b) -> p h b", h=DNH)

                step(nc.vector.tensor_copy(beta, at(0)))
                step(nc.vector.tensor_copy(qk, at(2)))
                dve.wait_ge(S["multiplied"], 1)
                step(nc.vector.tensor_tensor(junk, eg, products[:, :, :, 1], ALU.mult))
                step(nc.vector.tensor_tensor(junk, v, junk, ALU.subtract))
                nc.vector.tensor_tensor(vnew, beta, junk, ALU.mult).then_inc(S["vnew_ready"], 1)
                step(nc.vector.tensor_tensor(o, eg, products[:, :, :, 0], ALU.mult))
                dve.wait_ge(S["vnew_ready"], 1)
                step(nc.vector.tensor_tensor(junk, qk, vnew, ALU.mult))
                step(nc.vector.tensor_tensor(o, o, junk, ALU.add))
                nc.vector.tensor_tensor(o2, o, o, ALU.mult).then_inc(S["vnew_ready"], 1)
                step(nc.vector.tensor_tensor(o, o, z, ALU.mult))
                step(nc.vector.tensor_scalar(o, o, m.dn_gain[:, 0:1], None, ALU.mult))
                dve.wait_ge(S["squares_summed"], 1)
                nc.vector.tensor_scalar(junk, at(3), 1.0 / DK, EPS, ALU.mult, ALU.add).then_inc(S["mean_ready"], 1)
                for n, (b, h) in enumerate(pairs):
                    dve.wait_ge(S["outer_ready"], n + 1)
                    s = state[b // 4][:, b % 4, h, :]
                    nc.vector.scalar_tensor_tensor(s, s, eg[:, h, b:b + 1], outer[:, n // 4 % 2, n % 4, :], ALU.mult,
                                                   ALU.add).then_inc(S["S_ready"], 1)
                dve.wait_ge(S["rstd_ready"], 1)
                step(nc.vector.tensor_tensor(m.oBT[:, :, SEQ:TOK], o, rstd, ALU.mult))

            @block.gpsimd
            def _(pool):
                pool.wait_ge(S["mean_ready"], 1)
                nc.gpsimd.tensor_tensor(rstd, junk, m.minus_half[:, 0:HB].rearrange("p (h b) -> p h b", h=DNH), ALU.pow
                                        ).then_inc(S["rstd_ready"], 1)

            @block.scalar
            def _(act):
                act.wait_ge(S["gates_spread"], 1)
                nc.scalar.activation(eg.rearrange("p h b -> p (h b)"), small[:, HB:2 * HB], ACT.Exp
                                     ).then_inc(S["eg_ready"], 1)
                for j in range(6):
                    act.wait_ge(S["tails_turned"], j + 1)
                    nc.scalar.activation(tail_rows[:, 512 * j:512 * (j + 1)], tails[:, j % 4, :], ACT.Copy
                                         ).then_inc(S["tails_copied"], 1)
                for n, (b, h) in enumerate(pairs):
                    j, c = divmod(n, 4)
                    if c == 0:
                        act.wait_ge(S["v_spread"], j + 1)
                        if j >= 2:
                            act.wait_ge(S["S_ready"], 4 * (j - 1))
                    nc.scalar.activation(outer[:, j % 2, c, :], spread[:, j % 2, c, :], ACT.Copy, scale=k[:, h, b:b + 1]
                                         ).then_inc(S["outer_ready"], 1)


TILES = [(t, P) for t in range(NT)] + [(NT, NB)]


def stage_mix(nc, m):
    with ExitStack() as ctx:
        def sb(name, shape, dt=F32):
            return ctx.enter_context(nc.sbuf_tensor("mx_" + name, shape, dt))[:]

        o_in = sb("o_in", [P, NG, OROW])
        lse, weight = (sb(x, [P, NG, NH]) for x in ("lse", "weight"))
        top, total = (sb(x, [P, NH]) for x in ("top", "total"))
        oAT = sb("oAT", [P, 4, P])
        gates = sb("gates", [P, 2, 512])
        mixed = sb("mixed", [P, 2, 512])
        part = sb("part", [P, 512])
        w_a = sb("w_a", [P, 4, D])
        prod = ctx.enter_context(nc.psum_tensor("mx_prod", [P, 6, 512], F32))[:]
        oA_ps = ctx.enter_context(nc.psum_tensor("mx_oA", [P, 4, P], F32))[:]
        mix_ps = ctx.enter_context(nc.psum_tensor("mx_mix", [P, 4, P], F32))[:]
        S = semaphores(nc, m, "mx", "w_a_landed ln_done lse_ready exp_done merge_step oA_ready oA_turned oAT_ready "
                       "product_done gate_ready y_used mix_ready mix_turned mixT_ready zeros_ready y_cleared")
        zeros = m.tails.rearrange("p c r -> p (c r)")[:, 0:256]
        y_cleared = m.y_scr.rearrange("(p f r) (c n) -> p f (r c) n", p=P, r=4, n=256)
        fills = y_cleared.shape[1]
        o_landed = semaphore(nc, m, "mx_o_landed")
        items = [("ga", 0), ("gb", 0), ("ya", 0), ("yb", 0), ("ga", 1), ("gb", 1), ("ya", 1), ("yb", 1)]

        def gates_upto(n):
            return 4 * (n // 8) + (1, 2, 2, 2, 3, 4, 4, 4)[n % 8]

        def ys_upto(n):
            return 4 * (n // 8) + (0, 0, 1, 2, 2, 2, 3, 4)[n % 8]

        with nc.Block() as block:
            @block.sync
            def _(sp):
                sp.dma_start(o_in, m.o_scr[0:P]).then_inc(o_landed, 16)
                load_chunk(sp, m, m.plan.index(("gb", 0)))
                sp.dma_start(w_a, m.w_out_a.rearrange("(k p) n -> p k n", p=P)).then_inc(S["w_a_landed"], 16)
                for c in (("wb", 0), ("gb", 1), ("wb", 1)):
                    load_chunk(sp, m, m.plan.index(c))
                for t, r in TILES[1:]:
                    sp.wait_ge(S["oA_ready"], t)
                    sp.wait_ge(S["oA_turned"], t)
                    src = m.o_scr[t * P:(t + 1) * P] if t < NT else m.o_s_scr
                    sp.dma_start(o_in[0:r], src).then_inc(o_landed, 16)
                    if t == 1:
                        sp.wait_ge(S["zeros_ready"], 1)
                    for i in range(fills * (t - 1) // NT, fills * t // NT):
                        sp.dma_start(y_cleared[:, i], bcast(zeros.unsqueeze(1), [P, 16, 256])).then_inc(S["y_cleared"], 16)
                for half in range(2):
                    sp.wait_ge(S["product_done"], 8 * NT + half + 1)
                    load_chunk(sp, m, m.plan.index(("wo", half)))
                sp.wait_ge(S["y_cleared"], 16 * fills)

            @block.gpsimd
            def _(pool):
                nc.gpsimd.memset(zeros, 0.0).then_inc(S["zeros_ready"], 1)

            @block.tensor
            def _(pe):
                def mix_turn(t):
                    r = TILES[t][1]
                    for half in range(2):
                        pe.wait_ge(S["mix_ready"], 2 * t + half + 1)
                        if 2 * t + half:
                            pe.wait_ge(S["mixT_ready"], 2 * t + half)
                        for c in range(4):
                            mm = nc.tensor.transpose(mix_ps[:, c, 0:r], mixed[0:r, half, c * P:(c + 1) * P],
                                                     m.ident[0:r, 0:r])
                        mm.then_inc(S["mix_turned"], 1)

                for t, r in TILES:
                    for i, (kind, half) in enumerate(items):
                        n = 8 * t + i
                        if i == 2:
                            if t >= 1:
                                mix_turn(t - 1)
                            pe.wait_ge(S["oA_ready"], t + 1)
                            if t >= 1:
                                pe.wait_ge(S["oAT_ready"], t)
                            for c in range(4):
                                mm = nc.tensor.transpose(oA_ps[:, c, 0:r], o_in[0:r, 0, c * P:(c + 1) * P],
                                                         m.ident[0:r, 0:r])
                            mm.then_inc(S["oA_turned"], 1)
                            pe.wait_ge(S["oAT_ready"], t + 1)
                        if n >= 6:
                            last = n - 6
                            if items[last % 8][0][0] == "g":
                                pe.wait_ge(S["gate_ready"], gates_upto(last))
                            else:
                                pe.wait_ge(S["y_used"], ys_upto(last))
                        out = prod[0:r, n % 6, :]
                        if kind == "ya":
                            if n == 2:
                                pe.wait_ge(S["w_a_landed"], 16)
                            for k in range(4):
                                mm = nc.tensor.matmul(out, oAT[:, k, 0:r], w_a[:, k, half * 512:(half + 1) * 512],
                                                      start=(k == 0), stop=(k == 3))
                        else:
                            w = chunk(pe, m, "wb" if kind == "yb" else kind, half).rearrange("p (k n) -> p k n", k=KD)
                            src = m.oBT if kind == "yb" else m.hT
                            for k in range(KD):
                                mm = nc.tensor.matmul(out, src[:, k, t * P:t * P + r], w[:, k, :],
                                                      start=(k == 0), stop=(k == KD - 1))
                        mm.then_inc(S["product_done"], 1)
                mix_turn(NT)

            @block.scalar
            def _(act):
                for t, r in TILES:
                    den = o_in[0:r, :, HW + NH:OROW]
                    act.wait_ge(o_landed, 16 * (t + 1))
                    nc.scalar.activation(lse[0:r], den, ACT.Ln).then_inc(S["ln_done"], 1)
                    act.wait_ge(S["lse_ready"], t + 1)
                    nc.scalar.activation(lse[0:r], lse[0:r], ACT.Exp).then_inc(S["exp_done"], 1)
                    act.wait_ge(S["oA_turned"], t + 1)
                    nc.scalar.activation(oAT[:, :, 0:r], oA_ps[:, :, 0:r], ACT.Copy).then_inc(S["oAT_ready"], 1)
                    for half in range(2):
                        for w in range(2):
                            g = 4 * t + 2 * half + w
                            act.wait_ge(S["product_done"], 8 * t + 4 * half + w + 1)
                            if g >= 2:
                                act.wait_ge(S["y_used"], g - 1)
                            nc.scalar.activation(gates[0:r, w], prod[0:r, (8 * t + 4 * half + w) % 6], ACT.Sigmoid
                                                 ).then_inc(S["gate_ready"], 1)

            @block.vector
            def _(dve):
                step = Chain(dve, S["merge_step"])

                def merge(t, r):
                    den = o_in[0:r, :, HW + NH:OROW]
                    l, w, tp, s = lse[0:r], weight[0:r], top[0:r], total[0:r]
                    dve.wait_ge(S["ln_done"], t + 1)
                    step(nc.vector.tensor_tensor(l, l, o_in[0:r, :, HW:HW + NH], ALU.subtract))
                    step(nc.vector.tensor_reduce(tp, l.rearrange("p g h -> p h g"), AX.X, ALU.max))
                    nc.vector.tensor_tensor(l, l, bcast(tp.unsqueeze(1), [r, NG, NH]), ALU.subtract
                                            ).then_inc(S["lse_ready"], 1)
                    dve.wait_ge(S["exp_done"], t + 1)
                    step(nc.vector.tensor_reduce(s, l.rearrange("p g h -> p h g"), AX.X, ALU.add))
                    step(nc.vector.tensor_tensor(w, den, bcast(s.unsqueeze(1), [r, NG, NH]), ALU.mult))
                    step(nc.vector.reciprocal(w, w))
                    step(nc.vector.tensor_tensor(w, w, l, ALU.mult))
                    o = o_in[0:r, :, 0:HW]
                    for g in range(NG):
                        og = o[:, g, :].rearrange("p (h e) -> p h e", h=NH)
                        step(nc.vector.tensor_tensor(og, og, bcast(w[:, g, :].unsqueeze(2), [r, NH, E]), ALU.mult))
                    step(nc.vector.tensor_tensor(o[:, 0], o[:, 0], o[:, 1], ALU.add))
                    nc.vector.tensor_tensor(o[:, 0], o[:, 0], o[:, 2], ALU.add).then_inc(S["oA_ready"], 1)

                def turn_copy(t, r):
                    for half in range(2):
                        dve.wait_ge(S["mix_turned"], 2 * t + half + 1)
                        nc.vector.tensor_copy(m.hT[:, 4 * half:4 * half + 4, t * P:t * P + r], mix_ps[:, :, 0:r]
                                              ).then_inc(S["mixT_ready"], 1)

                for t, r in TILES:
                    merge(t, r)
                    if t >= 1:
                        turn_copy(t - 1, P)
                    for half in range(2):
                        n = 8 * t + 4 * half
                        dve.wait_ge(S["product_done"], n + 3)
                        dve.wait_ge(S["gate_ready"], 4 * t + 2 * half + 1)
                        if t >= 1:
                            dve.wait_ge(S["mix_turned"], 2 * (t - 1) + half + 1)
                        nc.vector.tensor_tensor(mixed[0:r, half], prod[0:r, (n + 2) % 6], gates[0:r, 0], ALU.mult
                                                ).then_inc(S["y_used"], 1)
                        dve.wait_ge(S["product_done"], n + 4)
                        dve.wait_ge(S["gate_ready"], 4 * t + 2 * half + 2)
                        nc.vector.tensor_tensor(part[0:r], prod[0:r, (n + 3) % 6], gates[0:r, 1], ALU.mult
                                                ).then_inc(S["y_used"], 1)
                        dve.wait_ge(S["y_used"], 4 * t + 2 * half + 2)
                        nc.vector.tensor_tensor(mixed[0:r, half], mixed[0:r, half], part[0:r], ALU.add
                                                ).then_inc(S["mix_ready"], 1)
                        dve.wait_ge(S["mix_ready"], 2 * t + half + 1)
                turn_copy(NT, NB)


def stage_residual(nc, m):
    with ExitStack() as ctx:
        def sb(name, shape, dt=F32):
            return ctx.enter_context(nc.sbuf_tensor("rs_" + name, shape, dt))[:]

        xs, hs = (sb(x, [P, 2, D]) for x in ("xs", "hs"))
        junk = sb("junk", [P, D])
        stat = sb("stat", [P, 2, 3])
        turned = sb("turned", [P, KD, P])
        x1_ps = ctx.enter_context(nc.psum_tensor("rs_x1", [P, 2, 2, 512], F32))[:]
        h_ps = ctx.enter_context(nc.psum_tensor("rs_h", [P, KD, P], F32))[:]
        l_ps = ctx.enter_context(nc.psum_tensor("rs_l", [P, 2, 512], F32))[:]
        S = semaphores(nc, m, "rs", "x1_done x1_ready squared mean_ready rstd_ready h_ready h_turned hT_ready "
                       "logits_done logits_ready zeroed")
        x_landed = [semaphore(nc, m, f"rs_x_landed{i}") for i in range(2)]
        h_stored = [semaphore(nc, m, f"rs_h_stored{i}") for i in range(2)]

        with nc.Block() as block:
            @block.sync
            def _(sp):
                def load(t, r):
                    if t >= 2:
                        sp.wait_ge(S["x1_ready"], 2 * (t - 1))
                    src = m.x_prompt[t * P:(t + 1) * P, :] if t < NT else m.x_sample
                    sp.dma_start(xs[0:r, t % 2, :], src).then_inc(x_landed[t % 2], 16)

                load(*TILES[0])
                for t, r in TILES:
                    if t < NT:
                        load(*TILES[t + 1])
                    sp.wait_ge(S["h_ready"], t + 1)
                    sp.dma_start(m.h2_scr[t * P:t * P + r, :], hs[0:r, t % 2, :]).then_inc(h_stored[t % 2], 16)
                sp.wait_ge(h_stored[0], 16 * 5)
                sp.wait_ge(h_stored[1], 16 * 4)

            @block.tensor
            def _(pe):
                def turn(t, r):
                    pe.wait_ge(S["h_ready"], t + 1)
                    if t >= 1:
                        pe.wait_ge(S["hT_ready"], t)
                    for k in range(KD):
                        mm = nc.tensor.transpose(h_ps[:, k, 0:r], hs[0:r, t % 2, k::KD], m.ident[0:r, 0:r])
                    mm.then_inc(S["h_turned"], 1)

                def route(t, r):
                    pe.wait_ge(S["hT_ready"], t + 1)
                    if t >= 2:
                        pe.wait_ge(S["logits_ready"], t - 1)
                    for k in range(KD):
                        mm = nc.tensor.matmul(l_ps[0:r, t % 2, 0:36], turned[:, k, 0:r], m.w_router[:, k, :],
                                              start=(k == 0), stop=(k == KD - 1))
                    mm.then_inc(S["logits_done"], 1)

                for t, r in TILES:
                    for half in range(2):
                        w = chunk(pe, m, "wo", half).rearrange("p (k n) -> p k n", k=KD)
                        if t >= 2:
                            pe.wait_ge(S["x1_ready"], 2 * (t - 2) + half + 1)
                        for k in range(KD):
                            mm = nc.tensor.matmul(x1_ps[0:r, t % 2, half, :], m.hT[:, k, t * P:t * P + r], w[:, k, :],
                                                  start=(k == 0), stop=(k == KD - 1))
                        mm.then_inc(S["x1_done"], 1)
                        if t >= 1:
                            (turn, route)[half](*TILES[t - 1])
                turn(*TILES[NT])
                route(*TILES[NT])

            @block.vector
            def _(dve):
                def copy_hT(t, r):
                    dve.wait_ge(S["h_turned"], t + 1)
                    if t >= 1:
                        dve.wait_ge(S["logits_done"], t)
                    nc.vector.tensor_tensor(turned[:, :, 0:r], h_ps[:, :, 0:r], bcast(m.ln2.unsqueeze(2), [P, KD, r]),
                                            ALU.mult).then_inc(S["hT_ready"], 1)

                def keep_logits(t, r):
                    dve.wait_ge(S["logits_done"], t + 1)
                    nc.vector.tensor_tensor(m.logits[0:r, t, :], l_ps[0:r, t % 2, 0:36], m.b_router[0:r], ALU.add
                                            ).then_inc(S["logits_ready"], 1)

                nc.vector.memset(m.logits, 0.0).then_inc(S["zeroed"], 1)
                dve.wait_ge(S["zeroed"], 1)
                for t, r in TILES:
                    x1 = m.x1[t]
                    if t >= 1:
                        copy_hT(*TILES[t - 1])
                    for half in range(2):
                        c = slice(512 * half, 512 * half + 512)
                        dve.wait_ge(S["x1_done"], 2 * t + half + 1)
                        dve.wait_ge(x_landed[t % 2], 16 * (t // 2 + 1))
                        nc.vector.tensor_tensor(x1[0:r, c], x1_ps[0:r, t % 2, half, :], xs[0:r, t % 2, c], ALU.add
                                                ).then_inc(S["x1_ready"], 1)
                    dve.wait_ge(S["rstd_ready"], t + 1)
                    if t >= 2:
                        dve.wait_ge(S["h_turned"], t - 1)
                        dve.wait_ge(h_stored[t % 2], 16 * (t // 2))
                    nc.vector.tensor_scalar(hs[0:r, t % 2], x1[0:r], stat[0:r, t % 2, 2:3], None, ALU.mult
                                            ).then_inc(S["h_ready"], 1)
                    if t >= 1:
                        keep_logits(*TILES[t - 1])
                copy_hT(*TILES[NT])
                keep_logits(*TILES[NT])

            @block.scalar
            def _(act):
                for t, r in TILES:
                    act.wait_ge(S["x1_ready"], 2 * t + 2)
                    if t >= 2:
                        act.wait_ge(S["mean_ready"], t - 1)
                    if t >= 1:
                        act.wait_ge(S["squared"], t)
                    nc.scalar.activation(junk[0:r], m.x1[t][0:r], ACT.Square, accum_out=stat[0:r, t % 2, 0:1]
                                         ).then_inc(S["squared"], 1)

            @block.gpsimd
            def _(pool):
                for t, r in TILES:
                    s = stat[0:r, t % 2]
                    pool.wait_ge(S["squared"], t + 1)
                    nc.gpsimd.tensor_scalar(s[:, 1:2], s[:, 0:1], 1.0 / D, EPS, ALU.mult, ALU.add
                                            ).then_inc(S["mean_ready"], 1)
                    pool.wait_ge(S["mean_ready"], t + 1)
                    if t >= 2:
                        pool.wait_ge(S["h_ready"], t - 1)
                    nc.gpsimd.tensor_tensor(s[:, 2:3], s[:, 1:2], m.minus_half[0:r, 0:1], ALU.pow
                                            ).then_inc(S["rstd_ready"], 1)


CE = mybir.EngineType


def stage_route(nc, m):
    T = NT + 1
    with ExitStack() as ctx:
        def sb(name, shape, dt=F32):
            return ctx.enter_context(nc.sbuf_tensor("rt_" + name, shape, dt))[:]

        count_i = sb("count_i", [P, 64], I32)
        count_f, by128, by2, keys = (sb(x, [P, 64]) for x in ("count_f", "by128", "by2", "keys"))
        token_i = sb("token_i", [P, T], I32)
        token = sb("token", [P, T])
        valid = sb("valid", [P, T])
        upto_mask = sb("upto_mask", [P, NE, NE])
        zeros = sb("zeros", [MAXB, P])
        top = sb("top", [P, 4, T])
        group = sb("group", [P, T, NGE])
        shifted = sb("shifted", [P, T, NGE])
        pick = sb("pick", [P, T, NGE, EPG])
        le = sb("le", [P, T, EPG])
        le2 = sb("le2", [P, T, EPG])
        one = [sb(f"one{i}", [P, T, EPG]) for i in range(2)]
        value = [sb(f"value{i}", [P, T]) for i in range(2)]
        hot = [sb(f"hot{i}", [P, T, NE]) for i in range(2)]
        both = sb("both", [P, T, NE])
        e2, s2, pg = (sb(x, [P, T]) for x in ("e2", "s2", "pg"))
        cnt, blocks, ends, start = (sb(x, [P, NE]) for x in ("cnt", "blocks", "ends", "start"))
        over = sb("over", [P, NE, 9])
        ends_by = sb("ends_by", [P, NE, NE])
        row = sb("row", [P, T, NE])
        dest = sb("dest", [P, 2, T])
        owner = sb("owner", [P, MAXB])
        owner_by = sb("owner_by", [P, MAXB, NE])
        pairs_by = sb("pairs_by", [P, 25])
        pairs = sb("pairs", [P, 1])
        rows = sb("rows", [MAXB, P])
        ranks = ctx.enter_context(nc.psum_tensor("rt_ranks", [P, 512], F32))[:, 0:T * NE].rearrange(
            "p (t e) -> p t e", t=T)
        counts = ctx.enter_context(nc.psum_tensor("rt_counts", [P, 512], F32))[:, 0:NE]
        turned = ctx.enter_context(nc.psum_tensor("rt_turned", [P, 512], F32))[:, 0:MAXB]
        S = semaphores(nc, m, "rt", "iotas step exp_done shifted second_ready pool_step consts hots_ready ranked "
                       "dest_ready zeros_ready cleared scattered rows_landed rows_turned")
        lg = m.logits[:, :, 0:4]
        le_all = m.logits[:, :, 4:36].rearrange("p t (g e) -> p t g e", g=NGE)

        with nc.Block() as block:
            @block.sync
            def _(sp):
                sp.wait_ge(S["zeros_ready"], 1)
                sp.dma_start(m.row_scr.rearrange("(b p) c -> b (p c)", p=P), zeros).then_inc(S["cleared"], 16)
                sp.wait_ge(S["scattered"], 16 * 2 * T)
                sp.dma_start(rows, m.row_scr.rearrange("(b p) c -> b (p c)", p=P)).then_inc(S["rows_landed"], 16)

            @block.gpsimd
            def _(pool):
                step = Chain(pool, S["pool_step"])
                nc.gpsimd.iota(count_i, pattern=[[1, 64]], base=0, channel_multiplier=0).then_inc(S["iotas"], 1)
                nc.gpsimd.iota(token_i, pattern=[[P, T]], base=0, channel_multiplier=1).then_inc(S["iotas"], 1)
                nc.gpsimd.memset(zeros, 0.0).then_inc(S["zeros_ready"], 1)
                step(nc.gpsimd.memset(valid, 1.0))
                step(nc.gpsimd.affine_select(out=valid[:, NT:T], in_=valid[:, NT:T], compare_op=ALU.is_ge, fill=0.0,
                                             base=NB - 1, pattern=[[0, 1]], channel_multiplier=-1))
                step(nc.gpsimd.memset(upto_mask, 1.0))
                nc.gpsimd.affine_select(out=upto_mask, in_=upto_mask, compare_op=ALU.is_ge, fill=0.0, base=0,
                                        pattern=[[1, NE], [-1, NE]], channel_multiplier=0).then_inc(S["consts"], 1)
                pool.wait_ge(S["cleared"], 16)
                pool.wait_ge(S["dest_ready"], 1)
                for t, r in TILES:
                    for i in range(2):
                        nc.gpsimd.indirect_dma_start(m.row_scr, bass.IndirectOffsetOnAxis(m.dest_u[0:r, i, t:t + 1], 0),
                                                     token[0:r, t:t + 1], None).then_inc(S["scattered"], 16)

            @block.scalar
            def _(act):
                act.wait_ge(S["shifted"], 1)
                nc.scalar.activation(shifted, shifted, ACT.Exp).then_inc(S["exp_done"], 1)
                act.wait_ge(S["second_ready"], 1)
                nc.scalar.activation(e2, e2, ACT.Exp).then_inc(S["exp_done"], 1)

            @block.tensor
            def _(pe):
                pe.wait_ge(S["hots_ready"], 1)
                for t in range(T):
                    nc.tensor.matmul(ranks[:, t, :], m.triu, both[:, t, :], start=True, stop=(t == 0))
                    for u in range(t):
                        nc.tensor.matmul(ranks[:, t, :], m.ones, both[:, u, :], start=False, stop=(u == t - 1))
                for t in range(T):
                    mm = nc.tensor.matmul(counts, m.ones, both[:, t, :], start=(t == 0), stop=(t == T - 1))
                mm.then_inc(S["ranked"], 1)
                pe.wait_ge(S["rows_landed"], 16)
                nc.tensor.transpose(turned, rows, m.ident[0:MAXB, 0:MAXB]).then_inc(S["rows_turned"], 1)

            @block.vector
            def _(dve):
                step = Chain(dve, S["step"])

                def first_hot(out, x, n, key):
                    step(nc.vector.tensor_reduce(top[:, key], x, AX.X, ALU.max))
                    step(nc.vector.tensor_tensor(out, x, bcast(top[:, key].unsqueeze(2), [P, T, n]), ALU.is_equal))
                    step(nc.vector.tensor_tensor(out, out, bcast(keys[:, 0:n].unsqueeze(1), [P, T, n]), ALU.mult))
                    step(nc.vector.tensor_reduce(top[:, 3], out, AX.X, ALU.max))
                    step(nc.vector.tensor_tensor(out, out, bcast(top[:, 3].unsqueeze(2), [P, T, n]), ALU.is_equal))

                dve.wait_ge(S["iotas"], 2)
                step(nc.vector.tensor_copy(count_f, count_i))
                step(nc.vector.tensor_copy(token, token_i))
                step(nc.vector.tensor_scalar(by128, count_f, float(P), None, ALU.mult))
                step(nc.vector.tensor_scalar(by2, count_f, 2.0, None, ALU.mult))
                step(nc.vector.tensor_scalar(keys, count_f, -1.0, 64.0, ALU.mult, ALU.add))
                first_hot(group, lg, NGE, 0)
                nc.vector.tensor_tensor(shifted, lg, bcast(top[:, 0].unsqueeze(2), [P, T, NGE]), ALU.subtract
                                        ).then_inc(S["shifted"], 1)
                step(nc.vector.tensor_tensor(pick, le_all, bcast(group.unsqueeze(3), [P, T, NGE, EPG]), ALU.mult))
                step(nc.vector.tensor_reduce(le, pick.rearrange("p t g e -> p t e g"), AX.X, ALU.add))
                first_hot(one[0], le, EPG, 1)
                step(nc.vector.tensor_scalar(le2, one[0], NEG, None, ALU.mult))
                step(nc.vector.tensor_tensor(le2, le2, le, ALU.add))
                first_hot(one[1], le2, EPG, 2)
                nc.vector.tensor_tensor(e2, top[:, 2], top[:, 1], ALU.subtract).then_inc(S["second_ready"], 1)
                dve.wait_ge(S["consts"], 1)
                step(nc.vector.tensor_tensor(group, group, bcast(valid.unsqueeze(2), [P, T, NGE]), ALU.mult))
                for i in range(2):
                    step(nc.vector.tensor_tensor(hot[i].rearrange("p t (g e) -> p t g e", g=NGE),
                                                 bcast(group.unsqueeze(3), [P, T, NGE, EPG]),
                                                 bcast(one[i].unsqueeze(2), [P, T, NGE, EPG]), ALU.mult))
                nc.vector.tensor_tensor(both, hot[0], hot[1], ALU.add).then_inc(S["hots_ready"], 1)
                dve.wait_ge(S["exp_done"], 2)
                step(nc.vector.tensor_reduce(pg, shifted, AX.X, ALU.add))
                step(nc.vector.tensor_scalar(s2, e2, 1.0, None, ALU.add))
                step(nc.vector.tensor_tensor(s2, s2, pg, ALU.mult))
                step(nc.vector.reciprocal(m.row_w[:, 0], s2))
                step(nc.vector.tensor_tensor(m.row_w[:, 1], m.row_w[:, 0], e2, ALU.mult))
                dve.wait_ge(S["ranked"], 1)
                step(nc.vector.tensor_copy(cnt, counts))
                step(nc.vector.tensor_tensor(over, bcast(cnt.unsqueeze(2), [P, NE, 9]),
                                             bcast(by128[:, 0:9].unsqueeze(1), [P, NE, 9]), ALU.is_gt))
                step(nc.vector.tensor_reduce(blocks, over, AX.X, ALU.add))
                step(nc.vector.tensor_tensor(ends_by, upto_mask, bcast(blocks.unsqueeze(1), [P, NE, NE]), ALU.mult))
                step(nc.vector.tensor_reduce(ends, ends_by, AX.X, ALU.add))
                step(nc.vector.tensor_tensor(start, ends, blocks, ALU.subtract))
                step(nc.vector.tensor_scalar(start, start, float(P), -1.0, ALU.mult, ALU.add))
                step(nc.vector.tensor_tensor(row, ranks, bcast(start.unsqueeze(1), [P, T, NE]), ALU.add))
                for i in range(2):
                    step(nc.vector.tensor_tensor(hot[i], hot[i], row, ALU.mult))
                    step(nc.vector.tensor_reduce(dest[:, i], hot[i], AX.X, ALU.add))
                nc.vector.tensor_copy(m.dest_u, dest).then_inc(S["dest_ready"], 1)
                step(nc.vector.tensor_tensor(owner_by, bcast(count_f[:, 0:MAXB].unsqueeze(2), [P, MAXB, NE]),
                                             bcast(ends.unsqueeze(1), [P, MAXB, NE]), ALU.is_ge))
                step(nc.vector.tensor_reduce(owner, owner_by, AX.X, ALU.add))
                step(nc.vector.tensor_scalar(owner, owner, float(NE - 1), None, ALU.min))
                step(nc.vector.tensor_copy(m.block_expert, owner))
                step(nc.vector.tensor_tensor(pairs_by, bcast(ends[:, NE - 1:NE], [P, 25]), by2[:, 0:25], ALU.is_gt))
                step(nc.vector.tensor_reduce(pairs, pairs_by, AX.X, ALU.add))
                step(nc.vector.tensor_copy(m.n_pairs, pairs))
                dve.wait_ge(S["rows_turned"], 1)
                step(nc.vector.tensor_copy(m.row_token, turned))


def stage_experts(nc, m):
    pairs_max = (MAXB - 2) // 2
    with ExitStack() as ctx:
        def sb(name, shape, dt=F32):
            return ctx.enter_context(nc.sbuf_tensor("ex_" + name, shape, dt))[:]

        wg, wu = ([m.ring[:, 3 * p + i, :].rearrange("p (k n) -> p k n", k=KD) for p in range(2)] for i in range(2))
        wd = [m.ring[:, 3 * p + 2, :].rearrange("p (k n) -> p k n", k=4) for p in range(2)]
        x = sb("x", [P, 2, D])
        xT = sb("xT", [P, 2, KD, P])
        gated = sb("gated", [P, 512])
        hid = sb("hid", [P, 512])
        hidT = sb("hidT", [P, 2, 4, P])
        y = sb("y", [P, 2, D])
        column = sb("column", [P, 2], U32)
        x_ps = ctx.enter_context(nc.psum_tensor("ex_x_turned", [P, KD, P], F32))[:]
        g_ps, u_ps = (ctx.enter_context(nc.psum_tensor("ex_ps_" + n, [P, 512], F32))[:] for n in "gu")
        h_ps = ctx.enter_context(nc.psum_tensor("ex_h_turned", [P, 4, P], F32))[:]
        y_ps = ctx.enter_context(nc.psum_tensor("ex_y_ps", [P, 2, 512], F32))[:]
        S = semaphores(nc, m, "ex", "gate_done up_done down_done x_turned xT_ready silu_done hid_ready hid_turned "
                       "hidT_ready y_copied column_ready fetch_next all_stored")
        g_landed, u_landed, d_landed, x_landed, y_stored = (
            [semaphore(nc, m, f"ex_{n}_landed{p}") for p in range(2)] for n in ("g", "u", "d", "x", "y"))

        def pairs(kind):
            return nc.values_load(m.n_pairs[0:1, 0:1], engines=(kind,), min_val=1, max_val=pairs_max)

        with nc.Block() as block:
            @block.sync
            def _(sp):
                n = pairs(CE.SP)
                sp.sem_inc(S["gate_done"], 2)
                sp.sem_inc(S["up_done"], 2)
                sp.sem_inc(S["down_done"], 3)
                with sp.Fori(0, n) as i:
                    for p in range(2):
                        b = i * 2 + p
                        e = nc.values_load(m.block_expert[0:1, bass.ds(b, 1)], engines=(CE.SP,), min_val=0, max_val=NE - 1)
                        for w, src, landed, sem, need in ((wg, m.w_e_gate, g_landed, "gate_done", b + 1),
                                                          (wu, m.w_e_up, u_landed, "up_done", b + 1),
                                                          (wd, m.w_e_down, d_landed, "down_done", b * 2 + 1)):
                            sp.wait_ge(S[sem], need)
                            sp.dma_start(w[p], src[bass.ds(e, 1)].rearrange("a (p k) n -> (a p) k n", p=P)
                                         ).then_inc(landed[p], 16)

            @block.gpsimd
            def _(pool):
                n = pairs(CE.Pool)

                def fetch(p):
                    nc.gpsimd.indirect_dma_start(x[:, p, :], None, m.h2_scr,
                                                 bass.IndirectOffsetOnAxis(column[:, p:p + 1], 0)
                                                 ).then_inc(x_landed[p], 16)

                for p in range(2):
                    nc.gpsimd.tensor_copy(column[:, p:p + 1], m.row_token[:, p:p + 1]).then_inc(S["column_ready"], 1)
                    pool.wait_ge(S["column_ready"], p + 1)
                    fetch(p)
                with pool.Fori(0, n) as i:
                    for p in range(2):
                        b = i * 2 + p
                        pool.wait_ge(S["x_turned"], b * 2 + 2)
                        nc.gpsimd.tensor_copy(column[:, p:p + 1], m.row_token[:, bass.ds(b + 2, 1)]
                                              ).then_inc(S["column_ready"], 1)
                        pool.wait_ge(S["column_ready"], b + 3)
                        pool.sem_inc(S["fetch_next"], 1)
                        fetch(p)
                pool.wait_ge(x_landed[0], n * 16 + 16)
                pool.wait_ge(x_landed[1], n * 16 + 16)

            @block.tensor
            def _(pe):
                n = pairs(CE.PE)

                def turn_x(p):
                    for half in range(2):
                        for c in range(4):
                            k = 4 * half + c
                            mm = nc.tensor.transpose(x_ps[:, k, :], x[:, p, k::KD], m.ident)
                        mm.then_inc(S["x_turned"], 1)

                pe.wait_ge(x_landed[0], 16)
                turn_x(0)
                with pe.Fori(0, n) as i:
                    for p in range(2):
                        b = i * 2 + p
                        pe.wait_ge(g_landed[p], i * 16 + 16)
                        pe.wait_ge(S["xT_ready"], b * 2 + 2)
                        pe.wait_ge(S["silu_done"], b + 1)
                        for k in range(KD):
                            mm = nc.tensor.matmul(g_ps, xT[:, p, k, :], wg[p][:, k, :], start=(k == 0), stop=(k == KD - 1))
                        mm.then_inc(S["gate_done"], 1)
                        pe.wait_ge(u_landed[p], i * 16 + 16)
                        for k in range(KD):
                            mm = nc.tensor.matmul(u_ps, xT[:, p, k, :], wu[p][:, k, :], start=(k == 0), stop=(k == KD - 1))
                        mm.then_inc(S["up_done"], 1)
                        pe.wait_ge(x_landed[1 - p], i * 16 + 16 * (1 + p))
                        turn_x(1 - p)
                        pe.wait_ge(S["hid_ready"], b + 1)
                        for k in range(4):
                            mm = nc.tensor.transpose(h_ps[:, k, :], hid[:, k::4], m.ident)
                        mm.then_inc(S["hid_turned"], 1)
                        pe.wait_ge(S["hidT_ready"], b + 1)
                        pe.wait_ge(d_landed[p], i * 16 + 16)
                        pe.wait_ge(S["y_copied"], b * 2 + 1)
                        for half in range(2):
                            for k in range(4):
                                mm = nc.tensor.matmul(y_ps[:, half, :], hidT[:, p, k, :],
                                                      wd[p][:, k, 512 * half:512 * (half + 1)],
                                                      start=(k == 0), stop=(k == 3))
                            mm.then_inc(S["down_done"], 1)

            @block.vector
            def _(dve):
                n = pairs(CE.DVE)

                def copy_x(p, first):
                    for half in range(2):
                        k = slice(4 * half, 4 * half + 4)
                        dve.wait_ge(S["x_turned"], first + half)
                        nc.vector.tensor_tensor(xT[:, p, k, :], x_ps[:, k, :], bcast(m.ln2[:, k].unsqueeze(2), [P, 4, P]),
                                                ALU.mult).then_inc(S["xT_ready"], 1)

                copy_x(0, 1)
                with dve.Fori(0, n) as i:
                    for p in range(2):
                        b = i * 2 + p
                        dve.wait_ge(S["up_done"], b + 3)
                        dve.wait_ge(S["silu_done"], b + 2)
                        nc.vector.tensor_tensor(hid, u_ps, gated, ALU.mult).then_inc(S["hid_ready"], 1)
                        copy_x(1 - p, b * 2 + 3)
                        dve.wait_ge(S["hid_turned"], b + 1)
                        nc.vector.tensor_copy(hidT[:, p], h_ps).then_inc(S["hidT_ready"], 1)

            @block.scalar
            def _(act):
                n = pairs(CE.Activation)
                act.sem_inc(S["silu_done"], 1)
                act.sem_inc(S["y_copied"], 1)
                act.sem_inc(y_stored[0], 1)
                act.sem_inc(y_stored[1], 1)
                with act.Fori(0, n) as i:
                    for p in range(2):
                        b = i * 2 + p
                        act.wait_ge(S["gate_done"], b + 3)
                        nc.scalar.activation(gated, g_ps, ACT.Silu).then_inc(S["silu_done"], 1)
                        act.wait_ge(y_stored[p], i * 16 + 1)
                        for half in range(2):
                            act.wait_ge(S["down_done"], b * 2 + half + 4)
                            nc.scalar.activation(y[:, p, 512 * half:512 * (half + 1)], y_ps[:, half, :], ACT.Copy
                                                 ).then_inc(S["y_copied"], 1)
                        act.wait_ge(S["y_copied"], b * 2 + 3)
                        act.dma_start(m.y_scr[bass.ds(b * P, P), :], y[:, p, :]).then_inc(y_stored[p], 16)
                act.wait_ge(y_stored[0], n * 16 + 1)
                act.wait_ge(y_stored[1], n * 16 + 1)
                act.sem_inc(S["all_stored"], 1)


def stage_combine(nc, m):
    with ExitStack() as ctx:
        y = ctx.enter_context(nc.sbuf_tensor("cb_y", [P, 2, 2, D], F32))[:]
        out = ctx.enter_context(nc.sbuf_tensor("cb_out", [P, 2, D], F32))[:]
        first_added, both_added = (semaphore(nc, m, "cb_" + n) for n in ("first_added", "both_added"))
        y_landed, stored = ([semaphore(nc, m, f"cb_{n}{p}") for p in range(2)] for n in ("y_landed", "stored"))
        with nc.Block() as block:
            @block.gpsimd
            def _(pool):
                for t, r in TILES:
                    if t >= 2:
                        pool.wait_ge(both_added, t - 1)
                    for i in range(2):
                        nc.gpsimd.indirect_dma_start(y[0:r, t % 2, i, :], None, m.y_scr,
                                                     bass.IndirectOffsetOnAxis(m.dest_u[0:r, i, t:t + 1], 0)
                                                     ).then_inc(y_landed[t % 2], 16)

            @block.vector
            def _(dve):
                for t, r in TILES:
                    dve.wait_ge(y_landed[t % 2], 32 * (t // 2 + 1))
                    if t >= 2:
                        dve.wait_ge(stored[t % 2], 16 * (t // 2))
                    o = out[0:r, t % 2]
                    nc.vector.scalar_tensor_tensor(o, y[0:r, t % 2, 0], m.row_w[0:r, 0, t:t + 1], m.x1[t][0:r],
                                                   ALU.mult, ALU.add).then_inc(first_added, 1)
                    dve.wait_ge(first_added, t + 1)
                    nc.vector.scalar_tensor_tensor(o, y[0:r, t % 2, 1], m.row_w[0:r, 1, t:t + 1], o,
                                                   ALU.mult, ALU.add).then_inc(both_added, 1)

            @block.sync
            def _(sp):
                for t, r in TILES:
                    sp.wait_ge(both_added, t + 1)
                    dst = m.y_prompt[t * P:(t + 1) * P, :] if t < NT else m.y_sample
                    sp.dma_start(dst, out[0:r, t % 2]).then_inc(stored[t % 2], 16)
                sp.wait_ge(stored[0], 16 * 5)
                sp.wait_ge(stored[1], 16 * 4)


_SHAPES = dict(
    x_prompt=(1, 1024, 1024), x_sample=(8, 1, 1024),
    cache_swa0_kv=(1, 8, 128, 2, 8, 64), cache_swa1_kv=(1, 8, 512, 2, 8, 64), cache_swa2_kv=(1, 8, 2048, 2, 8, 64),
    state_dn_conv=(1, 8, 3, 3072), state_dn_S=(1, 8, 8, 128, 128), ln1_g=(1, 1024), w_in=(1, 1024, 10768),
    q_norm_g=(1, 3, 64), k_norm_g=(1, 3, 64), dn_conv_w=(1, 4, 3072), dn_a_log=(1, 8), dn_dt_bias=(1, 8),
    dn_norm_g=(1, 128), w_out_a=(1, 512, 1024), w_out_b=(1, 1024, 1024), w_o=(1, 1024, 1024), ln2_g=(1, 1024),
    w_rg=(1, 1024, 4), b_rg=(1, 4), w_re=(1, 1024, 32), b_re=(1, 32), w_e_gate=(1, 32, 1024, 512),
    w_e_up=(1, 32, 1024, 512), w_e_down=(1, 32, 512, 1024))
_OUTS = [("y_prompt", (1, 1024, 1024)), ("y_sample", (8, 1, 1024)), ("p_swa0", (1, 1, 128, 2, 8, 64)),
         ("p_swa1", (1, 1, 512, 2, 8, 64)), ("p_swa2", (1, 1, 1024, 2, 8, 64)), ("p_conv", (1, 1, 3, 3072)),
         ("p_S", (1, 1, 8, 128, 128)), ("s_swa0", (1, 8, 1, 2, 8, 64)), ("s_swa1", (1, 8, 1, 2, 8, 64)),
         ("s_swa2", (1, 8, 1, 2, 8, 64)), ("s_conv", (1, 8, 3, 3072)), ("s_S", (1, 8, 8, 128, 128))]


def build(nc, a, out, upto=None, debug=None):
    m = Shared()
    m.plan = weight_plan()
    m.last_use = {}
    m.taken = []
    m.n_outputs = 0
    m.x_prompt = a["x_prompt"].rearrange("a t d -> (a t) d")
    m.x_sample = a["x_sample"].rearrange("b t d -> (b t) d")
    m.w_in_v = a["w_in"].rearrange("a (p k) n -> (a p) k n", k=KD)
    m.w_out_a = a["w_out_a"].rearrange("a k n -> (a k) n")
    m.w_out_b = a["w_out_b"].rearrange("a k n -> (a k) n")
    m.w_o = a["w_o"].rearrange("a k n -> (a k) n")
    m.p_swa = [out[f"p_swa{g}"].rearrange("a b t k h e -> (a b t) (k h e)") for g in range(NG)]
    m.s_swa = [out[f"s_swa{g}"].rearrange("a b t k h e -> (a b t) k (h e)") for g in range(NG)]
    m.o_s_scr = nc.dram_tensor("o_s_scratch", [NB, NG, OROW], F32, kind="Internal").ap()
    m.conv_w_rows = a["dn_conv_w"].rearrange("a i c -> (a i) c")
    m.conv_state_rows = a["state_dn_conv"].rearrange("a b i c -> (a b i) c")
    m.s_conv = out["s_conv"].rearrange("a b i c -> (a b) i c")
    m.p_conv = out["p_conv"].rearrange("a b i c -> (a b i) c")
    m.p_S = out["p_S"].rearrange("a b h k v -> (a b h) k v")
    m.s_S = out["s_S"].rearrange("a b h k v -> (a b) h k v")
    m.state_S = a["state_dn_S"].rearrange("a b h k v -> (a b) h k v")
    m.caches = [a[f"cache_swa{g}_kv"].rearrange("a b t k h e -> t (a b) (k h e)") for g in range(NG)]
    m.o_scr = nc.dram_tensor("o_scratch", [SEQ, NG, OROW], F32, kind="Internal").ap()
    m.row_scr = nc.dram_tensor("row_scratch", [MAXB * P, 1], F32, kind="Internal").ap()
    m.y_scr = nc.dram_tensor("y_scratch", [(MAXB - 2) * P, D], F32, kind="Internal").ap()
    m.y_prompt = out["y_prompt"].rearrange("a t d -> (a t) d")
    m.y_sample = out["y_sample"].rearrange("b t d -> (b t) d")
    m.w_e_gate, m.w_e_up, m.w_e_down = (a[n].rearrange("a e k n -> (a e) k n") for n in
                                        ("w_e_gate", "w_e_up", "w_e_down"))
    m.h2_scr = nc.dram_tensor("h_scratch", [TOK, D], F32, kind="Internal").ap()

    ctx = ExitStack()
    with ctx:
        def sb(name, shape, dt=F32):
            return ctx.enter_context(nc.sbuf_tensor(name, shape, dt))[:]

        m.hT = sb("hT", [P, KD, TOK])
        m.ring = sb("ring", [P, RING, SLOT])
        m.ident, m.ones, m.triu = (sb(x, [P, P]) for x in ("ident", "ones", "triu"))
        m.oBT = sb("oBT", [P, DNH, TOK])
        early = m.oBT.rearrange("p h t -> p (h t)")[0:NB]
        m.q_s = early[:, 0:NG * HW].rearrange("p (g c) -> p g c", g=NG)
        m.kv_s = early[:, NG * HW:3 * NG * HW].rearrange("p (g w c) -> p g w c", g=NG, w=2)
        m.pick_row = early[:, 3 * NG * HW:3 * NG * HW + NB * P].rearrange("p (b c) -> p b c", b=NB)
        m.w_ba = sb("w_ba", [P, KD, 16])
        m.dt_bias, m.neg_a = (sb(x, [P, DNH]) for x in ("dt_bias", "neg_a"))
        m.beta_all, m.g_all = (sb(x, [P, NT + 1, DNH]) for x in ("beta_all", "g_all"))
        m.conv_w = sb("conv_w", [P, 24, 4])
        m.conv_state = sb("conv_state", [P, 24, NB, 3])
        m.tails = sb("tails", [P, 24, 11])
        m.dn_s = sb("dn_s", [P, 4, DNH, NB])
        m.dn_gain = sb("dn_gain", [P, 1])
        m.ident_b = sb("ident_b", [P, P], BF16)
        m.scratch_mask = m.hT[:, 0, 0:2 * P]
        m.odd = m.hT[:, 1, 0:P].bitcast(I32)
        m.odd_f = m.hT[:, 2, 0:P]
        m.mask_band = sb("mask_band", [P, 2 * P], BF16)
        m.mask_pair, m.mask_decay = (sb(x, [P, P], BF16) for x in ("mask_pair", "mask_decay"))
        m.iota_ready, m.parity_ready = (nc.alloc_semaphore(x) for x in ("iota_ready", "parity_ready"))
        m.minus_half = sb("minus_half", [P, 128])
        m.ln1 = sb("ln1", [P, KD])
        m.ln2 = sb("ln2", [P, KD])
        m.w_router = sb("w_router", [P, KD, 36])
        m.b_router = sb("b_router", [P, 36])
        m.logits = m.conv_state.rearrange("p c b i -> p (c b i)")[:, 0:36 * (NT + 1)].rearrange("p (t n) -> p t n", n=36)
        at = m.conv_state.rearrange("p c b i -> p (c b i)")[:, 36 * (NT + 1):]
        m.row_w = at[:, 0:18].rearrange("p (i t) -> p i t", i=2)
        m.dest_u = at[:, 18:36].bitcast(U32).rearrange("p (i t) -> p i t", i=2)
        m.n_pairs = at[:, 36:37].bitcast(I32)
        m.block_expert = at[:, 40:40 + MAXB].bitcast(I32)
        m.row_token = at[:, 100:100 + MAXB].bitcast(U32)
        x1 = m.oBT.rearrange("p h t -> p (h t)")
        m.x1 = [x1[:, t * D:(t + 1) * D] for t in range(NT)] + [m.hT[0:NB, 0, 0:D]]
        m.qk_gain = sb("qk_gain", [P, 2, NG, E])
        m.pick_col = sb("pick_col", [P, NB, NB])
        m.w_landed = [nc.alloc_semaphore(f"w_landed{i}") for i in range(RING)]
        m.small_landed = nc.alloc_semaphore("small_landed")
        m.outputs_stored = nc.alloc_semaphore("outputs_stored")
        m.pool_step = nc.alloc_semaphore("pool_step")
        m.small_loads = [
            (m.w_router[:, :, 0:4], a["w_rg"].rearrange("a (p k) n -> (a p) k n", k=KD)),
            (m.w_router[:, :, 4:36], a["w_re"].rearrange("a (p k) n -> (a p) k n", k=KD)),
            (m.b_router[:, 0:4], a["b_rg"].to_broadcast([P, 4])),
            (m.b_router[:, 4:36], a["b_re"].to_broadcast([P, 32])),
            (m.w_ba, m.w_in_v[:, :, COL_BETA:COL_BETA + 16]),
            (m.dt_bias, a["dn_dt_bias"].to_broadcast([P, DNH])),
            (m.neg_a, a["dn_a_log"].to_broadcast([P, DNH])),
            (m.dn_gain, a["dn_norm_g"].rearrange("a (p c) -> (a p) c", c=1)),
            (m.ln1, a["ln1_g"].rearrange("a (p k) -> (a p) k", k=KD)),
            (m.ln2, a["ln2_g"].rearrange("a (p k) -> (a p) k", k=KD)),
            (m.qk_gain[:, 0], a["q_norm_g"].rearrange("a g e -> a (g e)").to_broadcast([P, NG * E]).rearrange("p (g e) -> p g e", g=NG)),
            (m.qk_gain[:, 1], a["k_norm_g"].rearrange("a g e -> a (g e)").to_broadcast([P, NG * E]).rearrange("p (g e) -> p g e", g=NG)),
        ]
        stages = [stage_constants, stage_norm1, stage_attention, stage_decode_attention, stage_conv_state,
                  stage_deltanet, stage_decode_deltanet, stage_mix, stage_residual,
                  stage_route, stage_experts, stage_combine]
        for stage in stages[:upto]:
            stage(nc, m)
            if m.taken:
                nc.clear_and_free_semaphores(m.taken)
                nc.all_engine_barrier()
            m.taken = []
            m.last_use = {}
        if debug:
            debug(nc, m)
        with nc.Block() as block:
            @block.sync
            def _(sp):
                sp.wait_ge(m.outputs_stored, 16 * m.n_outputs)


def kernel(**inputs):
    import numpy as np
    import concourse.bacc as bacc
    from concourse.bass_utils import run_bass_kernel_spmd

    nc = bacc.Bacc("TRN2", target_bir_lowering=False, num_devices=1)
    arrays = {"in_" + n: np.ascontiguousarray(inputs[n]) for n in _SHAPES}
    a = {n: nc.dram_tensor("in_" + n, shape, F32, kind="ExternalInput").ap() for n, shape in _SHAPES.items()}
    out = {n: nc.dram_tensor("out_" + n, shape, F32, kind="ExternalOutput").ap() for n, shape in _OUTS}
    build(nc, a, out)
    r = run_bass_kernel_spmd(nc, [arrays], core_ids=[0])
    return tuple(r.results[0]["out_" + n] for n, _ in _OUTS)
```

```python
from contextlib import ExitStack

import concourse.bass as bass
from concourse import mybir

F32 = mybir.dt.float32
BF16 = mybir.dt.bfloat16
I32 = mybir.dt.int32
U32 = mybir.dt.uint32
ALU = mybir.AluOpType
ACT = mybir.ActivationFunctionType
AX = mybir.AxisListType

P = 128
D = 1024
KD = D // P
SEQ = 1024
NB = 8
TOK = SEQ + NB
NT = SEQ // P
EPS = 1e-6
NG, NH, E = 3, 8, 64
HW = NH * E
SWA = ((128, 1), (512, 4), (2048, 16))
DNH, DK = 8, 128
COL_Q, COL_K, COL_V = 0, 1536, 3072
COL_DN = 4608
COL_BETA = COL_DN + 3072
COL_Z = COL_BETA + 16
COL_GA = COL_Z + 1024
COL_GB = COL_GA + 1024
OROW = HW + 2 * NH
NEG = -1.0e30
NE, NGE, EPG = 32, 4, 8
MAXB = 50
RING = 6
SLOT = KD * 512


class Shared:
    pass


class Chain:

    def __init__(self, eng, sem):
        self.eng, self.sem, self.n = eng, sem, 0

    def __call__(self, ins):
        self.n += 1
        ins.then_inc(self.sem, 1)
        self.eng.wait_ge(self.sem, self.n)


def bcast(ap, shape):
    return ap.to_broadcast(shape)


def perm_tokens(hT, g, t, k):
    if g == 0:
        return hT[:, k, t * P:(t + 1) * P]
    if g == 1:
        s = 512 * (t % 2) + t // 2
        return hT[:, k, s:s + 4 * (P - 1) + 1:4]
    return hT[:, k, t:t + 8 * (P - 1) + 1:8]


def perm_rows(dram, g, t):
    if g == 0:
        return dram[t * P:(t + 1) * P, :]
    if g == 1:
        s = 512 * (t % 2) + t // 2
        return dram[s:s + 4 * (P - 1) + 1:4, :]
    return dram[t:t + 8 * (P - 1) + 1:8, :]


def weight_plan():
    plan = []
    for g in range(NG):
        plan += [("q", g), ("k", g), ("v", g)]
    plan += [("dn", h) for h in range(DNH)]
    for kind in ("ga", "gb", "wb", "wo"):
        plan += [(kind, 0), (kind, 1)]
    return plan


SLOTS = [0, 1, 2, 3, 4, 5, 0, 1, 2] + [3, 4] * 4 + [2, 5, 0, 1, 3, 4, 2, 0]

SLOTS_S = (3, 4)


def dmas_of(plan, n):
    return 4 if plan[n][0] == "dn" else 1


def load_chunk(sp, m, n):
    kind, i = m.plan[n]
    slot = m.ring[:, SLOTS[n], :]
    before = [j for j in range(n) if SLOTS[j] == SLOTS[n]]
    if before and before[-1] in m.last_use:
        sp.wait_ge(*m.last_use[before[-1]])
    if kind in "qkv":
        c = {"q": COL_Q, "k": COL_K, "v": COL_V}[kind] + i * HW
        parts = [(slot.rearrange("p (k n) -> p k n", k=KD), m.w_in_v[:, :, c:c + HW])]
    elif kind == "dn":
        v = slot.rearrange("p (k w n) -> p k w n", k=KD, w=4)
        parts = [(v[:, :, w, :], m.w_in_v[:, :, c:c + DK]) for w, c in
                 enumerate((COL_DN + i * DK, COL_DN + 1024 + i * DK, COL_DN + 2048 + i * DK, COL_Z + i * DK))]
    elif kind in ("ga", "gb"):
        c = (COL_GA if kind == "ga" else COL_GB) + i * 512
        parts = [(slot.rearrange("p (k n) -> p k n", k=KD), m.w_in_v[:, :, c:c + 512])]
    elif kind == "wb":
        parts = [(slot.rearrange("p (k n) -> p k n", k=KD),
                  m.w_out_b.rearrange("(k p) n -> p k n", p=P)[:, :, i * 512:(i + 1) * 512])]
    else:
        parts = [(slot.rearrange("p (k n) -> p k n", k=KD),
                  m.w_o.rearrange("(k p) n -> p k n", p=P)[:, :, i * 512:(i + 1) * 512])]
    for dst, src in parts:
        sp.dma_start(dst, src).then_inc(m.w_landed[SLOTS[n]], 16)


def chunk(pe, m, kind, i):
    n = m.plan.index((kind, i))
    pe.wait_ge(m.w_landed[SLOTS[n]], 16 * sum(dmas_of(m.plan, j) for j in range(n + 1) if SLOTS[j] == SLOTS[n]))
    return m.ring[:, SLOTS[n], :]


def stage_constants(nc, m):
    with nc.Block() as block:
        @block.sync
        def _(sp):
            for dst, src in m.small_loads:
                sp.dma_start(dst, src).then_inc(m.small_landed, 16)
            sp.wait_ge(m.small_landed, 16 * len(m.small_loads))

        @block.gpsimd
        def _(pool):
            step = Chain(pool, m.pool_step)
            nc.gpsimd.iota(m.odd, pattern=[[1, P]], base=0, channel_multiplier=1).then_inc(m.iota_ready, 1)
            for ap, value in ((m.ident, 0.0), (m.ones, 1.0), (m.minus_half, -0.5)):
                step(nc.gpsimd.memset(ap, value))
            step(nc.gpsimd.affine_select(out=m.ident, in_=m.ident, compare_op=ALU.not_equal, fill=1.0, base=0,
                                         pattern=[[-1, P]], channel_multiplier=1))
            step(nc.gpsimd.tensor_copy(m.ident_b, m.ident))

        @block.vector
        def _(dve):
            dve.wait_ge(m.iota_ready, 1)
            step = Chain(dve, m.parity_ready)
            step(nc.vector.tensor_single_scalar(m.odd, m.odd, 1, ALU.bitwise_and))
            step(nc.vector.tensor_copy(m.odd_f, m.odd))
            step(nc.vector.tensor_scalar(m.odd_f, m.odd_f, NEG, None, ALU.mult))


def semaphore(nc, m, name):
    m.taken.append(nc.alloc_semaphore(name))
    return m.taken[-1]


def semaphores(nc, m, stage, names):
    return {x: semaphore(nc, m, f"{stage}_{x}") for x in names.split()}


def build_masks(nc, m, pool):
    step = Chain(pool, m.mask_step)
    step(nc.gpsimd.memset(m.scratch_mask, 0.0))
    yield
    step(nc.gpsimd.tensor_scalar(m.qk_gain[:, 0], m.qk_gain[:, 0], float(E) ** -0.5, None, ALU.mult))
    yield
    step(nc.gpsimd.affine_select(out=m.triu, in_=m.ones, compare_op=ALU.is_ge, fill=0.0, base=0,
                                 pattern=[[1, P]], channel_multiplier=-1))
    yield
    step(nc.gpsimd.memset(m.pick_col, 0.0))
    yield
    step(nc.gpsimd.affine_select(out=m.pick_col, in_=m.pick_col, compare_op=ALU.not_equal, fill=1.0, base=0,
                                 pattern=[[-1, NB], [1, NB]], channel_multiplier=0))
    yield
    step(nc.gpsimd.affine_select(out=m.scratch_mask[:, 0:P], in_=m.scratch_mask[:, 0:P],
                                 compare_op=ALU.is_ge, fill=NEG, base=0,
                                 pattern=[[1, P]], channel_multiplier=-1))
    yield
    step(nc.gpsimd.affine_select(out=m.scratch_mask[:, P:2 * P], in_=m.scratch_mask[:, P:2 * P],
                                 compare_op=ALU.is_ge, fill=NEG, base=0,
                                 pattern=[[-1, P]], channel_multiplier=1))
    yield
    step(nc.gpsimd.tensor_copy(m.mask_band, m.scratch_mask))
    yield
    step(nc.gpsimd.tensor_tensor(m.mask_pair, m.scratch_mask[:, P:2 * P], m.odd_f, ALU.add))
    yield
    step(nc.gpsimd.memset(m.scratch_mask, 0.0))
    yield
    step(nc.gpsimd.affine_select(out=m.scratch_mask[:, 0:P], in_=m.scratch_mask[:, 0:P],
                                 compare_op=ALU.is_ge, fill=NEG, base=0,
                                 pattern=[[1, P]], channel_multiplier=-1))
    yield
    step(nc.gpsimd.tensor_copy(m.mask_decay, m.scratch_mask[:, 0:P]))


def stage_norm1(nc, m):
    tiles = [(t, P) for t in range(NT)] + [(NT, NB)]
    XB = 4
    with ExitStack() as ctx:
        xs = ctx.enter_context(nc.sbuf_tensor("n1_x", [P, XB, D], F32))
        hs = ctx.enter_context(nc.sbuf_tensor("n1_h", [P, 2, D], F32))
        junk = ctx.enter_context(nc.sbuf_tensor("n1_junk", [P, D], F32))
        ssq = ctx.enter_context(nc.sbuf_tensor("n1_ssq", [P, 2, 3], F32))
        hps = ctx.enter_context(nc.psum_tensor("n1_hps", [P, 2, KD, P], F32))
        x_landed = [semaphore(nc, m, f"n1_x_landed{i}") for i in range(XB)]
        squares_summed, rstd_ready, normed, turned, written, rstd_step = (
            semaphore(nc, m, f"n1_{x}") for x in
            ("squares_summed", "rstd_ready", "normed", "turned", "written", "rstd_step"))
        with nc.Block() as block:
            @block.sync
            def _(sp):
                for t, n in tiles:
                    if t >= XB:
                        sp.wait_ge(normed, t - XB + 1)
                    src = m.x_prompt[t * P:(t + 1) * P, :] if t < NT else m.x_sample
                    sp.dma_start(xs[0:n, t % XB, :], src).then_inc(x_landed[t % XB], 16)
                for n in range(RING):
                    load_chunk(sp, m, n)

            @block.scalar
            def _(act):
                for t, n in tiles:
                    act.wait_ge(x_landed[t % XB], 16 * (t // XB + 1))
                    if t >= 2:
                        act.wait_ge(rstd_ready, t - 1)
                    if t >= 1:
                        act.wait_ge(squares_summed, t)
                    nc.scalar.activation(junk[0:n, :], xs[0:n, t % XB, :], ACT.Square,
                                         accum_out=ssq[0:n, t % 2, 0:1]).then_inc(squares_summed, 1)

            @block.gpsimd
            def _(pool):
                masks = build_masks(nc, m, pool)
                for t, n in tiles:
                    s = ssq[0:n, t % 2, :]
                    pool.wait_ge(squares_summed, t + 1)
                    if t >= 2:
                        pool.wait_ge(normed, t - 1)
                    nc.gpsimd.tensor_scalar(s[:, 1:2], s[:, 0:1], 1.0 / D, EPS, ALU.mult, ALU.add).then_inc(rstd_step, 1)
                    pool.wait_ge(rstd_step, t + 1)
                    nc.gpsimd.tensor_tensor(s[:, 2:3], s[:, 1:2], m.minus_half[0:n, 0:1], ALU.pow).then_inc(rstd_ready, 1)
                    next(masks, None)
                    next(masks, None)
                for _ in masks:
                    pass

            @block.vector
            def _(dve):
                for t, n in tiles + [(NT + 1, 0)]:
                    if t <= NT:
                        dve.wait_ge(rstd_ready, t + 1)
                        if t >= 2:
                            dve.wait_ge(turned, t - 1)
                        nc.vector.tensor_scalar(hs[0:n, t % 2, :], xs[0:n, t % XB, :], ssq[0:n, t % 2, 2:3], None,
                                                ALU.mult).then_inc(normed, 1)
                    if t >= 1:
                        u, w = tiles[t - 1]
                        dve.wait_ge(turned, u + 1)
                        nc.vector.tensor_tensor(m.hT[:, :, u * P:u * P + w], hps[:, u % 2, :, 0:w],
                                                bcast(m.ln1.unsqueeze(2), [P, KD, w]), ALU.mult).then_inc(written, 1)

            @block.tensor
            def _(pe):
                for t, n in tiles:
                    pe.wait_ge(normed, t + 1)
                    if t >= 2:
                        pe.wait_ge(written, t - 1)
                    for k in range(KD):
                        last = nc.tensor.transpose(hps[:, t % 2, k, 0:n], hs[0:n, t % 2, k::KD], m.ident[0:n, 0:n])
                    last.then_inc(turned, 1)


def stage_attention(nc, m):
    jobs = [(g, t) for g in range(NG) for t in range(NT + 1)]
    prompt = [j for j in jobs if j[1] < NT]
    number = {j: n for n, j in enumerate(prompt)}

    def rows(t):
        return P if t < NT else NB

    def has_prev(g, t):
        return (g == 0 and t > 0) or (g == 1 and t % 2 == 1)

    with ExitStack() as ctx:
        def sb(name, shape, dt=F32):
            return ctx.enter_context(nc.sbuf_tensor("at_" + name, shape, dt))[:]

        qn = sb("qn", [P, HW])
        sq = sb("sq", [P, 2, HW])
        stat = sb("stat", [P, 2, 3, NH])
        kv = sb("kv", [P, 3, 2, HW])
        kT = sb("kT", [P, 2, 4, P])
        late = m.oBT.rearrange("p h t -> p (h t)")[:, 3 * NG * HW:]
        prob, pT = (late[:, 1024 * i:1024 * (i + 1)].rearrange("p (a h k) -> p a h k", a=2, h=2) for i in range(2))
        qT = late[:, 2048:2560].rearrange("p (h k) -> p h k", h=4)
        orow = sb("orow", [P, 2, OROW])
        pq, pk, po, tps = (ctx.enter_context(nc.psum_tensor(f"at_p{i}", [P, 512], F32))[:] for i in range(4))
        pv = pq
        sbanks = ctx.enter_context(nc.psum_tensor("at_scores", [P, 2, 2, 512], F32))[:]
        sps = sbanks[:, :, :, 0:2 * P]
        tk = sbanks[:, 1, 0, :]
        S = semaphores(nc, m, "at", "q_projected k_projected v_projected q_squared k_squared q_summed k_summed "
                       "q_rstd k_rstd q_scaled k_scaled q_normed k_normed v_copied q_turned k_turned qT_ready "
                       "kT_ready scores_ready max_ready probs_ready probs_turned pT_ready heads_done o_ready "
                       "q_mean k_mean")
        kv_out = [semaphore(nc, m, f"at_kv_out{i}") for i in range(3)]
        o_out = [semaphore(nc, m, f"at_o_out{i}") for i in range(2)]
        for g in range(NG):
            for i, x in enumerate(("q_projected", "k_projected", "v_projected")):
                m.last_use[3 * g + i] = (S[x], (g + 1) * (NT + 1))
        steps = [(jobs[n] if n >= 0 and jobs[n][1] < NT else None, jobs[n + 1] if n + 1 < len(jobs) else None)
                 for n in range(-1, len(jobs))]
        kv_stores = [0, 0, 0]
        stored_before = []
        for n, (g, t) in enumerate(jobs):
            stored_before.append(kv_stores[n % 3])
            if t < NT and (g == 2 or (g == 1 and t % 2 == 1) or (g == 0 and t == NT - 1)):
                kv_stores[n % 3] += 1

        def kv_free(eng, n):
            if stored_before[n]:
                eng.wait_ge(kv_out[n % 3], 16 * stored_before[n])

        def kv_rows(n, which):
            g, t = jobs[n]
            return kv[:, n % 3, which, :] if t < NT else m.kv_s[:, g, which, :]

        with nc.Block() as block:
            @block.sync
            def _(sp):
                o_stores = [0, 0]
                for n, (g, t) in enumerate(jobs):
                    if t == NT:
                        sp.wait_ge(S["k_normed"], n + 1)
                        sp.wait_ge(S["v_copied"], n + 1)
                        sp.dma_start(m.s_swa[g], m.kv_s[:, g, :, :]).then_inc(m.outputs_stored, 16)
                        m.n_outputs += 1
                        for j in {0: (6, 7, 8), 1: (9, 10), 2: ()}[g]:
                            load_chunk(sp, m, j)
                    elif g == 2 or (g == 1 and t % 2 == 1) or (g == 0 and t == NT - 1):
                        sp.wait_ge(S["k_normed"], n + 1)
                        sp.wait_ge(S["v_copied"], n + 1)
                        if g == 0:
                            dst = m.p_swa[0]
                        elif g == 1:
                            dst = m.p_swa[1][t // 2:t // 2 + 4 * (P - 1) + 1:4, :]
                        else:
                            dst = perm_rows(m.p_swa[2], 2, t)
                        sp.dma_start(dst, kv[:, n % 3, :, :].rearrange("p a b -> p (a b)")).then_inc(kv_out[n % 3], 16)
                    if n >= 1 and jobs[n - 1] in number:
                        a = number[jobs[n - 1]]
                        sp.wait_ge(S["o_ready"], a + 1)
                        sp.dma_start(perm_rows(m.o_scr[:, jobs[n - 1][0], :], *jobs[n - 1]), orow[:, a % 2, :]
                                     ).then_inc(o_out[a % 2], 16)
                for i in range(3):
                    sp.wait_ge(kv_out[i], 16 * kv_stores[i])
                for i in range(2):
                    sp.wait_ge(o_out[i], 16 * (len(prompt) // 2))

            @block.tensor
            def _(pe):
                def projections(n):
                    g, t = jobs[n]
                    if n >= 1:
                        pe.wait_ge(S["v_copied"], n)
                    for w, (name, bank) in enumerate((("q", pq), ("k", pk), ("v", pv))):
                        if n >= 1 and name == "k":
                            pe.wait_ge(S["k_scaled"], n)
                        if name == "v":
                            pe.wait_ge(S["q_scaled"], n + 1)
                        weights = chunk(pe, m, name, g).rearrange("p (k n) -> p k n", k=KD)
                        for k in range(KD):
                            tok = perm_tokens(m.hT, g, t, k) if t < NT else m.hT[:, k, SEQ:TOK]
                            mm = nc.tensor.matmul(bank[0:rows(t), :], tok, weights[:, k, :],
                                                  start=(k == 0), stop=(k == KD - 1))
                            if k == KD - 1:
                                mm.then_inc(S[name + "_projected"], 1)
                            yield

                def fill(source, n):
                    for _ in range(n):
                        if next(source, 0) == 0:
                            return

                def scores(a, hp):
                    g, t = prompt[a]
                    first = P * (not has_prev(g, t))
                    if 4 * a + hp >= 2:
                        pe.wait_ge(S["probs_ready"], 2 * (4 * a + hp - 1))
                    mask = m.mask_pair if g == 2 else m.mask_band[:, first:2 * P]
                    for h in range(2):
                        nc.tensor.matmul(sps[:, hp % 2, h, first:2 * P], m.ident_b, mask,
                                         start=True, stop=False, skip_group_check=True)
                    for blk in range(first // P, 2):
                        for h in range(2):
                            own = slice(64 * h, 64 * h + 64)
                            mm = nc.tensor.matmul(sps[:, hp % 2, h, blk * P:(blk + 1) * P], qT[own, hp, :],
                                                  kT[own, (a + 1 + blk) % 2, hp, :],
                                                  start=False, stop=True, skip_group_check=True)
                    mm.then_inc(S["scores_ready"], 1)

                def turn_probs(a, hp):
                    g, t = prompt[a]
                    pe.wait_ge(S["probs_ready"], 2 * (4 * a + hp + 1))
                    if hp >= 1:
                        pe.wait_ge(S["pT_ready"], 4 * a + hp)
                    for h in range(2):
                        for blk in range(not has_prev(g, t), 2):
                            c = h * 2 * P + blk * P
                            mm = nc.tensor.transpose(tps[:, c:c + P], prob[:, hp % 2, h, blk * P:(blk + 1) * P],
                                                     m.ident)
                    mm.then_inc(S["probs_turned"], 1)

                def weigh_values(a, hp):
                    g, t = prompt[a]
                    n = jobs.index(prompt[a])
                    pe.wait_ge(S["pT_ready"], 4 * a + hp + 1)
                    if a >= 1 and hp == 0:
                        pe.wait_ge(S["o_ready"], a)
                    for h in range(2):
                        c = (2 * hp + h) * E
                        blks = range(not has_prev(g, t), 2)
                        for blk in blks:
                            mm = nc.tensor.matmul(po[:, c:c + E], pT[:, hp % 2, h, blk * P:(blk + 1) * P],
                                                  kv[:, (n - 1 + blk) % 3, 1, c:c + E],
                                                  start=(blk == blks[0]), stop=(blk == 1))
                    mm.then_inc(S["heads_done"], 1)

                def turn_qk(n):
                    a = number[jobs[n]]
                    for which, src, bank in (("q", qn, tps), ("k", kv[:, n % 3, 0, :], tk)):
                        pe.wait_ge(S[which + "_normed"], n + 1)
                        if a >= 1 and which == "q":
                            pe.wait_ge(S["pT_ready"], 4 * a)
                        elif a >= 1:
                            pe.wait_ge(S["probs_ready"], 8 * a)
                        for hp in range(4):
                            mm = nc.tensor.transpose(bank[:, hp * P:(hp + 1) * P], src[:, hp * P:(hp + 1) * P], m.ident)
                        mm.then_inc(S[which + "_turned"], 1)

                for att, nxt in steps:
                    source = projections(jobs.index(nxt)) if nxt else iter(())
                    if att:
                        a = number[att]
                        pe.wait_ge(S["qT_ready"], a + 1)
                        pe.wait_ge(S["kT_ready"], a + 1)
                        pe.wait_ge(S["v_copied"], jobs.index(att) + 1)
                        scores(a, 0)
                        scores(a, 1)
                        fill(source, 6)
                        turn_probs(a, 0)
                        scores(a, 2)
                        fill(source, 6)
                        weigh_values(a, 0)
                        turn_probs(a, 1)
                        scores(a, 3)
                        fill(source, 6)
                        weigh_values(a, 1)
                        turn_probs(a, 2)
                        fill(source, 5)
                        weigh_values(a, 2)
                        turn_probs(a, 3)
                        fill(source, 1)
                        weigh_values(a, 3)
                    fill(source, 24)
                    if nxt in number:
                        turn_qk(jobs.index(nxt))

            @block.vector
            def _(dve):
                def row_max(a, hp):
                    g, t = prompt[a]
                    dve.wait_ge(S["scores_ready"], 4 * a + hp + 1)
                    if a >= 2 and hp == 0:
                        dve.wait_ge(o_out[a % 2], 16 * (a // 2))
                    first = P * (not has_prev(g, t))
                    nc.vector.tensor_reduce(orow[:, a % 2, HW + 2 * hp:HW + 2 * hp + 2], sps[:, hp % 2, :, first:2 * P],
                                            AX.X, ALU.max, negate=True).then_inc(S["max_ready"], 1)

                def copy_pT(a, hp):
                    g, t = prompt[a]
                    first = P * (not has_prev(g, t))
                    dve.wait_ge(S["probs_turned"], 4 * a + hp + 1)
                    if 4 * a + hp >= 2:
                        dve.wait_ge(S["heads_done"], 4 * a + hp - 1)
                    nc.vector.tensor_copy(pT[:, hp % 2, :, first:2 * P],
                                          tps.rearrange("p (h k) -> p h k", h=2)[:, :, first:2 * P]
                                          ).then_inc(S["pT_ready"], 1)

                def square_sum(n, which):
                    t, w = jobs[n][1], "qk".index(which)
                    dve.wait_ge(S[which + "_squared"], n + 1)
                    if n >= 1:
                        dve.wait_ge(S[which + "_rstd"], n)
                    nc.vector.tensor_reduce(stat[0:rows(t), w, 0, :],
                                            sq[0:rows(t), w, :].rearrange("p (h e) -> p h e", h=NH),
                                            AX.X, ALU.add).then_inc(S[which + "_summed"], 1)

                def scale(n, which, bank):
                    t, w = jobs[n][1], "qk".index(which)
                    r = rows(t)
                    dve.wait_ge(S[which + "_rstd"], n + 1)
                    nc.vector.tensor_tensor(sq[0:r, w, :].rearrange("p (h e) -> p h e", h=NH),
                                            bank[0:r, :].rearrange("p (h e) -> p h e", h=NH),
                                            bcast(stat[0:r, w, 2, :].unsqueeze(2), [r, NH, E]),
                                            ALU.mult).then_inc(S[which + "_scaled"], 1)

                for att, nxt in steps:
                    a = number.get(att)
                    n = jobs.index(nxt) if nxt else None
                    if att:
                        row_max(a, 0)
                        row_max(a, 1)
                        copy_pT(a, 0)
                        row_max(a, 2)
                    if nxt:
                        square_sum(n, "q")
                    if att:
                        copy_pT(a, 1)
                        row_max(a, 3)
                    if nxt:
                        scale(n, "q", pq)
                        square_sum(n, "k")
                    if att:
                        copy_pT(a, 2)
                    if nxt:
                        scale(n, "k", pk)
                    if att:
                        copy_pT(a, 3)
                    if nxt in number:
                        b = number[nxt]
                        dve.wait_ge(S["q_turned"], b + 1)
                        nc.vector.tensor_copy(qT, tps.rearrange("p (h k) -> p h k", h=4)).then_inc(S["qT_ready"], 1)
                        dve.wait_ge(S["k_turned"], b + 1)
                        nc.vector.tensor_copy(kT[:, b % 2, :, :], tk.rearrange("p (h k) -> p h k", h=4)
                                              ).then_inc(S["kT_ready"], 1)

            @block.scalar
            def _(act):
                def square(n, which, bank):
                    t, w = jobs[n][1], "qk".index(which)
                    act.wait_ge(S[which + "_projected"], n + 1)
                    if n >= 1:
                        act.wait_ge(S[which + "_normed"], n)
                    nc.scalar.activation(sq[0:rows(t), w, :], bank[0:rows(t), :], ACT.Square
                                         ).then_inc(S[which + "_squared"], 1)

                def exps(a, hp):
                    g, t = prompt[a]
                    first = P * (not has_prev(g, t))
                    act.wait_ge(S["max_ready"], 4 * a + hp + 1)
                    if 4 * a + hp >= 2:
                        act.wait_ge(S["probs_turned"], 4 * a + hp - 1)
                    for h in range(2):
                        c = 2 * hp + h
                        nc.scalar.activation(prob[:, hp % 2, h, first:2 * P],
                                             sps[:, hp % 2, h, first:2 * P], ACT.Exp,
                                             bias=orow[:, a % 2, HW + c:HW + c + 1],
                                             accum_out=orow[:, a % 2, HW + NH + c:HW + NH + c + 1]
                                             ).then_inc(S["probs_ready"], 1)

                for att, nxt in steps:
                    a = number.get(att)
                    n = jobs.index(nxt) if nxt else None
                    if att:
                        exps(a, 0)
                        exps(a, 1)
                    if nxt:
                        square(n, "q", pq)
                    if att:
                        exps(a, 2)
                    if nxt:
                        square(n, "k", pk)
                    if att:
                        exps(a, 3)
                    if nxt:
                        t = nxt[1]
                        act.wait_ge(S["v_projected"], n + 1)
                        kv_free(act, n)
                        nc.scalar.activation(kv_rows(n, 1)[0:rows(t), :], pv[0:rows(t), :], ACT.Copy
                                             ).then_inc(S["v_copied"], 1)
                    if att:
                        act.wait_ge(S["heads_done"], 4 * a + 4)
                        nc.scalar.activation(orow[:, a % 2, 0:HW], po[:, :], ACT.Copy).then_inc(S["o_ready"], 1)

            @block.gpsimd
            def _(pool):
                for n, (g, t) in enumerate(jobs):
                    r = rows(t)
                    for w, which in enumerate("qk"):
                        pool.wait_ge(S[which + "_summed"], n + 1)
                        nc.gpsimd.tensor_scalar(stat[0:r, w, 1, :], stat[0:r, w, 0, :], 1.0 / E, EPS,
                                                ALU.mult, ALU.add).then_inc(S[which + "_mean"], 1)
                        pool.wait_ge(S[which + "_mean"], n + 1)
                        if n >= 1:
                            pool.wait_ge(S[which + "_scaled"], n)
                        nc.gpsimd.tensor_tensor(stat[0:r, w, 2, :], stat[0:r, w, 1, :], m.minus_half[0:r, 0:NH],
                                                ALU.pow).then_inc(S[which + "_rstd"], 1)
                        pool.wait_ge(S[which + "_scaled"], n + 1)
                        if which == "k":
                            kv_free(pool, n)
                            dst = kv_rows(n, 0)
                        else:
                            if t < NT and number[(g, t)] >= 1:
                                pool.wait_ge(S["q_turned"], number[(g, t)])
                            dst = qn if t < NT else m.q_s[:, g, :]
                        nc.gpsimd.tensor_tensor(dst[0:r, :].rearrange("p (h e) -> p h e", h=NH),
                                                sq[0:r, w, :].rearrange("p (h e) -> p h e", h=NH),
                                                bcast(m.qk_gain[0:r, w, g, :].unsqueeze(1), [r, NH, E]),
                                                ALU.mult).then_inc(S[which + "_normed"], 1)
                pool.wait_ge(S["o_ready"], len(prompt))


def stage_decode_attention(nc, m):
    with ExitStack() as ctx:
        def sb(name, shape, dt=F32):
            return ctx.enter_context(nc.sbuf_tensor("da_" + name, shape, dt))[:]

        keys, vals = ([m.ring[:, j, :].rearrange("p (b c) -> p b c", b=NB) for j in js] for js in ((0, 1), (2, 5)))
        o_s = sb("o_s", [NB, NG, OROW])
        prod = sb("prod", [P, 2, HW])
        weighed = sb("weighed", [P, 2, HW])
        score = sb("score", [P, NH, NB])
        pT = sb("pT", [P, NH, NB])
        prob = sb("prob", [NB, NH, P])
        new = sb("new", [NB, HW])
        s_new = sb("s_new", [NB, 4, NH])
        QB = 6
        qb = sb("qb", [P, QB, HW])
        q_spread = [semaphore(nc, m, f"da_q_spread{i}") for i in range(QB)]
        sT = ctx.enter_context(nc.psum_tensor("da_sT", [P, NH, P], F32))[0:NB]
        pb = ctx.enter_context(nc.psum_tensor("da_pb", [P, 512], F32))[:, 0:NH * NB].rearrange("p (h b) -> p h b", h=NH)
        acc = ctx.enter_context(nc.psum_tensor("da_acc", [P, 512], F32))[0:NB]
        late = m.oBT.rearrange("p h t -> p (h t)")[0:28, 3 * NG * HW:]
        conv_rows = [late[:, 0:20 * P], sb("conv_rows", [28, 4 * P])]
        conv_ps = ctx.enter_context(nc.psum_tensor("da_conv", [P, 2, 16, 32], F32))[:]
        rows_landed, conv_turned = (semaphore(nc, m, "da_" + n) for n in ("rows_landed", "conv_turned"))
        S = semaphores(nc, m, "da", "q_stored scored dve_step scores_turned shifted exp_done new_exp_done probs_turned "
                       "pT_ready values_weighed summed_over_keys o_ready o_stored")
        keys_landed = [semaphore(nc, m, f"da_keys_landed{g}") for g in range(NG)]
        vals_landed = [semaphore(nc, m, f"da_vals_landed{g}") for g in range(NG)]

        with nc.Block() as block:
            @block.sync
            def _(sp):
                for part, c in ((conv_rows[0], slice(0, 20 * P)), (conv_rows[1], slice(20 * P, 24 * P))):
                    sp.dma_start(part[0:24], m.conv_state_rows[:, c]).then_inc(rows_landed, 16)
                    sp.dma_start(part[24:28], m.conv_w_rows[:, c]).then_inc(rows_landed, 16)
                sp.dma_start(m.s_conv[:, 0:2, :], m.conv_state_rows.rearrange("(b i) c -> b i c", i=3)[:, 1:3, :]
                             ).then_inc(m.outputs_stored, 16)
                m.n_outputs += 1
                sp.dma_start(m.q_scr, m.q_s.rearrange("p g c -> p (g c)")).then_inc(S["q_stored"], 16)
                sp.wait_ge(S["q_stored"], 16)

                def load_keys(g):
                    if g >= 2:
                        sp.wait_ge(S["scored"], NB * (g - 1))
                    sp.dma_start(keys[g % 2], m.caches[g][0:P * SWA[g][1]:SWA[g][1], :, 0:HW]
                                 ).then_inc(keys_landed[g], 16)

                def load_vals(g):
                    if g >= 2:
                        sp.wait_ge(S["values_weighed"], NB * (g - 1))
                    sp.dma_start(vals[g % 2], m.caches[g][0:P * SWA[g][1]:SWA[g][1], :, HW:2 * HW]
                                 ).then_inc(vals_landed[g], 16)

                extra = {0: lambda: load_keys(0), 4: lambda: load_vals(0), 8: lambda: load_keys(1),
                         10: lambda: load_vals(1), 13: lambda: load_keys(2), 20: lambda: load_vals(2)}
                for n in range(NG * NB):
                    if n in extra:
                        extra[n]()
                    if n >= QB:
                        sp.wait_ge(S["scored"], n - QB + 1)
                    g, b = divmod(n, NB)
                    sp.dma_start(qb[:, n % QB, :], m.q_scr[b:b + 1, g * HW:(g + 1) * HW].to_broadcast([P, HW])
                                 ).then_inc(q_spread[n % QB], 16)
                sp.wait_ge(S["o_ready"], NG)
                sp.dma_start(m.o_s_scr, o_s).then_inc(S["o_stored"], 16)
                sp.wait_ge(S["o_stored"], 16)

            @block.tensor
            def _(pe):
                pe.wait_ge(rows_landed, 64)
                for cw in range(24):
                    src = conv_rows[0][:, cw * P:(cw + 1) * P] if cw < 20 else conv_rows[1][:, (cw - 20) * P:(cw - 19) * P]
                    mm = nc.tensor.transpose(conv_ps[:, cw // 16, cw % 16, 0:28], src, m.ident[0:28, 0:28])
                mm.then_inc(conv_turned, 1)
                for g in range(NG):
                    pe.wait_ge(S["scored"], NB * (g + 1))
                    for h in range(NH):
                        mm = nc.tensor.transpose(sT[:, h, :], score[:, h, :], m.ident)
                    mm.then_inc(S["scores_turned"], 1)
                    pe.wait_ge(S["exp_done"], g + 1)
                    for h in range(NH):
                        mm = nc.tensor.transpose(pb[:, h, :], prob[:, h, :], m.ident[0:NB, 0:NB])
                    mm.then_inc(S["probs_turned"], 1)
                    for b in range(NB):
                        pe.wait_ge(S["values_weighed"], g * NB + b + 1)
                        mm = nc.tensor.matmul(acc, m.pick_col[:, b, :], weighed[:, b % 2, :],
                                              start=(b == 0), stop=(b == NB - 1))
                        mm.then_inc(S["summed_over_keys"], 1)

            @block.vector
            def _(dve):
                step = Chain(dve, S["dve_step"])
                heads = "p (h e) -> p h e"

                def scores(g):
                    dve.wait_ge(keys_landed[g], 16)
                    for b in range(NB):
                        n = g * NB + b
                        dve.wait_ge(q_spread[n % QB], 16 * (n // QB + 1))
                        step(nc.vector.tensor_tensor(prod[:, b % 2], keys[g % 2][:, b, :], qb[:, n % QB, :], ALU.mult))
                        nc.vector.tensor_reduce(score[:, :, b], prod[:, b % 2].rearrange(heads, h=NH), AX.X, ALU.add
                                                ).then_inc(S["scored"], 1)
                    step(nc.vector.tensor_tensor(new, m.q_s[:, g], m.kv_s[:, g, 0], ALU.mult))
                    step(nc.vector.tensor_reduce(s_new[:, 0], new.rearrange(heads, h=NH), AX.X, ALU.add))

                def softmax(g):
                    row = o_s[:, g, :]
                    dve.wait_ge(S["scores_turned"], g + 1)
                    step(nc.vector.tensor_reduce(s_new[:, 3], sT, AX.X, ALU.max))
                    step(nc.vector.tensor_tensor(s_new[:, 3], s_new[:, 3], s_new[:, 0], ALU.max))
                    step(nc.vector.tensor_tensor(prob, sT, bcast(s_new[:, 3].unsqueeze(2), [NB, NH, P]), ALU.subtract))
                    nc.vector.tensor_tensor(s_new[:, 1], s_new[:, 0], s_new[:, 3], ALU.subtract).then_inc(S["shifted"], 1)
                    step(nc.vector.tensor_scalar(row[:, HW:HW + NH], s_new[:, 3], -1.0, None, ALU.mult))
                    dve.wait_ge(S["exp_done"], g + 1)
                    dve.wait_ge(S["new_exp_done"], g + 1)
                    dve.wait_ge(S["probs_turned"], g + 1)
                    nc.vector.tensor_copy(pT, pb).then_inc(S["pT_ready"], 1)
                    step(nc.vector.tensor_reduce(row[:, HW + NH:OROW], prob, AX.X, ALU.add))
                    step(nc.vector.tensor_tensor(row[:, HW + NH:OROW], row[:, HW + NH:OROW], s_new[:, 2], ALU.add))

                def finish(g):
                    row = o_s[:, g, :]
                    step(nc.vector.tensor_tensor(new.rearrange(heads, h=NH), m.kv_s[:, g, 1].rearrange(heads, h=NH),
                                                 bcast(s_new[:, 2].unsqueeze(2), [NB, NH, E]), ALU.mult))
                    dve.wait_ge(S["summed_over_keys"], NB * (g + 1))
                    nc.vector.tensor_tensor(row[:, 0:HW], acc, new, ALU.add).then_inc(S["o_ready"], 1)
                    dve.wait_ge(S["o_ready"], g + 1)

                dve.wait_ge(conv_turned, 1)
                for a, n in ((0, 16), (1, 8)):
                    c = slice(16 * a, 16 * a + n)
                    nc.vector.tensor_copy(m.conv_state[:, c].rearrange("p c b i -> p c (b i)"), conv_ps[:, a, 0:n, 0:24])
                    nc.vector.tensor_copy(m.conv_w[:, c], conv_ps[:, a, 0:n, 24:28])
                scores(0)
                for g in range(NG):
                    softmax(g)
                    if g + 1 < NG:
                        scores(g + 1)
                    finish(g)

            @block.scalar
            def _(act):
                for g in range(NG):
                    act.wait_ge(S["shifted"], g + 1)
                    nc.scalar.activation(prob, prob, ACT.Exp).then_inc(S["exp_done"], 1)
                    nc.scalar.activation(s_new[:, 2], s_new[:, 1], ACT.Exp).then_inc(S["new_exp_done"], 1)

            @block.gpsimd
            def _(pool):
                for g in range(NG):
                    pool.wait_ge(vals_landed[g], 16)
                    pool.wait_ge(S["pT_ready"], g + 1)
                    for b in range(NB):
                        n = g * NB + b
                        if n >= 2:
                            pool.wait_ge(S["summed_over_keys"], n - 1)
                        nc.gpsimd.tensor_tensor(weighed[:, b % 2].rearrange("p (h e) -> p h e", h=NH),
                                                vals[g % 2][:, b].rearrange("p (h e) -> p h e", h=NH),
                                                bcast(pT[:, :, b].unsqueeze(2), [P, NH, E]), ALU.mult
                                                ).then_inc(S["values_weighed"], 1)


def stage_deltanet(nc, m):
    G3, C3 = 3, TOK // 3
    NC = NT
    with ExitStack() as ctx:
        def sb(name, shape, dt=F32):
            return ctx.enter_context(nc.sbuf_tensor("dn_" + name, shape, dt))[:]

        work, at = m.ring[:, 0:3, :].rearrange("p a b -> p (a b)"), [0]

        def carve(n):
            at[0] += n
            return work[:, at[0] - n:at[0]]

        cm = carve(2 * 4 * TOK).rearrange("p (a w t) -> p a w t", a=2, w=4)
        raw = carve(TOK + 3)
        conv = carve(TOK)
        decay = carve(1024).rearrange("p (c k) -> p c k", c=NC)
        spare = m.ring[:, 5, :].rearrange("p (a c k) -> p a c k", a=4, c=NC)
        aT, U_, Us, T = (spare[:, i] for i in range(4))
        big = [sb(f"big{i}", [P, NC, P]) for i in range(5)]
        Tt, M, Vt, Kdec, o_all = big
        sqs = m.ring[:, 5, 2 * P * NC:2 * P * NC + TOK]
        rs = sb("rs", [P, 2, 2, NT + 1])
        level = sb("level", [P, 7, P])
        S_ = sb("S", [P, 2, P])
        X = sb("X", [P, P])
        vn = sb("vn", [P, P])
        qs = sb("qs", [P, P])
        st_o = sb("st_o", [P, 3, NC])
        gate = sb("gate", [P, 6, NT + 1, DNH])
        beta, egc, neg_egc, kd, gcp, neg_gc, egt = (sb(x, [P, NC, DNH]) for x in
                                                    ("beta", "egc", "neg_egc", "kd", "gcp", "neg_gc", "egt"))
        bankp = [ctx.enter_context(nc.psum_tensor(f"dn_p{i}", [P, 512], F32))[:] for i in range(3)]
        x = [ctx.enter_context(nc.psum_tensor(f"dn_x{i}", [P, 4, P], F32))[:] for i in range(5)]
        qk_bank = [b.rearrange("p (c k) -> p c k", c=4) for b in bankp[0:2]]
        kv_bank = [x[4], bankp[2].rearrange("p (c k) -> p c k", c=4)] * 2
        S = semaphores(nc, m, "dn", "ba_done gates_stepped dve_step g_ready gc_done act_gates gates_ready projected "
                       "evac_act ssq_done evac_dve spread tap0 conv_done silu_done squared rs_ready "
                       "R_done decay_ready KK_done U_ready QK_done kv_turned kv_ready "
                       "aT_ready turned_T Tt_ready T_ready Us_ready M_done M_copied TMt_done TM_done "
                       "Tt_updated T_updated ks_done qs_done X_ready qs_scaled v_done vn_copied o2_done "
                       "ds_done S_ready o_added o_squared o_summed o_rstd o_scaled o_turned oT_ready "
                       "tails_kept pool_step raw_zero tapped S_zero")
        S_stored = [semaphore(nc, m, f"dn_S_stored{i}") for i in range(2)]
        for h in range(DNH):
            m.last_use[m.plan.index(("dn", h))] = (S["projected"], 12 * (h + 1))
        W_ORDER = ("k", "q", "v", "z")
        WPOS = {"q": 0, "k": 1, "v": 2, "z": 3}

        def half(t, u):
            return t[:, 4 * u:4 * u + 4]

        def evac_ready(i):
            return 8 * (i + 1) + (1 if i >= 6 else 0) + (4 if i >= 9 else 0)

        def head_items():
            return [("proj", "k"), ("proj", "q"), ("ssq", "k"), ("proj", "v"), ("spread", "k"), ("ssq", "q"),
                    ("proj", "z"), ("spread", "q")]

        def chunks_of(j):
            return [(4 * j + c, P, c * P) for c in range(4)] if j < 2 else [(NT, NB, 0)]

        with nc.Block() as block:
            @block.sync
            def _(sp):
                for h in range(DNH):
                    if h + 2 < DNH:
                        load_chunk(sp, m, m.plan.index(("dn", h)) + 2)
                    else:
                        i = h + 2 - DNH
                        sp.wait_ge(S["projected"], 12 * (h + 1))
                        sp.dma_start(m.ring[:, SLOTS_S[i], :].rearrange("p (n v) -> p n v", v=DK),
                                     m.state_S[4 * i:4 * i + 4].rearrange("b h k v -> k (b h) v")
                                     ).then_inc(m.S_landed[i], 16)
                    if h >= 1:
                        sp.wait_ge(S["S_ready"], NC * h)
                        sp.dma_start(m.p_S[h - 1], S_[:, (h - 1) % 2, :]).then_inc(S_stored[(h - 1) % 2], 16)
                sp.wait_ge(S["S_ready"], NC * DNH)
                sp.dma_start(m.p_S[DNH - 1], S_[:, (DNH - 1) % 2, :]).then_inc(S_stored[1], 16)
                for i in range(2):
                    sp.wait_ge(S_stored[i], 16 * (DNH // 2))

            @block.tensor
            def _(pe):
                pe.wait_ge(m.small_landed, 16 * len(m.small_loads))
                ba = x[0].rearrange("p c k -> p (c k)")[:, 0:16 * (NT + 1)].rearrange("p (t c) -> p t c", c=16)
                for t in range(NT + 1):
                    r = P if t < NT else NB
                    for k in range(KD):
                        mm = nc.tensor.matmul(ba[0:r, t, :], m.hT[:, k, t * P:t * P + r], m.w_ba[:, k, :],
                                              start=(k == 0), stop=(k == KD - 1))
                mm.then_inc(S["ba_done"], 1)
                pe.wait_ge(S["g_ready"], 1)
                g = m.g_all[:, 0:NT, :].rearrange("p t h -> p (t h)")
                nc.tensor.matmul(x[1][:, 0, 0:64], m.triu, g, start=True, stop=True)
                nc.tensor.matmul(x[2][:, 0, 0:64], m.ones, g, start=True, stop=True).then_inc(S["gc_done"], 1)

                def projections(h):
                    weights = chunk(pe, m, "dn", h).rearrange("p (k w n) -> p k w n", k=KD, w=4)
                    acts, dves = 12 * h, 8 * h
                    read = [(S["evac_act"], acts - 2 + j) for j in range(G3)] if h else [None] * G3
                    for kind, part in head_items():
                        which = "kq".find(part)
                        if kind == "ssq":
                            pe.wait_ge(*read[0])
                            pe.wait_ge(S["squared"], 2 * h + which + 1)
                            for t in range(NT + 1):
                                n = P if t < NT else NB
                                mm = nc.tensor.matmul(bankp[0][0:n, t:t + 1], sqs[:, t * P:t * P + n], m.ones[:, 0:1],
                                                      start=True, stop=True)
                            mm.then_inc(S["ssq_done"], 1)
                            dves += 1
                            read[0] = (S["evac_dve"], dves)
                            yield
                            continue
                        for j in range(G3):
                            if read[j]:
                                pe.wait_ge(*read[j])
                            if kind == "proj":
                                for k in range(KD):
                                    mm = nc.tensor.matmul(bankp[j][:, 0:C3], weights[:, k, WPOS[part], :],
                                                          m.hT[:, k, j * C3:(j + 1) * C3],
                                                          start=(k == 0), stop=(k == KD - 1))
                                    if k == KD - 1:
                                        mm.then_inc(S["projected"], 1)
                                    yield
                                acts += 1
                                read[j] = (S["evac_act"], acts)
                            else:
                                pe.wait_ge(S["rs_ready"], 2 * h + which + 1)
                                for t, n, col in chunks_of(j):
                                    mm = nc.tensor.matmul(bankp[j][:, col:col + n],
                                                          bcast(rs[0:n, which, 1, t:t + 1], [n, P]), m.ident[0:n, 0:n],
                                                          start=True, stop=True)
                                mm.then_inc(S["spread"], 1)
                                dves += 1
                                read[j] = (S["evac_dve"], dves)
                                yield

                def fill(source, n):
                    for _ in range(n):
                        if next(source, 0) == 0:
                            return

                def prepare(h):
                    q, k, v = (cm[:, h % 2, w] for w in range(3))

                    def own(t, c):
                        return t[:, c * P:(c + 1) * P]

                    if h >= 1:
                        pe.wait_ge(S["o_added"], NC * h)
                        pe.wait_ge(S["qs_scaled"], NC * h)
                    pe.wait_ge(S["evac_dve"], 8 * h + 4)
                    for u in range(2):
                        for c in range(4):
                            kc = own(k, 4 * u + c)
                            mm = nc.tensor.matmul(x[2 + u][:, c, :], kc, kc, start=True, stop=True)
                        mm.then_inc(S["KK_done"], 1)
                    pe.wait_ge(S["gates_ready"], 1)
                    for u in range(2):
                        nc.tensor.matmul(x[u], m.ident_b, bcast(m.mask_decay.unsqueeze(1), [P, 4, P]),
                                         start=True, stop=False, skip_group_check=True)
                        for c in range(4):
                            mm = nc.tensor.matmul(x[u][:, c, :], bcast(m.g_all[:, 4 * u + c, h:h + 1], [P, P]), m.triu,
                                                  start=False, stop=True, skip_group_check=True)
                        mm.then_inc(S["R_done"], 1)
                    for i, (src, u) in enumerate(((k, 0), (k, 1), (v, 0), (v, 1))):
                        if i == 1:
                            pe.wait_ge(S["evac_dve"], 8 * h + 8)
                        if i == 2:
                            pe.wait_ge(S["silu_done"], 3 * h + 3)
                        if i >= 2:
                            pe.wait_ge(S["kv_ready"], 4 * h + i - 1)
                        for c in range(4):
                            mm = nc.tensor.transpose(kv_bank[i][:, c, :], own(src, 4 * u + c), m.ident)
                        mm.then_inc(S["kv_turned"], 1)
                    for u in range(2):
                        for c in range(4):
                            mm = nc.tensor.matmul(qk_bank[u][:, c, :], own(k, 4 * u + c), own(q, 4 * u + c),
                                                  start=True, stop=True)
                        mm.then_inc(S["QK_done"], 1)
                    if h >= 1:
                        turn_o(h - 1)
                    for u in range(2):
                        pe.wait_ge(S["Tt_ready"], 2 * h + u + 1)
                        for c in range(4):
                            mm = nc.tensor.transpose(x[2 + u][:, c, :], Tt[:, 4 * u + c, :], m.ident)
                        mm.then_inc(S["turned_T"], 1)
                    for lev in range(6):
                        for u in range(2):
                            n = 12 * h + 2 * lev + u
                            pe.wait_ge(S["Us_ready"], n + 1)
                            if lev == 0:
                                pe.wait_ge(S["T_ready"], 2 * h + u + 1)
                                if h:
                                    pe.wait_ge(S["oT_ready"], 2 * (h - 1) + u + 1)
                                else:
                                    pe.wait_ge(S["decay_ready"], 4 * (u + 1))
                            else:
                                pe.wait_ge(S["T_updated"], 10 * h + 2 * (lev - 1) + u + 1)
                            for c in range(4):
                                mm = nc.tensor.matmul(x[u][:, c, :], Us[:, 4 * u + c, :], T[:, 4 * u + c, :],
                                                      start=True, stop=True)
                            mm.then_inc(S["M_done"], 1)
                        for u in range(2):
                            n = 12 * h + 2 * lev + u
                            pe.wait_ge(S["M_copied"], n + 1)
                            if lev:
                                pe.wait_ge(S["Tt_updated"], 12 * h + 2 * (lev - 1) + u + 1)
                            if lev < 5:
                                for c in range(4):
                                    mm = nc.tensor.matmul(x[u][:, c, :], Tt[:, 4 * u + c, :], M[:, 4 * u + c, :],
                                                          start=True, stop=True)
                                mm.then_inc(S["TM_done"], 1)
                            for c in range(4):
                                mm = nc.tensor.matmul(x[2 + u][:, c, :], M[:, 4 * u + c, :], Tt[:, 4 * u + c, :],
                                                      start=True, stop=True)
                            mm.then_inc(S["TMt_done"], 1)

                def turn_o(h):
                    for u in range(2):
                        pe.wait_ge(S["o_scaled"], h + 1)
                        if h + 1 < DNH:
                            pe.wait_ge(S["decay_ready"], 8 * (h + 1) + 4 * (u + 1))
                        for c in range(4):
                            mm = nc.tensor.transpose(x[u][:, c, :], o_all[:, 4 * u + c, :], m.ident)
                        mm.then_inc(S["o_turned"], 1)

                def recur(h, c, point):
                    q, k = (cm[:, h % 2, w, c * P:(c + 1) * P] for w in range(2))
                    n = NC * h + c
                    state = S_[:, h % 2, :]
                    if point == 0:
                        if c:
                            pe.wait_ge(S["S_ready"], n)
                        else:
                            pe.wait_ge(S["S_zero"], h + 1)
                            pe.wait_ge(S["Tt_updated"], 12 * (h + 1))
                            pe.wait_ge(S["M_copied"], 12 * (h + 1))
                            pe.wait_ge(S["aT_ready"], 2 * (h + 1))
                        nc.tensor.matmul(x[0][:, 0, :], k, state, start=True, stop=True).then_inc(S["ks_done"], 1)
                        if n:
                            pe.wait_ge(S["qs_scaled"], n)
                        nc.tensor.matmul(x[4][:, 0, :], q, state, start=True, stop=True).then_inc(S["qs_done"], 1)
                    elif point == 1:
                        pe.wait_ge(S["X_ready"], n + 1)
                        nc.tensor.matmul(x[1][:, 0, :], Tt[:, c, :], X, start=True, stop=True).then_inc(S["v_done"], 1)
                    else:
                        pe.wait_ge(S["vn_copied"], n + 1)
                        nc.tensor.matmul(x[3][:, 0, :], Kdec[:, c, :], vn, start=True, stop=True).then_inc(S["ds_done"], 1)
                        if n:
                            pe.wait_ge(S["o_added"], n)
                        nc.tensor.matmul(x[2][:, 0, :], aT[:, c, :], vn, start=True, stop=True).then_inc(S["o2_done"], 1)

                for h in range(-1, DNH):
                    source = projections(h + 1) if h + 1 < DNH else iter(())
                    for c in range(NC):
                        for point in range(3):
                            if h >= 0:
                                recur(h, c, point)
                            fill(source, 4)
                    fill(source, 200)
                    if h + 1 < DNH:
                        prepare(h + 1)
                    else:
                        turn_o(h)

            @block.scalar
            def _(act):
                gates = Chain(act, S["act_gates"])
                act.wait_ge(S["gates_stepped"], 1)
                nb, tokens = gate[:, 1], gate[:, 0]
                gates(nc.scalar.activation(gate[:, 1], gate[:, 1], ACT.Exp, scale=-1.0))
                gates(nc.scalar.activation(gate[:, 2], gate[:, 0], ACT.Abs))
                gates(nc.scalar.activation(gate[:, 3], gate[:, 2], ACT.Exp, scale=-1.0))
                gates(nc.scalar.activation(gate[:, 4], gate[:, 3], ACT.Ln, bias=1.0))
                gates(nc.scalar.activation(m.neg_a, m.neg_a, ACT.Exp))
                act.wait_ge(S["gc_done"], 1)
                act.wait_ge(S["gates_stepped"], 2)
                gates(nc.scalar.activation(egc, gcp, ACT.Exp))
                gates(nc.scalar.activation(kd, kd, ACT.Exp))
                gates(nc.scalar.activation(egt, x[2][:, 0, 0:64].rearrange("p (t h) -> p t h", h=DNH), ACT.Exp))

                def evacuate(h, i):
                    part, j = W_ORDER[i // 3], i % 3
                    n = 12 * h + i
                    act.wait_ge(S["projected"], n + 1)
                    bank = bankp[j][:, 0:C3]
                    if part == "z":
                        ins = nc.scalar.activation(cm[:, h % 2, 3, j * C3:(j + 1) * C3], bank, ACT.Silu)
                    else:
                        if j == 0:
                            act.wait_ge(S["raw_zero"], 1)
                            if h or i >= 3:
                                act.wait_ge(S["conv_done"], 3 * h + i // 3)
                                act.wait_ge(S["tails_kept"], 3 * h + i // 3)
                        ins = nc.scalar.activation(raw[:, 3 + j * C3:3 + (j + 1) * C3], bank, ACT.Copy)
                    ins.then_inc(S["evac_act"], 1)

                def silu(h, part):
                    i = W_ORDER.index(part)
                    act.wait_ge(S["conv_done"], 3 * h + i + 1)
                    nc.scalar.activation(cm[:, h % 2, WPOS[part], :], conv, ACT.Silu).then_inc(S["silu_done"], 1)

                def square(h, part):
                    i = W_ORDER.index(part)
                    act.wait_ge(S["silu_done"], 3 * h + i + 1)
                    if h or part == "q":
                        act.wait_ge(S["ssq_done"], 2 * h + (part == "q"))
                    nc.scalar.activation(sqs, cm[:, h % 2, WPOS[part], :], ACT.Square
                                         ).then_inc(S["squared"], 1)

                def prepare(h):
                    act.wait_ge(S["gates_ready"], 1)
                    if h:
                        act.wait_ge(S["o_summed"], h)
                    for c in range(NC):
                        act.wait_ge(S["R_done"], 2 * h + c // 4 + 1)
                        nc.scalar.activation(decay[:, c, :], x[c // 4][:, c % 4, :], ACT.Exp,
                                             bias=neg_gc[:, c, h:h + 1]).then_inc(S["decay_ready"], 1)
                    for u in range(2):
                        act.wait_ge(S["turned_T"], 2 * h + u + 1)
                        nc.scalar.activation(half(T, u), x[2 + u], ACT.Copy).then_inc(S["T_ready"], 1)
                    for lev in range(6):
                        for u in range(2):
                            act.wait_ge(S["M_done"], 12 * h + 2 * lev + u + 1)
                            if h or lev:
                                act.wait_ge(S["TMt_done"], 12 * h + 2 * (lev - 1) + u + 1)
                            nc.scalar.activation(half(M, u), x[u], ACT.Copy).then_inc(S["M_copied"], 1)

                def recur(h, c, point):
                    n = NC * h + c
                    if point == 0:
                        act.wait_ge(S["qs_done"], n + 1)
                        if n:
                            act.wait_ge(S["o_added"], n)
                        nc.scalar.activation(qs, x[4][:, 0, :], ACT.Copy, scale=egc[:, c, h:h + 1]
                                             ).then_inc(S["qs_scaled"], 1)
                    elif point == 1:
                        act.wait_ge(S["v_done"], n + 1)
                        if n:
                            act.wait_ge(S["o2_done"], n)
                        nc.scalar.activation(vn, x[1][:, 0, :], ACT.Copy, scale=beta[:, c, h:h + 1]
                                             ).then_inc(S["vn_copied"], 1)

                for h in range(-1, DNH):
                    done = 0
                    for c in range(NC):
                        for point in range(3):
                            if h >= 0:
                                recur(h, c, point)
                            if h + 1 < DNH:
                                filled = 4 * (3 * c + point + 1)
                                while done < 12 and evac_ready(done) <= filled:
                                    evacuate(h + 1, done)
                                    done += 1
                                if (c, point) == (3, 0):
                                    silu(h + 1, "k")
                                if (c, point) == (3, 1):
                                    square(h + 1, "k")
                                if (c, point) == (5, 0):
                                    silu(h + 1, "q")
                                if (c, point) == (5, 1):
                                    square(h + 1, "q")
                    if h + 1 < DNH:
                        while done < 12:
                            evacuate(h + 1, done)
                            done += 1
                        silu(h + 1, "v")
                    if h >= 0:
                        act.wait_ge(S["o_added"], NC * (h + 1))
                        nc.scalar.activation(decay, o_all, ACT.Square).then_inc(S["o_squared"], 1)
                    if h + 1 < DNH:
                        prepare(h + 1)

            @block.vector
            def _(dve):
                step = Chain(dve, S["dve_step"])
                ba = x[0].rearrange("p c k -> p (c k)")[:, 0:16 * (NT + 1)].rearrange("p (t c) -> p t c", c=16)
                nc.vector.memset(raw[:, 0:3], 0.0).then_inc(S["raw_zero"], 1)
                step(nc.vector.memset(rs, 1.0))
                step(nc.vector.memset(gate[:, 0:2], 0.0))
                dve.wait_ge(S["ba_done"], 1)
                for t0, t1, rows in ((0, NT, P), (NT, NT + 1, NB)):
                    step(nc.vector.tensor_copy(gate[0:rows, 1, t0:t1], ba[0:rows, t0:t1, 0:DNH]))
                    step(nc.vector.tensor_tensor(gate[0:rows, 0, t0:t1], ba[0:rows, t0:t1, DNH:16],
                                                 bcast(m.dt_bias[0:rows].unsqueeze(1), [rows, t1 - t0, DNH]), ALU.add))
                nc.vector.tensor_copy(gate[:, 5], gate[:, 0]).then_inc(S["gates_stepped"], 1)
                dve.wait_ge(S["act_gates"], 5)
                dve.wait_ge(S["gates_stepped"], 1)
                step(nc.vector.tensor_scalar(gate[:, 1], gate[:, 1], 1.0, None, ALU.add))
                step(nc.vector.reciprocal(m.beta_all, gate[:, 1]))
                step(nc.vector.scalar_tensor_tensor(out=gate[:, 5], in0=gate[:, 0], scalar=0.0, in1=gate[:, 4],
                                                    op0=ALU.max, op1=ALU.add))
                step(nc.vector.tensor_scalar(m.neg_a, m.neg_a, -1.0, None, ALU.mult))
                nc.vector.tensor_tensor(m.g_all, gate[:, 5], bcast(m.neg_a.unsqueeze(1), [P, NT + 1, DNH]), ALU.mult
                                        ).then_inc(S["g_ready"], 1)
                dve.wait_ge(S["gc_done"], 1)
                gc = x[1][:, 0, 0:64].rearrange("p (t h) -> p t h", h=DNH)
                gt = x[2][:, 0, 0:64].rearrange("p (t h) -> p t h", h=DNH)
                step(nc.vector.tensor_copy(gcp, gc))
                step(nc.vector.tensor_scalar(neg_gc, gc, -1.0, None, ALU.mult))
                step(nc.vector.tensor_tensor(kd, gt, gcp, ALU.subtract))
                nc.vector.tensor_copy(beta, m.beta_all[:, 0:NT]).then_inc(S["gates_stepped"], 1)
                dve.wait_ge(S["act_gates"], 8)
                dve.wait_ge(S["gates_stepped"], 2)
                nc.vector.tensor_scalar(neg_egc, egc, -1.0, None, ALU.mult).then_inc(S["gates_ready"], 1)
                dve.wait_ge(S["gates_ready"], 1)

                def conv_taps(h, part, tap):
                    i = W_ORDER.index(part)
                    cw = 8 * WPOS[part] + h
                    n = 3 * h + i
                    if tap == 1:
                        dve.wait_ge(S["tap0"], n + 1)
                    else:
                        dve.wait_ge(S["tapped"], 2 * n + tap - 1)
                    ins = nc.vector.scalar_tensor_tensor(out=conv[:, 0:SEQ], in0=raw[:, tap:tap + SEQ],
                                                         scalar=m.conv_w[:, cw, tap:tap + 1], in1=conv[:, 0:SEQ],
                                                         op0=ALU.mult, op1=ALU.add)
                    if tap < 3:
                        ins.then_inc(S["tapped"], 1)
                        return
                    new = conv[:, SEQ:TOK]
                    step(nc.vector.tensor_scalar(new, raw[:, 3 + SEQ:3 + TOK], m.conv_w[:, cw, 3:4], None, ALU.mult))
                    for j in range(3):
                        ins = nc.vector.scalar_tensor_tensor(out=new, in0=m.conv_state[:, cw, :, j],
                                                             scalar=m.conv_w[:, cw, j:j + 1], in1=new,
                                                             op0=ALU.mult, op1=ALU.add)
                        if j < 2:
                            step(ins)
                    ins.then_inc(S["conv_done"], 1)

                def ssq_copy(h, part):
                    w = "kq".index(part)
                    dve.wait_ge(S["ssq_done"], 2 * h + w + 1)
                    if h:
                        dve.wait_ge(S["rs_ready"], 2 * (h - 1) + w + 1)
                    nc.vector.tensor_scalar(rs[:, w, 0, 0:NT], bankp[0][:, 0:NT], EPS, None, ALU.add)
                    nc.vector.tensor_scalar(rs[0:NB, w, 0, NT:NT + 1], bankp[0][0:NB, NT:NT + 1], EPS, None, ALU.add
                                            ).then_inc(S["evac_dve"], 1)

                def normalise(h, part):
                    w = "kq".index(part)
                    v = cm[:, h % 2, WPOS[part], :]
                    for j in range(G3):
                        dve.wait_ge(S["spread"], 6 * h + 3 * w + j + 1)
                        t = slice(512 * j, min(512 * j + 512, TOK))
                        n = t.stop - t.start
                        nc.vector.scalar_tensor_tensor(out=v[:, t], in0=v[:, t], scalar=(float(DK) ** -0.5 if w else 1.0),
                                                       in1=bankp[j][:, 0:n], op0=ALU.mult, op1=ALU.mult
                                                       ).then_inc(S["evac_dve"], 1)

                side = {(2, 0): lambda h: conv_taps(h, "k", 1), (2, 1): lambda h: conv_taps(h, "k", 2),
                        (2, 2): lambda h: conv_taps(h, "k", 3),
                        (4, 0): lambda h: (ssq_copy(h, "k"), conv_taps(h, "q", 1)), (4, 1): lambda h: conv_taps(h, "q", 2),
                        (4, 2): lambda h: conv_taps(h, "q", 3),
                        (6, 0): lambda h: normalise(h, "k"), (6, 1): lambda h: ssq_copy(h, "q"),
                        (7, 0): lambda h: conv_taps(h, "v", 1), (7, 1): lambda h: conv_taps(h, "v", 2),
                        (7, 2): lambda h: conv_taps(h, "v", 3)}

                def prepare(h):
                    if h:
                        dve.wait_ge(S["Us_ready"], 12 * h)
                    for u in range(2):
                        dve.wait_ge(S["KK_done"], 2 * h + u + 1)
                        dve.wait_ge(S["decay_ready"], 8 * h + 4 * (u + 1))
                        for c in range(4 * u, 4 * u + 4):
                            ins = nc.vector.scalar_tensor_tensor(out=U_[:, c, :], in0=x[2 + u][:, c - 4 * u, :],
                                                                 scalar=beta[:, c, h:h + 1], in1=decay[:, c, :],
                                                                 op0=ALU.mult, op1=ALU.mult)
                        ins.then_inc(S["U_ready"], 1)
                    for u in range(2):
                        dve.wait_ge(S["U_ready"], 2 * h + u + 1)
                        step(nc.vector.tensor_tensor(half(Tt, u), half(U_, u),
                                                     bcast(level[:, 0, :].unsqueeze(1), [P, 4, P]), ALU.mult))
                        nc.vector.tensor_tensor(half(Tt, u), bcast(m.ident.unsqueeze(1), [P, 4, P]), half(Tt, u),
                                                ALU.subtract).then_inc(S["Tt_ready"], 1)
                    if h:
                        keep_o(h - 1)
                    for u in range(2):
                        dve.wait_ge(S["QK_done"], 2 * h + u + 1)
                        nc.vector.tensor_tensor(half(aT, u), qk_bank[u], half(decay, u), ALU.mult
                                                ).then_inc(S["aT_ready"], 1)
                    for lev in range(6):
                        for u in range(2):
                            if lev < 5:
                                dve.wait_ge(S["TM_done"], 10 * h + 2 * lev + u + 1)
                                nc.vector.tensor_tensor(half(T, u), half(T, u), x[u], ALU.subtract
                                                        ).then_inc(S["T_updated"], 1)
                            dve.wait_ge(S["TMt_done"], 12 * h + 2 * lev + u + 1)
                            nc.vector.tensor_tensor(half(Tt, u), half(Tt, u), x[2 + u], ALU.subtract
                                                    ).then_inc(S["Tt_updated"], 1)

                def keep_o(h):
                    dve.wait_ge(S["evac_act"], 12 * (h + 1))
                    for u in range(2):
                        dve.wait_ge(S["o_turned"], 2 * h + u + 1)
                        nc.vector.scalar_tensor_tensor(
                            out=m.oBT[:, h, 512 * u:512 * u + 512], in0=x[u].rearrange("p c k -> p (c k)"),
                            scalar=m.dn_gain[:, 0:1], in1=cm[:, h % 2, 3, 512 * u:512 * u + 512],
                            op0=ALU.mult, op1=ALU.mult).then_inc(S["oT_ready"], 1)

                def keys_values(h):
                    for i in range(4):
                        u = i % 2
                        dve.wait_ge(S["kv_turned"], 4 * h + i + 1)
                        if i < 2:
                            ins = nc.vector.tensor_tensor(half(Kdec, u), kv_bank[i],
                                                          half(bcast(kd[:, :, h:h + 1], [P, NC, P]), u), ALU.mult)
                        else:
                            ins = nc.vector.tensor_copy(half(Vt, u), kv_bank[i])
                        ins.then_inc(S["kv_ready"], 1)

                def recur(h, c, point):
                    n = NC * h + c
                    state = S_[:, h % 2, :]
                    if point == 0:
                        dve.wait_ge(S["ks_done"], n + 1)
                        nc.vector.scalar_tensor_tensor(out=X, in0=x[0][:, 0, :], scalar=neg_egc[:, c, h:h + 1],
                                                       in1=Vt[:, c, :], op0=ALU.mult, op1=ALU.add
                                                       ).then_inc(S["X_ready"], 1)
                    elif point == 2:
                        dve.wait_ge(S["ds_done"], n + 1)
                        nc.vector.scalar_tensor_tensor(out=state, in0=state, scalar=egt[:, c, h:h + 1],
                                                       in1=x[3][:, 0, :], op0=ALU.mult, op1=ALU.add
                                                       ).then_inc(S["S_ready"], 1)
                        dve.wait_ge(S["o2_done"], n + 1)
                        dve.wait_ge(S["qs_scaled"], n + 1)
                        nc.vector.tensor_tensor(o_all[:, c, :], x[2][:, 0, :], qs, ALU.add).then_inc(S["o_added"], 1)

                for h in range(-1, DNH):
                    if h >= 0:
                        if h >= 2:
                            dve.wait_ge(S_stored[h % 2], 16 * (h // 2))
                        nc.vector.memset(S_[:, h % 2, :], 0.0).then_inc(S["S_zero"], 1)
                        dve.wait_ge(S["S_zero"], h + 1)
                    for c in range(NC):
                        for point in range(3):
                            if h >= 0:
                                recur(h, c, point)
                            if h + 1 < DNH and (c, point) in side:
                                side[(c, point)](h + 1)
                    if h + 1 < DNH:
                        normalise(h + 1, "q")
                    if h >= 0:
                        dve.wait_ge(S["o_squared"], h + 1)
                        nc.vector.tensor_reduce(st_o[:, 0, :], decay, AX.X, ALU.add).then_inc(S["o_summed"], 1)
                    if h + 1 < DNH:
                        keys_values(h + 1)
                    if h >= 0:
                        dve.wait_ge(S["o_rstd"], h + 1)
                        nc.vector.tensor_tensor(o_all, o_all, bcast(st_o[:, 2, :].unsqueeze(2), [P, NC, P]), ALU.mult
                                                ).then_inc(S["o_scaled"], 1)
                    if h + 1 < DNH:
                        prepare(h + 1)
                    else:
                        keep_o(h)

            @block.gpsimd
            def _(pool):
                step = Chain(pool, S["pool_step"])

                def tap0(h, part):
                    i = W_ORDER.index(part)
                    cw = 8 * WPOS[part] + h
                    n = 3 * h + i
                    pool.wait_ge(S["evac_act"], 12 * h + 3 * i + 3)
                    if n:
                        pool.wait_ge(S["silu_done"], n)
                    nc.gpsimd.tensor_scalar(conv[:, 0:SEQ], raw[:, 0:SEQ], m.conv_w[:, cw, 0:1], None, ALU.mult
                                            ).then_inc(S["tap0"], 1)
                    nc.gpsimd.tensor_copy(m.tails[:, cw, :], raw[:, SEQ:SEQ + 11]).then_inc(S["tails_kept"], 1)

                def rsqrt(h, part):
                    w = "kq".index(part)
                    pool.wait_ge(S["evac_dve"], 8 * h + (5 if w else 1))
                    if h:
                        pool.wait_ge(S["spread"], 6 * (h - 1) + 3 * w + 3)
                    nc.gpsimd.tensor_tensor(rs[:, w, 1], rs[:, w, 0], m.minus_half[:, 0:NT + 1], ALU.pow
                                            ).then_inc(S["rs_ready"], 1)

                step(nc.gpsimd.memset(level, 0.0))
                for lev, s in enumerate((1, 2, 4, 8, 16, 32, 64)):
                    view = level[:, lev, :].rearrange("p (b x r) -> p b x r", x=2, r=s)[:, :, 1, :]
                    step(nc.gpsimd.memset(view, 1.0))
                    step(nc.gpsimd.affine_select(out=view, in_=view, compare_op=ALU.is_ge, fill=0.0, base=0,
                                                 pattern=[[-2 * s, P // (2 * s)], [0, s]], channel_multiplier=1))
                    step(nc.gpsimd.affine_select(out=view, in_=view, compare_op=ALU.is_ge, fill=0.0, base=s - 1,
                                                 pattern=[[2 * s, P // (2 * s)], [0, s]], channel_multiplier=-1))

                for h in range(-1, DNH):
                    if h + 1 < DNH:
                        g = h + 1
                        tap0(g, "k")
                        tap0(g, "q")
                        rsqrt(g, "k")
                        tap0(g, "v")
                        rsqrt(g, "q")
                    if h >= 0:
                        pool.wait_ge(S["o_summed"], h + 1)
                        step(nc.gpsimd.tensor_scalar(st_o[:, 1, :], st_o[:, 0, :], 1.0 / DK, EPS, ALU.mult, ALU.add))
                        nc.gpsimd.tensor_tensor(st_o[:, 2, :], st_o[:, 1, :], m.minus_half[:, 0:NC], ALU.pow
                                                ).then_inc(S["o_rstd"], 1)
                    if h + 1 < DNH:
                        g = h + 1
                        pool.wait_ge(S["evac_dve"], 8 * g + 8)
                        pool.wait_ge(S["silu_done"], 3 * g + 3)
                        pool.wait_ge(S["evac_act"], 12 * g + 12)
                        step(nc.gpsimd.tensor_copy(m.dn_s[:, :, g, :], cm[:, g % 2, :, SEQ:TOK]))
                        for lev in range(6):
                            for u in range(2):
                                n = 12 * g + 2 * lev + u
                                if lev == 0:
                                    pool.wait_ge(S["U_ready"], 2 * g + u + 1)
                                if n >= 2:
                                    pool.wait_ge(S["M_done"], n - 1)
                                nc.gpsimd.tensor_tensor(half(Us, u), half(U_, u),
                                                        bcast(level[:, 1 + lev, :].unsqueeze(1), [P, 4, P]),
                                                        ALU.mult).then_inc(S["Us_ready"], 1)


def stage_decode_deltanet(nc, m):
    HB = DNH * NB
    with ExitStack() as ctx:
        def sb(name, shape, dt=F32):
            return ctx.enter_context(nc.sbuf_tensor("dd_" + name, shape, dt))[:]

        def ps(name, shape):
            return ctx.enter_context(nc.psum_tensor("dd_" + name, shape, F32))[:]

        state = [m.ring[:, j, :].rearrange("p (b h v) -> p b h v", b=4, h=DNH) for j in SLOTS_S]
        diag = sb("diag", [NB, 2, DNH, NB])
        beta, eg, qk, vnew, o, o2, rstd, junk = (sb(x, [P, DNH, NB]) for x in
                                                 ("beta", "eg", "qk", "vnew", "o", "o2", "rstd", "junk"))
        qkprod = sb("qkprod", [P, DNH, NB])
        outer = sb("outer", [P, 2, 4, DK])
        tail_rows = sb("tail_rows", [11, 24 * P])
        small = ps("small", [P, 512])
        products = ps("products", [P, 512])[:, 0:2 * HB].rearrange("p (h b w) -> p h b w", h=DNH, b=NB)
        spread = ps("spread", [P, 2, 4, DK])
        tails = ps("tails", [P, 4, 512])[0:11]
        S = semaphores(nc, m, "dd", "diag_ready gates_spread eg_ready step qk_spread multiplied vnew_ready v_spread "
                       "outer_ready S_ready squares_summed mean_ready rstd_ready tails_turned tails_copied")
        q, k, v, z = (m.dn_s[:, w] for w in range(4))
        pairs = [(b, h) for b in range(NB) for h in range(DNH)]

        with nc.Block() as block:
            @block.sync
            def _(sp):
                for c in (("ga", 0), ("ga", 1), ("gb", 0), ("gb", 1)):
                    load_chunk(sp, m, m.plan.index(c))
                sp.wait_ge(S["tails_copied"], 6)
                sp.dma_start(m.p_conv, tail_rows[0:3]).then_inc(m.outputs_stored, 16)
                sp.dma_start(m.s_conv[:, 2, :], tail_rows[3:11]).then_inc(m.outputs_stored, 16)
                m.n_outputs += 2
                sp.wait_ge(m.outputs_stored, 16 * m.n_outputs)
                for i in range(2):
                    sp.wait_ge(S["S_ready"], 32 * (i + 1))
                    sp.dma_start(m.s_S[4 * i:4 * i + 4].rearrange("b h k v -> k (b h) v"),
                                 state[i].rearrange("p b h v -> p (b h) v")).then_inc(m.outputs_stored, 16)
                m.n_outputs += 2

            @block.tensor
            def _(pe):
                pe.wait_ge(S["diag_ready"], 3)
                nc.tensor.matmul(small[:, 0:2 * HB], m.ones[0:NB, :], diag.rearrange("p w h b -> p (w h b)"),
                                 start=True, stop=True)
                nc.tensor.matmul(small[:, 2 * HB:3 * HB], m.ones, qkprod.rearrange("p h b -> p (h b)"),
                                 start=True, stop=True).then_inc(S["gates_spread"], 1)
                for j in range(6):
                    if j >= 4:
                        pe.wait_ge(S["tails_copied"], j - 3)
                    for c in range(4):
                        mm = nc.tensor.transpose(tails[:, j % 4, c * P:(c + 1) * P], m.tails[:, 4 * j + c, :], m.ident)
                    mm.then_inc(S["tails_turned"], 1)
                for n, (b, h) in enumerate(pairs):
                    if n % 32 == 0:
                        pe.wait_ge(m.S_landed[n // 32], 16)
                    mm = nc.tensor.matmul(products[:, h, b, :], state[b // 4][:, b % 4, h, :], m.dn_s[:, 0:2, h, b],
                                          start=True, stop=True)
                mm.then_inc(S["multiplied"], 1)
                pe.wait_ge(S["vnew_ready"], 1)
                for j in range(16):
                    if j >= 2:
                        pe.wait_ge(S["outer_ready"], 4 * (j - 1))
                    for c in range(4):
                        b, h = pairs[4 * j + c]
                        mm = nc.tensor.matmul(spread[:, j % 2, c, :], bcast(vnew[:, h, b:b + 1], [P, P]), m.ident,
                                              start=True, stop=True)
                    mm.then_inc(S["v_spread"], 1)
                    if j == 0:
                        pe.wait_ge(S["vnew_ready"], 2)
                        nc.tensor.matmul(small[:, 3 * HB:4 * HB], m.ones, o2.rearrange("p h b -> p (h b)"),
                                         start=True, stop=True).then_inc(S["squares_summed"], 1)

            @block.vector
            def _(dve):
                step = Chain(dve, S["step"])
                for w, src in enumerate((m.beta_all, m.g_all)):
                    nc.vector.tensor_tensor(diag[:, w], bcast(src[0:NB, NT, :].unsqueeze(2), [NB, DNH, NB]),
                                            bcast(m.ident[0:NB, 0:NB].unsqueeze(1), [NB, DNH, NB]), ALU.mult
                                            ).then_inc(S["diag_ready"], 1)
                nc.vector.tensor_tensor(qkprod, q, k, ALU.mult).then_inc(S["diag_ready"], 1)
                dve.wait_ge(S["eg_ready"], 1)

                def at(i):
                    return small[:, i * HB:(i + 1) * HB].rearrange("p (h b) -> p h b", h=DNH)

                step(nc.vector.tensor_copy(beta, at(0)))
                step(nc.vector.tensor_copy(qk, at(2)))
                dve.wait_ge(S["multiplied"], 1)
                step(nc.vector.tensor_tensor(junk, eg, products[:, :, :, 1], ALU.mult))
                step(nc.vector.tensor_tensor(junk, v, junk, ALU.subtract))
                nc.vector.tensor_tensor(vnew, beta, junk, ALU.mult).then_inc(S["vnew_ready"], 1)
                step(nc.vector.tensor_tensor(o, eg, products[:, :, :, 0], ALU.mult))
                dve.wait_ge(S["vnew_ready"], 1)
                step(nc.vector.tensor_tensor(junk, qk, vnew, ALU.mult))
                step(nc.vector.tensor_tensor(o, o, junk, ALU.add))
                nc.vector.tensor_tensor(o2, o, o, ALU.mult).then_inc(S["vnew_ready"], 1)
                step(nc.vector.tensor_tensor(o, o, z, ALU.mult))
                step(nc.vector.tensor_scalar(o, o, m.dn_gain[:, 0:1], None, ALU.mult))
                dve.wait_ge(S["squares_summed"], 1)
                nc.vector.tensor_scalar(junk, at(3), 1.0 / DK, EPS, ALU.mult, ALU.add).then_inc(S["mean_ready"], 1)
                for n, (b, h) in enumerate(pairs):
                    dve.wait_ge(S["outer_ready"], n + 1)
                    s = state[b // 4][:, b % 4, h, :]
                    nc.vector.scalar_tensor_tensor(s, s, eg[:, h, b:b + 1], outer[:, n // 4 % 2, n % 4, :], ALU.mult,
                                                   ALU.add).then_inc(S["S_ready"], 1)
                dve.wait_ge(S["rstd_ready"], 1)
                step(nc.vector.tensor_tensor(m.oBT[:, :, SEQ:TOK], o, rstd, ALU.mult))

            @block.gpsimd
            def _(pool):
                pool.wait_ge(S["mean_ready"], 1)
                nc.gpsimd.tensor_tensor(rstd, junk, m.minus_half[:, 0:HB].rearrange("p (h b) -> p h b", h=DNH), ALU.pow
                                        ).then_inc(S["rstd_ready"], 1)

            @block.scalar
            def _(act):
                act.wait_ge(S["gates_spread"], 1)
                nc.scalar.activation(eg.rearrange("p h b -> p (h b)"), small[:, HB:2 * HB], ACT.Exp
                                     ).then_inc(S["eg_ready"], 1)
                for j in range(6):
                    act.wait_ge(S["tails_turned"], j + 1)
                    nc.scalar.activation(tail_rows[:, 512 * j:512 * (j + 1)], tails[:, j % 4, :], ACT.Copy
                                         ).then_inc(S["tails_copied"], 1)
                for n, (b, h) in enumerate(pairs):
                    j, c = divmod(n, 4)
                    if c == 0:
                        act.wait_ge(S["v_spread"], j + 1)
                        if j >= 2:
                            act.wait_ge(S["S_ready"], 4 * (j - 1))
                    nc.scalar.activation(outer[:, j % 2, c, :], spread[:, j % 2, c, :], ACT.Copy, scale=k[:, h, b:b + 1]
                                         ).then_inc(S["outer_ready"], 1)


TILES = [(t, P) for t in range(NT)] + [(NT, NB)]


def stage_mix(nc, m):
    with ExitStack() as ctx:
        def sb(name, shape, dt=F32):
            return ctx.enter_context(nc.sbuf_tensor("mx_" + name, shape, dt))[:]

        o_in = sb("o_in", [P, NG, OROW])
        lse, weight = (sb(x, [P, NG, NH]) for x in ("lse", "weight"))
        top, total = (sb(x, [P, NH]) for x in ("top", "total"))
        oAT = sb("oAT", [P, 4, P])
        gates = sb("gates", [P, 2, 512])
        mixed = sb("mixed", [P, 2, 512])
        part = sb("part", [P, 512])
        w_a = sb("w_a", [P, 4, D])
        prod = ctx.enter_context(nc.psum_tensor("mx_prod", [P, 6, 512], F32))[:]
        oA_ps = ctx.enter_context(nc.psum_tensor("mx_oA", [P, 4, P], F32))[:]
        mix_ps = ctx.enter_context(nc.psum_tensor("mx_mix", [P, 4, P], F32))[:]
        S = semaphores(nc, m, "mx", "w_a_landed ln_done lse_ready exp_done merge_step oA_ready oA_turned oAT_ready "
                       "product_done gate_ready y_used mix_ready mix_turned mixT_ready zeros_ready y_cleared")
        zeros = m.tails.rearrange("p c r -> p (c r)")[:, 0:256]
        y_cleared = m.y_scr.rearrange("(p f r) (c n) -> p f (r c) n", p=P, r=4, n=256)
        fills = y_cleared.shape[1]
        o_landed = semaphore(nc, m, "mx_o_landed")
        items = [("ga", 0), ("gb", 0), ("ya", 0), ("yb", 0), ("ga", 1), ("gb", 1), ("ya", 1), ("yb", 1)]

        def gates_upto(n):
            return 4 * (n // 8) + (1, 2, 2, 2, 3, 4, 4, 4)[n % 8]

        def ys_upto(n):
            return 4 * (n // 8) + (0, 0, 1, 2, 2, 2, 3, 4)[n % 8]

        with nc.Block() as block:
            @block.sync
            def _(sp):
                sp.dma_start(o_in, m.o_scr[0:P]).then_inc(o_landed, 16)
                sp.dma_start(w_a, m.w_out_a.rearrange("(k p) n -> p k n", p=P)).then_inc(S["w_a_landed"], 16)
                sp.wait_ge(m.outputs_stored, 16 * m.n_outputs)
                for c in (("wb", 0), ("wb", 1)):
                    load_chunk(sp, m, m.plan.index(c))
                for t, r in TILES[1:]:
                    sp.wait_ge(S["oA_ready"], t)
                    sp.wait_ge(S["oA_turned"], t)
                    src = m.o_scr[t * P:(t + 1) * P] if t < NT else m.o_s_scr
                    sp.dma_start(o_in[0:r], src).then_inc(o_landed, 16)
                    if t == 1:
                        sp.wait_ge(S["zeros_ready"], 1)
                    for i in range(fills * (t - 1) // NT, fills * t // NT):
                        sp.dma_start(y_cleared[:, i], bcast(zeros.unsqueeze(1), [P, 16, 256])).then_inc(S["y_cleared"], 16)
                for half in range(2):
                    sp.wait_ge(S["product_done"], 8 * NT + half + 1)
                    load_chunk(sp, m, m.plan.index(("wo", half)))
                sp.wait_ge(S["y_cleared"], 16 * fills)

            @block.gpsimd
            def _(pool):
                nc.gpsimd.memset(zeros, 0.0).then_inc(S["zeros_ready"], 1)

            @block.tensor
            def _(pe):
                def mix_turn(t, half):
                    r = TILES[t][1]
                    pe.wait_ge(S["mix_ready"], 2 * t + half + 1)
                    if 2 * t + half:
                        pe.wait_ge(S["mixT_ready"], 2 * t + half)
                    for c in range(4):
                        mm = nc.tensor.transpose(mix_ps[:, c, 0:r], mixed[0:r, half, c * P:(c + 1) * P],
                                                 m.ident[0:r, 0:r])
                    mm.then_inc(S["mix_turned"], 1)

                for t, r in TILES:
                    for i, (kind, half) in enumerate(items):
                        n = 8 * t + i
                        if t >= 1 and i in (1, 2):
                            mix_turn(t - 1, i - 1)
                        if i == 2:
                            pe.wait_ge(S["oA_ready"], t + 1)
                            if t >= 1:
                                pe.wait_ge(S["oAT_ready"], t)
                            for c in range(4):
                                mm = nc.tensor.transpose(oA_ps[:, c, 0:r], o_in[0:r, 0, c * P:(c + 1) * P],
                                                         m.ident[0:r, 0:r])
                            mm.then_inc(S["oA_turned"], 1)
                            pe.wait_ge(S["oAT_ready"], t + 1)
                        if n >= 6:
                            last = n - 6
                            if items[last % 8][0][0] == "g":
                                pe.wait_ge(S["gate_ready"], gates_upto(last))
                            else:
                                pe.wait_ge(S["y_used"], ys_upto(last))
                        out = prod[0:r, n % 6, :]
                        if kind == "ya":
                            if n == 2:
                                pe.wait_ge(S["w_a_landed"], 16)
                            for k in range(4):
                                mm = nc.tensor.matmul(out, oAT[:, k, 0:r], w_a[:, k, half * 512:(half + 1) * 512],
                                                      start=(k == 0), stop=(k == 3))
                        else:
                            w = chunk(pe, m, "wb" if kind == "yb" else kind, half).rearrange("p (k n) -> p k n", k=KD)
                            src = m.oBT if kind == "yb" else m.hT
                            for k in range(KD):
                                mm = nc.tensor.matmul(out, src[:, k, t * P:t * P + r], w[:, k, :],
                                                      start=(k == 0), stop=(k == KD - 1))
                        mm.then_inc(S["product_done"], 1)
                mix_turn(NT, 0)
                mix_turn(NT, 1)

            @block.scalar
            def _(act):
                for t, r in TILES:
                    den = o_in[0:r, :, HW + NH:OROW]
                    act.wait_ge(o_landed, 16 * (t + 1))
                    nc.scalar.activation(lse[0:r], den, ACT.Ln).then_inc(S["ln_done"], 1)
                    act.wait_ge(S["lse_ready"], t + 1)
                    nc.scalar.activation(lse[0:r], lse[0:r], ACT.Exp).then_inc(S["exp_done"], 1)
                    act.wait_ge(S["oA_turned"], t + 1)
                    nc.scalar.activation(oAT[:, :, 0:r], oA_ps[:, :, 0:r], ACT.Copy).then_inc(S["oAT_ready"], 1)
                    for half in range(2):
                        for w in range(2):
                            g = 4 * t + 2 * half + w
                            act.wait_ge(S["product_done"], 8 * t + 4 * half + w + 1)
                            if g >= 2:
                                act.wait_ge(S["y_used"], g - 1)
                            nc.scalar.activation(gates[0:r, w], prod[0:r, (8 * t + 4 * half + w) % 6], ACT.Sigmoid
                                                 ).then_inc(S["gate_ready"], 1)

            @block.vector
            def _(dve):
                step = Chain(dve, S["merge_step"])

                def merge(t, r):
                    den = o_in[0:r, :, HW + NH:OROW]
                    l, w, tp, s = lse[0:r], weight[0:r], top[0:r], total[0:r]
                    dve.wait_ge(S["ln_done"], t + 1)
                    step(nc.vector.tensor_tensor(l, l, o_in[0:r, :, HW:HW + NH], ALU.subtract))
                    step(nc.vector.tensor_reduce(tp, l.rearrange("p g h -> p h g"), AX.X, ALU.max))
                    nc.vector.tensor_tensor(l, l, bcast(tp.unsqueeze(1), [r, NG, NH]), ALU.subtract
                                            ).then_inc(S["lse_ready"], 1)
                    dve.wait_ge(S["exp_done"], t + 1)
                    step(nc.vector.tensor_reduce(s, l.rearrange("p g h -> p h g"), AX.X, ALU.add))
                    step(nc.vector.tensor_tensor(w, den, bcast(s.unsqueeze(1), [r, NG, NH]), ALU.mult))
                    step(nc.vector.reciprocal(w, w))
                    step(nc.vector.tensor_tensor(w, w, l, ALU.mult))
                    o = o_in[0:r, :, 0:HW]
                    for g in range(NG):
                        og = o[:, g, :].rearrange("p (h e) -> p h e", h=NH)
                        step(nc.vector.tensor_tensor(og, og, bcast(w[:, g, :].unsqueeze(2), [r, NH, E]), ALU.mult))
                    step(nc.vector.tensor_tensor(o[:, 0], o[:, 0], o[:, 1], ALU.add))
                    nc.vector.tensor_tensor(o[:, 0], o[:, 0], o[:, 2], ALU.add).then_inc(S["oA_ready"], 1)

                def turn_copy(t, r):
                    for half in range(2):
                        dve.wait_ge(S["mix_turned"], 2 * t + half + 1)
                        nc.vector.tensor_copy(m.hT[:, 4 * half:4 * half + 4, t * P:t * P + r], mix_ps[:, :, 0:r]
                                              ).then_inc(S["mixT_ready"], 1)

                for t, r in TILES:
                    merge(t, r)
                    if t >= 1:
                        turn_copy(t - 1, P)
                    for half in range(2):
                        n = 8 * t + 4 * half
                        dve.wait_ge(S["product_done"], n + 3)
                        dve.wait_ge(S["gate_ready"], 4 * t + 2 * half + 1)
                        if t >= 1:
                            dve.wait_ge(S["mix_turned"], 2 * (t - 1) + half + 1)
                        nc.vector.tensor_tensor(mixed[0:r, half], prod[0:r, (n + 2) % 6], gates[0:r, 0], ALU.mult
                                                ).then_inc(S["y_used"], 1)
                        dve.wait_ge(S["product_done"], n + 4)
                        dve.wait_ge(S["gate_ready"], 4 * t + 2 * half + 2)
                        nc.vector.tensor_tensor(part[0:r], prod[0:r, (n + 3) % 6], gates[0:r, 1], ALU.mult
                                                ).then_inc(S["y_used"], 1)
                        dve.wait_ge(S["y_used"], 4 * t + 2 * half + 2)
                        nc.vector.tensor_tensor(mixed[0:r, half], mixed[0:r, half], part[0:r], ALU.add
                                                ).then_inc(S["mix_ready"], 1)
                        dve.wait_ge(S["mix_ready"], 2 * t + half + 1)
                turn_copy(NT, NB)


def stage_residual(nc, m):
    with ExitStack() as ctx:
        def sb(name, shape, dt=F32):
            return ctx.enter_context(nc.sbuf_tensor("rs_" + name, shape, dt))[:]

        xs, hs = (sb(x, [P, 2, D]) for x in ("xs", "hs"))
        junk = sb("junk", [P, D])
        stat = sb("stat", [P, 2, 3])
        turned = sb("turned", [P, KD, P])
        x1_ps = ctx.enter_context(nc.psum_tensor("rs_x1", [P, 2, 2, 512], F32))[:]
        h_ps = ctx.enter_context(nc.psum_tensor("rs_h", [P, KD, P], F32))[:]
        l_ps = ctx.enter_context(nc.psum_tensor("rs_l", [P, 2, 512], F32))[:]
        S = semaphores(nc, m, "rs", "x1_done x1_ready squared mean_ready rstd_ready h_ready h_turned hT_ready "
                       "logits_done logits_ready zeroed")
        x_landed = [semaphore(nc, m, f"rs_x_landed{i}") for i in range(2)]
        h_stored = [semaphore(nc, m, f"rs_h_stored{i}") for i in range(2)]

        with nc.Block() as block:
            @block.sync
            def _(sp):
                def load(t, r):
                    if t >= 2:
                        sp.wait_ge(S["x1_ready"], 2 * (t - 1))
                    src = m.x_prompt[t * P:(t + 1) * P, :] if t < NT else m.x_sample
                    sp.dma_start(xs[0:r, t % 2, :], src).then_inc(x_landed[t % 2], 16)

                load(*TILES[0])
                for t, r in TILES:
                    if t < NT:
                        load(*TILES[t + 1])
                    sp.wait_ge(S["h_ready"], t + 1)
                    sp.dma_start(m.h2_scr[t * P:t * P + r, :], hs[0:r, t % 2, :]).then_inc(h_stored[t % 2], 16)
                sp.wait_ge(h_stored[0], 16 * 5)
                sp.wait_ge(h_stored[1], 16 * 4)

            @block.tensor
            def _(pe):
                def turn(t, r):
                    pe.wait_ge(S["h_ready"], t + 1)
                    if t >= 1:
                        pe.wait_ge(S["hT_ready"], t)
                    for k in range(KD):
                        mm = nc.tensor.transpose(h_ps[:, k, 0:r], hs[0:r, t % 2, k::KD], m.ident[0:r, 0:r])
                    mm.then_inc(S["h_turned"], 1)

                def route(t, r):
                    pe.wait_ge(S["hT_ready"], t + 1)
                    if t >= 2:
                        pe.wait_ge(S["logits_ready"], t - 1)
                    for k in range(KD):
                        mm = nc.tensor.matmul(l_ps[0:r, t % 2, 0:36], turned[:, k, 0:r], m.w_router[:, k, :],
                                              start=(k == 0), stop=(k == KD - 1))
                    mm.then_inc(S["logits_done"], 1)

                for t, r in TILES:
                    for half in range(2):
                        w = chunk(pe, m, "wo", half).rearrange("p (k n) -> p k n", k=KD)
                        if t >= 2:
                            pe.wait_ge(S["x1_ready"], 2 * (t - 2) + half + 1)
                        for k in range(KD):
                            mm = nc.tensor.matmul(x1_ps[0:r, t % 2, half, :], m.hT[:, k, t * P:t * P + r], w[:, k, :],
                                                  start=(k == 0), stop=(k == KD - 1))
                        mm.then_inc(S["x1_done"], 1)
                        if t >= 1:
                            (turn, route)[half](*TILES[t - 1])
                turn(*TILES[NT])
                route(*TILES[NT])

            @block.vector
            def _(dve):
                def copy_hT(t, r):
                    dve.wait_ge(S["h_turned"], t + 1)
                    if t >= 1:
                        dve.wait_ge(S["logits_done"], t)
                    nc.vector.tensor_tensor(turned[:, :, 0:r], h_ps[:, :, 0:r], bcast(m.ln2.unsqueeze(2), [P, KD, r]),
                                            ALU.mult).then_inc(S["hT_ready"], 1)

                def keep_logits(t, r):
                    dve.wait_ge(S["logits_done"], t + 1)
                    nc.vector.tensor_tensor(m.logits[0:r, t, :], l_ps[0:r, t % 2, 0:36], m.b_router[0:r], ALU.add
                                            ).then_inc(S["logits_ready"], 1)

                nc.vector.memset(m.logits, 0.0).then_inc(S["zeroed"], 1)
                dve.wait_ge(S["zeroed"], 1)
                for t, r in TILES:
                    x1 = m.x1[t]
                    if t >= 1:
                        copy_hT(*TILES[t - 1])
                    for half in range(2):
                        c = slice(512 * half, 512 * half + 512)
                        dve.wait_ge(S["x1_done"], 2 * t + half + 1)
                        dve.wait_ge(x_landed[t % 2], 16 * (t // 2 + 1))
                        nc.vector.tensor_tensor(x1[0:r, c], x1_ps[0:r, t % 2, half, :], xs[0:r, t % 2, c], ALU.add
                                                ).then_inc(S["x1_ready"], 1)
                    dve.wait_ge(S["rstd_ready"], t + 1)
                    if t >= 2:
                        dve.wait_ge(S["h_turned"], t - 1)
                        dve.wait_ge(h_stored[t % 2], 16 * (t // 2))
                    nc.vector.tensor_scalar(hs[0:r, t % 2], x1[0:r], stat[0:r, t % 2, 2:3], None, ALU.mult
                                            ).then_inc(S["h_ready"], 1)
                    if t >= 1:
                        keep_logits(*TILES[t - 1])
                copy_hT(*TILES[NT])
                keep_logits(*TILES[NT])

            @block.scalar
            def _(act):
                for t, r in TILES:
                    act.wait_ge(S["x1_ready"], 2 * t + 2)
                    if t >= 2:
                        act.wait_ge(S["mean_ready"], t - 1)
                    if t >= 1:
                        act.wait_ge(S["squared"], t)
                    nc.scalar.activation(junk[0:r], m.x1[t][0:r], ACT.Square, accum_out=stat[0:r, t % 2, 0:1]
                                         ).then_inc(S["squared"], 1)

            @block.gpsimd
            def _(pool):
                for t, r in TILES:
                    s = stat[0:r, t % 2]
                    pool.wait_ge(S["squared"], t + 1)
                    nc.gpsimd.tensor_scalar(s[:, 1:2], s[:, 0:1], 1.0 / D, EPS, ALU.mult, ALU.add
                                            ).then_inc(S["mean_ready"], 1)
                    pool.wait_ge(S["mean_ready"], t + 1)
                    if t >= 2:
                        pool.wait_ge(S["h_ready"], t - 1)
                    nc.gpsimd.tensor_tensor(s[:, 2:3], s[:, 1:2], m.minus_half[0:r, 0:1], ALU.pow
                                            ).then_inc(S["rstd_ready"], 1)


CE = mybir.EngineType


def load_expert(sp, m, w, e, p):
    src = (m.w_e_gate, m.w_e_up, m.w_e_down)[w][bass.ds(e, 1)].rearrange("a (p k) n -> (a p) (k n)", p=P)
    sp.dma_start(m.ring[:, 3 * p + w, :], src).then_inc(m.expert_landed[w][p], 16)


def stage_route(nc, m):
    T = NT + 1
    with ExitStack() as ctx:
        def sb(name, shape, dt=F32):
            return ctx.enter_context(nc.sbuf_tensor("rt_" + name, shape, dt))[:]

        count_i = sb("count_i", [P, P], I32)
        count_f, by128, by2, keys = (sb(x, [P, P]) for x in ("count_f", "by128", "by2", "keys"))
        token_i = sb("token_i", [P, T], I32)
        token = sb("token", [P, T])
        valid = sb("valid", [P, T])
        upto_mask = sb("upto_mask", [P, NE, NE])
        work = m.ring[:, 5, :]
        in_block = work[:, 0:2 * T * P].rearrange("p (a r) -> p a r", r=P)
        of_block = work[:, 2 * T * P:2 * T * (P + MAXB)].rearrange("p (a b) -> p a b", b=MAXB)
        top = sb("top", [P, 4, T])
        group = sb("group", [P, T, NGE])
        shifted = sb("shifted", [P, T, NGE])
        pick = sb("pick", [P, T, NGE, EPG])
        le = sb("le", [P, T, EPG])
        le2 = sb("le2", [P, T, EPG])
        one = [sb(f"one{i}", [P, T, EPG]) for i in range(2)]
        value = [sb(f"value{i}", [P, T]) for i in range(2)]
        hot = [sb(f"hot{i}", [P, T, NE]) for i in range(2)]
        both = sb("both", [P, T, NE])
        e2, s2, pg = (sb(x, [P, T]) for x in ("e2", "s2", "pg"))
        blocks, ends, start = (sb(x, [P, NE]) for x in ("blocks", "ends", "start"))
        before = sb("before", [P, T + 1, NE])
        over = sb("over", [P, NE, 9])
        ends_by = sb("ends_by", [P, NE, NE])
        row = sb("row", [P, T, NE])
        dest = sb("dest", [P, 2, T])
        owner = sb("owner", [P, MAXB])
        owner_by = sb("owner_by", [P, MAXB, NE])
        pairs_by = sb("pairs_by", [P, 25])
        pairs = sb("pairs", [P, 1])
        dest_i = sb("dest_i", [P, 2 * T], I32)
        offset, block_of = (sb(x, [P, 2 * T]) for x in ("offset", "block_of"))
        ranks = ctx.enter_context(nc.psum_tensor("rt_ranks", [P, 512], F32))[:, 0:T * NE].rearrange(
            "p (t e) -> p t e", t=T)
        counts = ctx.enter_context(nc.psum_tensor("rt_counts", [P, 512], F32))[:, 0:T * NE].rearrange(
            "p (t e) -> p t e", t=T)
        tokens = ctx.enter_context(nc.psum_tensor("rt_tokens", [P, 512], F32))[:, 0:MAXB]
        S = semaphores(nc, m, "rt", "iotas step exp_done shifted second_ready pool_step consts hots_ready ranked "
                       "owners_ready one_hots_ready tokens_placed")
        lg = m.logits[:, :, 0:4]
        le_all = m.logits[:, :, 4:36].rearrange("p t (g e) -> p t g e", g=NGE)

        with nc.Block() as block:
            @block.sync
            def _(sp):
                sp.wait_ge(S["owners_ready"], 1)
                first = nc.values_load(m.block_expert[0:1, 0:1], engines=(CE.SP,), min_val=0, max_val=NE - 1)
                load_expert(sp, m, 0, first, 0)
                load_expert(sp, m, 1, first, 0)

            @block.gpsimd
            def _(pool):
                step = Chain(pool, S["pool_step"])
                nc.gpsimd.iota(count_i, pattern=[[1, P]], base=0, channel_multiplier=0).then_inc(S["iotas"], 1)
                nc.gpsimd.iota(token_i, pattern=[[P, T]], base=0, channel_multiplier=1).then_inc(S["iotas"], 1)
                step(nc.gpsimd.memset(valid, 1.0))
                step(nc.gpsimd.affine_select(out=valid[:, NT:T], in_=valid[:, NT:T], compare_op=ALU.is_ge, fill=0.0,
                                             base=NB - 1, pattern=[[0, 1]], channel_multiplier=-1))
                step(nc.gpsimd.memset(upto_mask, 1.0))
                nc.gpsimd.affine_select(out=upto_mask, in_=upto_mask, compare_op=ALU.is_ge, fill=0.0, base=0,
                                        pattern=[[1, NE], [-1, NE]], channel_multiplier=0).then_inc(S["consts"], 1)

            @block.scalar
            def _(act):
                act.wait_ge(S["shifted"], 1)
                nc.scalar.activation(shifted, shifted, ACT.Exp).then_inc(S["exp_done"], 1)
                act.wait_ge(S["second_ready"], 1)
                nc.scalar.activation(e2, e2, ACT.Exp).then_inc(S["exp_done"], 1)

            @block.tensor
            def _(pe):
                pe.wait_ge(S["hots_ready"], 1)
                nc.tensor.matmul(ranks.rearrange("p t e -> p (t e)"), m.triu, both.rearrange("p t e -> p (t e)"),
                                 start=True, stop=True)
                nc.tensor.matmul(counts.rearrange("p t e -> p (t e)"), m.ones, both.rearrange("p t e -> p (t e)"),
                                 start=True, stop=True).then_inc(S["ranked"], 1)
                pe.wait_ge(S["one_hots_ready"], 1)
                for a in range(2 * T):
                    mm = nc.tensor.matmul(tokens, in_block[:, a, :], of_block[:, a, :], start=(a == 0),
                                          stop=(a == 2 * T - 1))
                mm.then_inc(S["tokens_placed"], 1)

            @block.vector
            def _(dve):
                step = Chain(dve, S["step"])

                def first_hot(out, x, n, key):
                    step(nc.vector.tensor_reduce(top[:, key], x, AX.X, ALU.max))
                    step(nc.vector.tensor_tensor(out, x, bcast(top[:, key].unsqueeze(2), [P, T, n]), ALU.is_equal))
                    step(nc.vector.tensor_tensor(out, out, bcast(keys[:, 0:n].unsqueeze(1), [P, T, n]), ALU.mult))
                    step(nc.vector.tensor_reduce(top[:, 3], out, AX.X, ALU.max))
                    step(nc.vector.tensor_tensor(out, out, bcast(top[:, 3].unsqueeze(2), [P, T, n]), ALU.is_equal))

                dve.wait_ge(S["iotas"], 2)
                step(nc.vector.tensor_copy(count_f, count_i))
                step(nc.vector.tensor_copy(token, token_i))
                step(nc.vector.tensor_scalar(by128, count_f, float(P), None, ALU.mult))
                step(nc.vector.tensor_scalar(by2, count_f, 2.0, None, ALU.mult))
                step(nc.vector.tensor_scalar(keys, count_f, -1.0, 64.0, ALU.mult, ALU.add))
                first_hot(group, lg, NGE, 0)
                nc.vector.tensor_tensor(shifted, lg, bcast(top[:, 0].unsqueeze(2), [P, T, NGE]), ALU.subtract
                                        ).then_inc(S["shifted"], 1)
                step(nc.vector.tensor_tensor(pick, le_all, bcast(group.unsqueeze(3), [P, T, NGE, EPG]), ALU.mult))
                step(nc.vector.tensor_reduce(le, pick.rearrange("p t g e -> p t e g"), AX.X, ALU.add))
                first_hot(one[0], le, EPG, 1)
                step(nc.vector.tensor_scalar(le2, one[0], NEG, None, ALU.mult))
                step(nc.vector.tensor_tensor(le2, le2, le, ALU.add))
                first_hot(one[1], le2, EPG, 2)
                nc.vector.tensor_tensor(e2, top[:, 2], top[:, 1], ALU.subtract).then_inc(S["second_ready"], 1)
                dve.wait_ge(S["consts"], 1)
                step(nc.vector.tensor_tensor(group, group, bcast(valid.unsqueeze(2), [P, T, NGE]), ALU.mult))
                for i in range(2):
                    step(nc.vector.tensor_tensor(hot[i].rearrange("p t (g e) -> p t g e", g=NGE),
                                                 bcast(group.unsqueeze(3), [P, T, NGE, EPG]),
                                                 bcast(one[i].unsqueeze(2), [P, T, NGE, EPG]), ALU.mult))
                nc.vector.tensor_tensor(both, hot[0], hot[1], ALU.add).then_inc(S["hots_ready"], 1)
                dve.wait_ge(S["exp_done"], 2)
                step(nc.vector.tensor_reduce(pg, shifted, AX.X, ALU.add))
                step(nc.vector.tensor_scalar(s2, e2, 1.0, None, ALU.add))
                step(nc.vector.tensor_tensor(s2, s2, pg, ALU.mult))
                step(nc.vector.reciprocal(m.row_w[:, 0], s2))
                step(nc.vector.tensor_tensor(m.row_w[:, 1], m.row_w[:, 0], e2, ALU.mult))
                dve.wait_ge(S["ranked"], 1)
                step(nc.vector.memset(before[:, 0], 0.0))
                for t in range(T):
                    step(nc.vector.tensor_tensor(before[:, t + 1], before[:, t], counts[:, t], ALU.add))
                cnt = before[:, T]
                step(nc.vector.tensor_tensor(over, bcast(cnt.unsqueeze(2), [P, NE, 9]),
                                             bcast(by128[:, 0:9].unsqueeze(1), [P, NE, 9]), ALU.is_gt))
                step(nc.vector.tensor_reduce(blocks, over, AX.X, ALU.add))
                step(nc.vector.tensor_tensor(ends_by, upto_mask, bcast(blocks.unsqueeze(1), [P, NE, NE]), ALU.mult))
                step(nc.vector.tensor_reduce(ends, ends_by, AX.X, ALU.add))
                step(nc.vector.tensor_tensor(owner_by, bcast(count_f[:, 0:MAXB].unsqueeze(2), [P, MAXB, NE]),
                                             bcast(ends.unsqueeze(1), [P, MAXB, NE]), ALU.is_ge))
                step(nc.vector.tensor_reduce(owner, owner_by, AX.X, ALU.add))
                step(nc.vector.tensor_scalar(owner, owner, float(NE - 1), None, ALU.min))
                step(nc.vector.tensor_tensor(pairs_by, bcast(ends[:, NE - 1:NE], [P, 25]), by2[:, 0:25], ALU.is_gt))
                step(nc.vector.tensor_reduce(pairs, pairs_by, AX.X, ALU.add))
                step(nc.vector.tensor_copy(m.block_expert, owner))
                nc.vector.tensor_copy(m.n_pairs, pairs).then_inc(S["owners_ready"], 1)
                step(nc.vector.tensor_tensor(start, ends, blocks, ALU.subtract))
                step(nc.vector.tensor_scalar(start, start, float(P), -1.0, ALU.mult, ALU.add))
                step(nc.vector.tensor_tensor(row, ranks, before[:, 0:T], ALU.add))
                step(nc.vector.tensor_tensor(row, row, bcast(start.unsqueeze(1), [P, T, NE]), ALU.add))
                for i in range(2):
                    step(nc.vector.tensor_tensor(hot[i], hot[i], row, ALU.mult))
                    step(nc.vector.tensor_reduce(dest[:, i], hot[i], AX.X, ALU.add))
                step(nc.vector.tensor_copy(m.dest_u, dest))
                flat = dest.rearrange("p i t -> p (i t)")
                step(nc.vector.tensor_copy(dest_i, flat))
                step(nc.vector.tensor_single_scalar(dest_i, dest_i, P - 1, ALU.bitwise_and))
                step(nc.vector.tensor_copy(offset, dest_i))
                step(nc.vector.tensor_tensor(block_of, flat, offset, ALU.subtract))
                step(nc.vector.tensor_tensor(in_block, bcast(count_f.unsqueeze(1), [P, 2 * T, P]),
                                             bcast(offset.unsqueeze(2), [P, 2 * T, P]), ALU.is_equal))
                step(nc.vector.tensor_tensor(of_block, bcast(by128[:, 0:MAXB].unsqueeze(1), [P, 2 * T, MAXB]),
                                             bcast(block_of.unsqueeze(2), [P, 2 * T, MAXB]), ALU.is_equal))
                step(nc.vector.tensor_tensor(token, token, valid, ALU.mult))
                nc.vector.tensor_tensor(of_block.rearrange("p (i t) b -> p i t b", i=2),
                                        of_block.rearrange("p (i t) b -> p i t b", i=2),
                                        bcast(token.unsqueeze(1).unsqueeze(3), [P, 2, T, MAXB]), ALU.mult
                                        ).then_inc(S["one_hots_ready"], 1)
                dve.wait_ge(S["tokens_placed"], 1)
                step(nc.vector.tensor_copy(m.row_token, tokens))


def stage_experts(nc, m):
    pairs_max = (MAXB - 2) // 2
    with ExitStack() as ctx:
        def sb(name, shape, dt=F32):
            return ctx.enter_context(nc.sbuf_tensor("ex_" + name, shape, dt))[:]

        wg, wu = ([m.ring[:, 3 * p + i, :].rearrange("p (k n) -> p k n", k=KD) for p in range(2)] for i in range(2))
        wd = [m.ring[:, 3 * p + 2, :].rearrange("p (k n) -> p k n", k=4) for p in range(2)]
        x = sb("x", [P, 2, D])
        xT = sb("xT", [P, 2, KD, P])
        gated = sb("gated", [P, 512])
        hid = sb("hid", [P, 512])
        hidT = sb("hidT", [P, 2, 4, P])
        y = sb("y", [P, 2, D])
        column = sb("column", [P, 2], U32)
        x_ps = ctx.enter_context(nc.psum_tensor("ex_x_turned", [P, KD, P], F32))[:]
        g_ps, u_ps = (ctx.enter_context(nc.psum_tensor("ex_ps_" + n, [P, 512], F32))[:] for n in "gu")
        h_ps = ctx.enter_context(nc.psum_tensor("ex_h_turned", [P, 4, P], F32))[:]
        y_ps = ctx.enter_context(nc.psum_tensor("ex_y_ps", [P, 2, 512], F32))[:]
        S = semaphores(nc, m, "ex", "gate_done up_done down_done x_turned xT_ready silu_done hid_ready hid_turned "
                       "hidT_ready y_copied column_ready fetch_next all_stored")
        g_landed, u_landed, d_landed = m.expert_landed
        x_landed, y_stored = ([semaphore(nc, m, f"ex_{n}{p}") for p in range(2)] for n in ("x_landed", "y_stored"))

        def pairs(kind):
            return nc.values_load(m.n_pairs[0:1, 0:1], engines=(kind,), min_val=1, max_val=pairs_max)

        with nc.Block() as block:
            @block.sync
            def _(sp):
                n = pairs(CE.SP)
                sp.sem_inc(S["gate_done"], 2)
                sp.sem_inc(S["up_done"], 2)
                sp.sem_inc(S["down_done"], 3)
                sp.wait_ge(x_landed[0], 16)
                sp.wait_ge(x_landed[1], 16)
                first, second = (nc.values_load(m.block_expert[0:1, p:p + 1], engines=(CE.SP,), min_val=0,
                                                max_val=NE - 1) for p in range(2))
                load_expert(sp, m, 2, first, 0)
                for w in range(3):
                    load_expert(sp, m, w, second, 1)
                with sp.Fori(1, n) as i:
                    for p in range(2):
                        b = i * 2 + p
                        e = nc.values_load(m.block_expert[0:1, bass.ds(b, 1)], engines=(CE.SP,), min_val=0, max_val=NE - 1)
                        for w, (sem, need) in enumerate((("gate_done", b + 1), ("up_done", b + 1),
                                                         ("down_done", b * 2 + 1))):
                            sp.wait_ge(S[sem], need)
                            load_expert(sp, m, w, e, p)

            @block.gpsimd
            def _(pool):
                n = pairs(CE.Pool)

                def fetch(p):
                    nc.gpsimd.indirect_dma_start(x[:, p, :], None, m.h2_scr,
                                                 bass.IndirectOffsetOnAxis(column[:, p:p + 1], 0)
                                                 ).then_inc(x_landed[p], 16)

                for p in range(2):
                    nc.gpsimd.tensor_copy(column[:, p:p + 1], m.row_token[:, p:p + 1]).then_inc(S["column_ready"], 1)
                    pool.wait_ge(S["column_ready"], p + 1)
                    fetch(p)
                with pool.Fori(0, n) as i:
                    for p in range(2):
                        b = i * 2 + p
                        pool.wait_ge(S["x_turned"], b * 2 + 2)
                        nc.gpsimd.tensor_copy(column[:, p:p + 1], m.row_token[:, bass.ds(b + 2, 1)]
                                              ).then_inc(S["column_ready"], 1)
                        pool.wait_ge(S["column_ready"], b + 3)
                        pool.sem_inc(S["fetch_next"], 1)
                        fetch(p)
                pool.wait_ge(x_landed[0], n * 16 + 16)
                pool.wait_ge(x_landed[1], n * 16 + 16)

            @block.tensor
            def _(pe):
                n = pairs(CE.PE)

                def turn_x(p, half):
                    for c in range(4):
                        k = 4 * half + c
                        mm = nc.tensor.transpose(x_ps[:, k, :], x[:, p, k::KD], m.ident)
                    mm.then_inc(S["x_turned"], 1)

                pe.wait_ge(x_landed[0], 16)
                turn_x(0, 0)
                turn_x(0, 1)
                with pe.Fori(0, n) as i:
                    for p in range(2):
                        b = i * 2 + p
                        pe.wait_ge(g_landed[p], i * 16 + 16)
                        pe.wait_ge(S["xT_ready"], b * 2 + 2)
                        pe.wait_ge(S["silu_done"], b + 1)
                        for k in range(KD):
                            mm = nc.tensor.matmul(g_ps, xT[:, p, k, :], wg[p][:, k, :], start=(k == 0), stop=(k == KD - 1))
                        mm.then_inc(S["gate_done"], 1)
                        pe.wait_ge(u_landed[p], i * 16 + 16)
                        for k in range(KD):
                            mm = nc.tensor.matmul(u_ps, xT[:, p, k, :], wu[p][:, k, :], start=(k == 0), stop=(k == KD - 1))
                        mm.then_inc(S["up_done"], 1)
                        pe.wait_ge(x_landed[1 - p], i * 16 + 16 * (1 + p))
                        turn_x(1 - p, 0)
                        pe.wait_ge(S["hid_ready"], b + 1)
                        for k in range(4):
                            mm = nc.tensor.transpose(h_ps[:, k, :], hid[:, k::4], m.ident)
                        mm.then_inc(S["hid_turned"], 1)
                        turn_x(1 - p, 1)
                        pe.wait_ge(S["hidT_ready"], b + 1)
                        pe.wait_ge(d_landed[p], i * 16 + 16)
                        pe.wait_ge(S["y_copied"], b * 2 + 1)
                        for half in range(2):
                            for k in range(4):
                                mm = nc.tensor.matmul(y_ps[:, half, :], hidT[:, p, k, :],
                                                      wd[p][:, k, 512 * half:512 * (half + 1)],
                                                      start=(k == 0), stop=(k == 3))
                            mm.then_inc(S["down_done"], 1)

            @block.vector
            def _(dve):
                n = pairs(CE.DVE)

                def copy_x(p, half, turned):
                    k = slice(4 * half, 4 * half + 4)
                    dve.wait_ge(S["x_turned"], turned)
                    nc.vector.tensor_tensor(xT[:, p, k, :], x_ps[:, k, :], bcast(m.ln2[:, k].unsqueeze(2), [P, 4, P]),
                                            ALU.mult).then_inc(S["xT_ready"], 1)

                copy_x(0, 0, 1)
                copy_x(0, 1, 2)
                with dve.Fori(0, n) as i:
                    for p in range(2):
                        b = i * 2 + p
                        dve.wait_ge(S["up_done"], b + 3)
                        dve.wait_ge(S["silu_done"], b + 2)
                        nc.vector.tensor_tensor(hid, u_ps, gated, ALU.mult).then_inc(S["hid_ready"], 1)
                        copy_x(1 - p, 0, b * 2 + 3)
                        dve.wait_ge(S["hid_turned"], b + 1)
                        nc.vector.tensor_copy(hidT[:, p], h_ps).then_inc(S["hidT_ready"], 1)
                        copy_x(1 - p, 1, b * 2 + 4)

            @block.scalar
            def _(act):
                n = pairs(CE.Activation)
                act.sem_inc(S["silu_done"], 1)
                act.sem_inc(S["y_copied"], 1)
                act.sem_inc(y_stored[0], 1)
                act.sem_inc(y_stored[1], 1)
                with act.Fori(0, n) as i:
                    for p in range(2):
                        b = i * 2 + p
                        act.wait_ge(S["gate_done"], b + 3)
                        nc.scalar.activation(gated, g_ps, ACT.Silu).then_inc(S["silu_done"], 1)
                        act.wait_ge(y_stored[p], i * 16 + 1)
                        for half in range(2):
                            act.wait_ge(S["down_done"], b * 2 + half + 4)
                            nc.scalar.activation(y[:, p, 512 * half:512 * (half + 1)], y_ps[:, half, :], ACT.Copy
                                                 ).then_inc(S["y_copied"], 1)
                        act.wait_ge(S["y_copied"], b * 2 + 3)
                        act.dma_start(m.y_scr[bass.ds(b * P, P), :], y[:, p, :]).then_inc(y_stored[p], 16)
                act.wait_ge(y_stored[0], n * 16 + 1)
                act.wait_ge(y_stored[1], n * 16 + 1)
                act.sem_inc(S["all_stored"], 1)


def stage_combine(nc, m):
    with ExitStack() as ctx:
        y = ctx.enter_context(nc.sbuf_tensor("cb_y", [P, 2, 2, D], F32))[:]
        out = ctx.enter_context(nc.sbuf_tensor("cb_out", [P, 2, D], F32))[:]
        first_added, both_added = (semaphore(nc, m, "cb_" + n) for n in ("first_added", "both_added"))
        y_landed, stored = ([semaphore(nc, m, f"cb_{n}{p}") for p in range(2)] for n in ("y_landed", "stored"))
        with nc.Block() as block:
            @block.gpsimd
            def _(pool):
                for t, r in TILES:
                    if t >= 2:
                        pool.wait_ge(both_added, t - 1)
                    for i in range(2):
                        nc.gpsimd.indirect_dma_start(y[0:r, t % 2, i, :], None, m.y_scr,
                                                     bass.IndirectOffsetOnAxis(m.dest_u[0:r, i, t:t + 1], 0)
                                                     ).then_inc(y_landed[t % 2], 16)

            @block.vector
            def _(dve):
                for t, r in TILES:
                    dve.wait_ge(y_landed[t % 2], 32 * (t // 2 + 1))
                    if t >= 2:
                        dve.wait_ge(stored[t % 2], 16 * (t // 2))
                    o = out[0:r, t % 2]
                    nc.vector.scalar_tensor_tensor(o, y[0:r, t % 2, 0], m.row_w[0:r, 0, t:t + 1], m.x1[t][0:r],
                                                   ALU.mult, ALU.add).then_inc(first_added, 1)
                    dve.wait_ge(first_added, t + 1)
                    nc.vector.scalar_tensor_tensor(o, y[0:r, t % 2, 1], m.row_w[0:r, 1, t:t + 1], o,
                                                   ALU.mult, ALU.add).then_inc(both_added, 1)

            @block.sync
            def _(sp):
                for t, r in TILES:
                    sp.wait_ge(both_added, t + 1)
                    dst = m.y_prompt[t * P:(t + 1) * P, :] if t < NT else m.y_sample
                    sp.dma_start(dst, out[0:r, t % 2]).then_inc(stored[t % 2], 16)
                sp.wait_ge(stored[0], 16 * 5)
                sp.wait_ge(stored[1], 16 * 4)


_SHAPES = dict(
    x_prompt=(1, 1024, 1024), x_sample=(8, 1, 1024),
    cache_swa0_kv=(1, 8, 128, 2, 8, 64), cache_swa1_kv=(1, 8, 512, 2, 8, 64), cache_swa2_kv=(1, 8, 2048, 2, 8, 64),
    state_dn_conv=(1, 8, 3, 3072), state_dn_S=(1, 8, 8, 128, 128), ln1_g=(1, 1024), w_in=(1, 1024, 10768),
    q_norm_g=(1, 3, 64), k_norm_g=(1, 3, 64), dn_conv_w=(1, 4, 3072), dn_a_log=(1, 8), dn_dt_bias=(1, 8),
    dn_norm_g=(1, 128), w_out_a=(1, 512, 1024), w_out_b=(1, 1024, 1024), w_o=(1, 1024, 1024), ln2_g=(1, 1024),
    w_rg=(1, 1024, 4), b_rg=(1, 4), w_re=(1, 1024, 32), b_re=(1, 32), w_e_gate=(1, 32, 1024, 512),
    w_e_up=(1, 32, 1024, 512), w_e_down=(1, 32, 512, 1024))
_OUTS = [("y_prompt", (1, 1024, 1024)), ("y_sample", (8, 1, 1024)), ("p_swa0", (1, 1, 128, 2, 8, 64)),
         ("p_swa1", (1, 1, 512, 2, 8, 64)), ("p_swa2", (1, 1, 1024, 2, 8, 64)), ("p_conv", (1, 1, 3, 3072)),
         ("p_S", (1, 1, 8, 128, 128)), ("s_swa0", (1, 8, 1, 2, 8, 64)), ("s_swa1", (1, 8, 1, 2, 8, 64)),
         ("s_swa2", (1, 8, 1, 2, 8, 64)), ("s_conv", (1, 8, 3, 3072)), ("s_S", (1, 8, 8, 128, 128))]


def build(nc, a, out):
    m = Shared()
    m.plan = weight_plan()
    m.last_use = {}
    m.taken = []
    m.n_outputs = 0
    m.x_prompt = a["x_prompt"].rearrange("a t d -> (a t) d")
    m.x_sample = a["x_sample"].rearrange("b t d -> (b t) d")
    m.w_in_v = a["w_in"].rearrange("a (p k) n -> (a p) k n", k=KD)
    m.w_out_a = a["w_out_a"].rearrange("a k n -> (a k) n")
    m.w_out_b = a["w_out_b"].rearrange("a k n -> (a k) n")
    m.w_o = a["w_o"].rearrange("a k n -> (a k) n")
    m.p_swa = [out[f"p_swa{g}"].rearrange("a b t k h e -> (a b t) (k h e)") for g in range(NG)]
    m.s_swa = [out[f"s_swa{g}"].rearrange("a b t k h e -> (a b t) k (h e)") for g in range(NG)]
    m.q_scr = nc.dram_tensor("q_s_scratch", [NB, NG * HW], F32, kind="Internal").ap()
    m.o_s_scr = nc.dram_tensor("o_s_scratch", [NB, NG, OROW], F32, kind="Internal").ap()
    m.conv_w_rows = a["dn_conv_w"].rearrange("a i c -> (a i) c")
    m.conv_state_rows = a["state_dn_conv"].rearrange("a b i c -> (a b i) c")
    m.s_conv = out["s_conv"].rearrange("a b i c -> (a b) i c")
    m.p_conv = out["p_conv"].rearrange("a b i c -> (a b i) c")
    m.p_S = out["p_S"].rearrange("a b h k v -> (a b h) k v")
    m.s_S = out["s_S"].rearrange("a b h k v -> (a b) h k v")
    m.state_S = a["state_dn_S"].rearrange("a b h k v -> (a b) h k v")
    m.caches = [a[f"cache_swa{g}_kv"].rearrange("a b t k h e -> t (a b) (k h e)") for g in range(NG)]
    m.o_scr = nc.dram_tensor("o_scratch", [SEQ, NG, OROW], F32, kind="Internal").ap()
    m.y_scr = nc.dram_tensor("y_scratch", [(MAXB - 2) * P, D], F32, kind="Internal").ap()
    m.y_prompt = out["y_prompt"].rearrange("a t d -> (a t) d")
    m.y_sample = out["y_sample"].rearrange("b t d -> (b t) d")
    m.w_e_gate, m.w_e_up, m.w_e_down = (a[n].rearrange("a e k n -> (a e) k n") for n in
                                        ("w_e_gate", "w_e_up", "w_e_down"))
    m.h2_scr = nc.dram_tensor("h_scratch", [TOK, D], F32, kind="Internal").ap()

    ctx = ExitStack()
    with ctx:
        def sb(name, shape, dt=F32):
            return ctx.enter_context(nc.sbuf_tensor(name, shape, dt))[:]

        m.hT = sb("hT", [P, KD, TOK])
        m.ring = sb("ring", [P, RING, SLOT])
        m.ident, m.ones, m.triu = (sb(x, [P, P]) for x in ("ident", "ones", "triu"))
        m.oBT = sb("oBT", [P, DNH, TOK])
        early = m.oBT.rearrange("p h t -> p (h t)")[0:NB]
        m.q_s = early[:, 0:NG * HW].rearrange("p (g c) -> p g c", g=NG)
        m.kv_s = early[:, NG * HW:3 * NG * HW].rearrange("p (g w c) -> p g w c", g=NG, w=2)
        m.w_ba = sb("w_ba", [P, KD, 16])
        m.dt_bias, m.neg_a = (sb(x, [P, DNH]) for x in ("dt_bias", "neg_a"))
        m.beta_all, m.g_all = (sb(x, [P, NT + 1, DNH]) for x in ("beta_all", "g_all"))
        m.conv_w = sb("conv_w", [P, 24, 4])
        m.conv_state = sb("conv_state", [P, 24, NB, 3])
        m.tails = sb("tails", [P, 24, 11])
        m.dn_s = sb("dn_s", [P, 4, DNH, NB])
        m.dn_gain = sb("dn_gain", [P, 1])
        m.ident_b = sb("ident_b", [P, P], BF16)
        m.scratch_mask = m.oBT[:, 6, 0:2 * P]
        m.odd = m.oBT[:, 7, 0:P].bitcast(I32)
        m.odd_f = m.oBT[:, 7, P:2 * P]
        m.mask_band = sb("mask_band", [P, 2 * P], BF16)
        m.mask_pair, m.mask_decay = (sb(x, [P, P], BF16) for x in ("mask_pair", "mask_decay"))
        m.iota_ready, m.parity_ready = (nc.alloc_semaphore(x) for x in ("iota_ready", "parity_ready"))
        m.minus_half = sb("minus_half", [P, 128])
        m.ln1 = sb("ln1", [P, KD])
        m.ln2 = sb("ln2", [P, KD])
        m.w_router = sb("w_router", [P, KD, 36])
        m.b_router = sb("b_router", [P, 36])
        m.logits = m.conv_state.rearrange("p c b i -> p (c b i)")[:, 0:36 * (NT + 1)].rearrange("p (t n) -> p t n", n=36)
        at = m.conv_state.rearrange("p c b i -> p (c b i)")[:, 36 * (NT + 1):]
        m.row_w = at[:, 0:18].rearrange("p (i t) -> p i t", i=2)
        m.dest_u = at[:, 18:36].bitcast(U32).rearrange("p (i t) -> p i t", i=2)
        m.n_pairs = at[:, 36:37].bitcast(I32)
        m.block_expert = at[:, 40:40 + MAXB].bitcast(I32)
        m.row_token = at[:, 100:100 + MAXB].bitcast(U32)
        x1 = m.oBT.rearrange("p h t -> p (h t)")
        m.x1 = [x1[:, t * D:(t + 1) * D] for t in range(NT)] + [m.hT[0:NB, 0, 0:D]]
        m.qk_gain = sb("qk_gain", [P, 2, NG, E])
        m.pick_col = sb("pick_col", [P, NB, NB])
        m.w_landed = [nc.alloc_semaphore(f"w_landed{i}") for i in range(RING)]
        m.expert_landed = [[nc.alloc_semaphore(f"expert_{w}_landed{p}") for p in range(2)]
                           for w in ("gate", "up", "down")]
        m.S_landed = [nc.alloc_semaphore(f"S_landed{i}") for i in range(2)]
        m.small_landed = nc.alloc_semaphore("small_landed")
        m.outputs_stored = nc.alloc_semaphore("outputs_stored")
        m.pool_step, m.mask_step = (nc.alloc_semaphore(x) for x in ("pool_step", "mask_step"))
        m.small_loads = [
            (m.w_router[:, :, 0:4], a["w_rg"].rearrange("a (p k) n -> (a p) k n", k=KD)),
            (m.w_router[:, :, 4:36], a["w_re"].rearrange("a (p k) n -> (a p) k n", k=KD)),
            (m.b_router[:, 0:4], a["b_rg"].to_broadcast([P, 4])),
            (m.b_router[:, 4:36], a["b_re"].to_broadcast([P, 32])),
            (m.w_ba, m.w_in_v[:, :, COL_BETA:COL_BETA + 16]),
            (m.dt_bias, a["dn_dt_bias"].to_broadcast([P, DNH])),
            (m.neg_a, a["dn_a_log"].to_broadcast([P, DNH])),
            (m.dn_gain, a["dn_norm_g"].rearrange("a (p c) -> (a p) c", c=1)),
            (m.ln1, a["ln1_g"].rearrange("a (p k) -> (a p) k", k=KD)),
            (m.ln2, a["ln2_g"].rearrange("a (p k) -> (a p) k", k=KD)),
            (m.qk_gain[:, 0], a["q_norm_g"].rearrange("a g e -> a (g e)").to_broadcast([P, NG * E]).rearrange("p (g e) -> p g e", g=NG)),
            (m.qk_gain[:, 1], a["k_norm_g"].rearrange("a g e -> a (g e)").to_broadcast([P, NG * E]).rearrange("p (g e) -> p g e", g=NG)),
        ]
        stages = [stage_constants, stage_norm1, stage_attention, stage_decode_attention,
                  stage_deltanet, stage_decode_deltanet, stage_mix, stage_residual,
                  stage_route, stage_experts, stage_combine]
        for stage in stages:
            stage(nc, m)
            if m.taken:
                nc.clear_and_free_semaphores(m.taken)
                nc.all_engine_barrier()
            m.taken = []
            m.last_use = {}
        with nc.Block() as block:
            @block.sync
            def _(sp):
                sp.wait_ge(m.outputs_stored, 16 * m.n_outputs)


def kernel(**inputs):
    import numpy as np
    import concourse.bacc as bacc
    from concourse.bass_utils import run_bass_kernel_spmd

    nc = bacc.Bacc("TRN2", target_bir_lowering=False, num_devices=1)
    arrays = {"in_" + n: np.ascontiguousarray(inputs[n]) for n in _SHAPES}
    a = {n: nc.dram_tensor("in_" + n, shape, F32, kind="ExternalInput").ap() for n, shape in _SHAPES.items()}
    out = {n: nc.dram_tensor("out_" + n, shape, F32, kind="ExternalOutput").ap() for n, shape in _OUTS}
    build(nc, a, out)
    r = run_bass_kernel_spmd(nc, [arrays], core_ids=[0])
    return tuple(r.results[0]["out_" + n] for n, _ in _OUTS)
```
